# Optimizing a Trainium2 kernel written in Bass

```python
import math
import jax, jax.numpy as jnp
from jax import lax
import numpy as np

D_MODEL = 1024
BATCH = 1
SEQ = 256
DEPTH = 2

PLE_DIM = 256
D_FF = 2816
DA_QK_DIM = 64
DA_V_DIM = 2 * DA_QK_DIM
DA_HEADS = (D_MODEL // 2) // DA_V_DIM
DA_WIDTH = DA_HEADS * DA_V_DIM
SSM_GROUP = 16
SSM_WIDTH = D_MODEL // 4
SSM_GROUPS = SSM_WIDTH // SSM_GROUP
SSM_STATE = 64
SA_HEAD_DIM = 64
SA_WIDTH = D_MODEL // 4
SA_HEADS = SA_WIDTH // SA_HEAD_DIM
IDX_HEADS = 8
IDX_DIM = 32
TOPK_MAX = 256
REL_BUCKETS = 32
REL_MAX_DIST = 128
N_ATT_HEADS = DA_HEADS + SA_HEADS
Q_BLOCK = 128
D_MIX = DA_WIDTH + SSM_WIDTH + SA_WIDTH
ALPHA = (2 * DEPTH) ** 0.25
BETA = (8 * DEPTH) ** -0.25
LN_EPS = 1e-5
IN_SIZES = (DA_HEADS * 2 * DA_QK_DIM, DA_HEADS * 2 * DA_QK_DIM, DA_HEADS * DA_V_DIM,
            SSM_WIDTH,
            SA_HEADS * SA_HEAD_DIM, SA_HEAD_DIM, SA_HEAD_DIM,
            IDX_HEADS * IDX_DIM, IDX_DIM, IDX_HEADS)
IN_COLS = sum(IN_SIZES)

kernel_name = "hybrid_diffattn_s5_dsa_macaron_deepnorm"

def layer_norm(x, g, b):
    xf = x.astype(jnp.float32)
    mu = xf.mean(-1, keepdims=True)
    var = jnp.square(xf - mu).mean(-1, keepdims=True)
    return ((xf - mu) * lax.rsqrt(var + LN_EPS) * g + b).astype(x.dtype)

def rms_norm(x, g):
    xf = x.astype(jnp.float32)
    return (xf * lax.rsqrt(jnp.mean(xf * xf, -1, keepdims=True) + LN_EPS) * g).astype(x.dtype)

def swiglu(x, w_gate, w_up, w_down):
    return (jax.nn.silu(x @ w_gate) * (x @ w_up)) @ w_down

def t5_bucket(rel):
    n = jnp.maximum(rel, 0)
    max_exact = REL_BUCKETS // 2
    nf = jnp.maximum(n, 1).astype(jnp.float32)
    large = max_exact + (jnp.log(nf / max_exact) / math.log(REL_MAX_DIST / max_exact)
                         * (REL_BUCKETS - max_exact)).astype(jnp.int32)
    large = jnp.minimum(large, REL_BUCKETS - 1)
    return jnp.where(n < max_exact, n, large)

def diff_attention(q, k, v, lam, bias_table):
    bsz, L, H = q.shape[0], q.shape[1], q.shape[2]
    nb = L // Q_BLOCK
    scale = DA_QK_DIM ** -0.5
    key_pos = jnp.arange(L)
    q_blocks = q.reshape(bsz, nb, Q_BLOCK, H, 2, DA_QK_DIM).swapaxes(0, 1)

    def block(args):
        qb, start = args
        qpos = start + jnp.arange(Q_BLOCK)
        rel = qpos[:, None] - key_pos[None, :]
        bias = bias_table[t5_bucket(rel)].transpose(2, 0, 1).astype(jnp.float32)
        s = jnp.einsum('bqhcd,bshcd->bhcqs', qb, k).astype(jnp.float32) * scale + bias[None, :, None]
        s = jnp.where(rel >= 0, s, -jnp.inf)
        pr = jax.nn.softmax(s, axis=-1)
        a = (pr[:, :, 0] - lam * pr[:, :, 1]).astype(v.dtype)
        return jnp.einsum('bhqs,bshe->bqhe', a, v)

    o = lax.map(block, (q_blocks, jnp.arange(nb) * Q_BLOCK))
    return o.swapaxes(0, 1).reshape(bsz, L, H, DA_V_DIM)

def _ssm_combine(e1, e2):
    a1r, a1i, b1r, b1i = e1
    a2r, a2i, b2r, b2i = e2
    return (a2r * a1r - a2i * a1i, a2r * a1i + a2i * a1r,
            a2r * b1r - a2i * b1i + b2r, a2r * b1i + a2i * b1r + b2i)

def s5_ssm(u, lam_re, lam_im, log_dt, b_re, b_im, c_re, c_im, d_skip, w_glu):
    f32 = jnp.float32
    bsz, L, _ = u.shape
    ug = u.reshape(bsz, L, SSM_GROUPS, SSM_GROUP).astype(f32)
    dt = jnp.exp(log_dt.astype(f32))[:, None]
    lr, li = lam_re.astype(f32), lam_im.astype(f32)
    mag = jnp.exp(lr * dt)
    ab_re, ab_im = mag * jnp.cos(li * dt), mag * jnp.sin(li * dt)
    den = lr * lr + li * li
    nr, ni = ab_re - 1.0, ab_im
    f_re, f_im = (nr * lr + ni * li) / den, (ni * lr - nr * li) / den
    br, bi = b_re.astype(f32), b_im.astype(f32)
    bb_re = f_re[..., None] * br - f_im[..., None] * bi
    bb_im = f_re[..., None] * bi + f_im[..., None] * br
    bu_re = jnp.einsum('gpc,blgc->blgp', bb_re, ug)
    bu_im = jnp.einsum('gpc,blgc->blgp', bb_im, ug)
    a_re = jnp.broadcast_to(ab_re, bu_re.shape)
    a_im = jnp.broadcast_to(ab_im, bu_re.shape)
    _, _, x_re, x_im = lax.associative_scan(_ssm_combine, (a_re, a_im, bu_re, bu_im), axis=1)
    y = (jnp.einsum('gcp,blgp->blgc', c_re.astype(f32), x_re)
         - jnp.einsum('gcp,blgp->blgc', c_im.astype(f32), x_im))
    y = y + d_skip.astype(f32).reshape(SSM_GROUPS, SSM_GROUP) * ug
    y = jax.nn.gelu(y.reshape(bsz, L, SSM_WIDTH))
    y = y * jax.nn.sigmoid(y @ w_glu.astype(f32))
    return y.astype(u.dtype)

def dsa_attention(q, k, v, qi, ki, wi, bias_table):
    bsz, L = q.shape[0], q.shape[1]
    topk = min(TOPK_MAX, L // 4)
    nb = L // Q_BLOCK
    key_pos = jnp.arange(L)
    scale = SA_HEAD_DIM ** -0.5
    w_scale = IDX_HEADS ** -0.5 * IDX_DIM ** -0.5

    def to_blocks(a):
        return a.reshape(bsz, nb, Q_BLOCK, *a.shape[2:]).swapaxes(0, 1)

    def block(args):
        qb, qib, wib, start = args
        qpos = start + jnp.arange(Q_BLOCK)
        iscore = jax.nn.relu(jnp.einsum('bqhd,bsd->bqhs', qib, ki).astype(jnp.float32))
        iscore = jnp.einsum('bqhs,bqh->bqs', iscore, wib.astype(jnp.float32) * w_scale)
        iscore = jnp.where(key_pos[None, :] <= qpos[:, None], iscore, -jnp.inf)
        _, idx = lax.top_k(iscore, topk)
        k_sel = jax.vmap(lambda kk, ii: kk[ii])(k, idx)
        v_sel = jax.vmap(lambda vv, ii: vv[ii])(v, idx)
        rel = qpos[None, :, None] - idx
        bias = bias_table[t5_bucket(rel)].transpose(0, 3, 1, 2).astype(jnp.float32)
        s = jnp.einsum('bqhd,bqkd->bhqk', qb, k_sel).astype(jnp.float32) * scale + bias
        s = jnp.where((rel >= 0)[:, None], s, -jnp.inf)
        pr = jax.nn.softmax(s, axis=-1).astype(v.dtype)
        return jnp.einsum('bhqk,bqkd->bqhd', pr, v_sel)

    o = lax.map(block, (to_blocks(q), to_blocks(qi), to_blocks(wi), jnp.arange(nb) * Q_BLOCK))
    return o.swapaxes(0, 1).reshape(bsz, L, SA_WIDTH)

def hybrid_mixer(x, w_in, w_o, lam_q1, lam_k1, lam_q2, lam_k2, lam_init, subln_g,
                 ssm_lam_re, ssm_lam_im, ssm_log_dt, ssm_b_re, ssm_b_im, ssm_c_re, ssm_c_im,
                 ssm_d, ssm_w_glu, rel_bias):
    bsz, L, _ = x.shape
    h = x @ w_in
    offsets = [int(o) for o in np.cumsum(IN_SIZES)[:-1]]
    da_q, da_k, da_v, ssm_u, sa_q, sa_k, sa_v, ix_q, ix_k, ix_w = jnp.split(h, offsets, axis=-1)
    lam = (jnp.exp(jnp.sum(lam_q1.astype(jnp.float32) * lam_k1))
           - jnp.exp(jnp.sum(lam_q2.astype(jnp.float32) * lam_k2)) + lam_init)
    o_da = diff_attention(da_q.reshape(bsz, L, DA_HEADS, 2, DA_QK_DIM),
                          da_k.reshape(bsz, L, DA_HEADS, 2, DA_QK_DIM),
                          da_v.reshape(bsz, L, DA_HEADS, DA_V_DIM),
                          lam, rel_bias[:, :DA_HEADS])
    o_da = (rms_norm(o_da, subln_g) * (1.0 - lam_init)).reshape(bsz, L, DA_WIDTH)
    o_ssm = s5_ssm(ssm_u, ssm_lam_re, ssm_lam_im, ssm_log_dt, ssm_b_re, ssm_b_im,
                   ssm_c_re, ssm_c_im, ssm_d, ssm_w_glu)
    o_sa = dsa_attention(sa_q.reshape(bsz, L, SA_HEADS, SA_HEAD_DIM), sa_k, sa_v,
                         ix_q.reshape(bsz, L, IDX_HEADS, IDX_DIM), ix_k, ix_w,
                         rel_bias[:, DA_HEADS:])
    return jnp.concatenate([o_da, o_ssm, o_sa], axis=-1) @ w_o

def setup_inputs(seed: int = 0) -> dict:
    key = jax.random.key(seed)
    ks = iter(jax.random.split(key, 40))
    f32 = jnp.float32

    def nrm(shape, scale):
        return jax.random.normal(next(ks), shape, f32) * scale

    def gain(shape):
        return 1.0 + nrm(shape, 0.02)

    N = DEPTH
    n_idx = jnp.arange(SSM_STATE, dtype=f32)
    log_dt = jax.random.uniform(next(ks), (N, SSM_GROUPS), f32, math.log(1e-3), math.log(1e-1))
    return {
        'x': nrm((BATCH, SEQ, D_MODEL), 1.0),
        'p': nrm((DEPTH, BATCH, SEQ, PLE_DIM), 1.0),
        'rel_bias': nrm((REL_BUCKETS, N_ATT_HEADS), 0.5),
        'ffn1_w_gate': nrm((N, D_MODEL, D_FF), D_MODEL ** -0.5),
        'ffn1_w_up': nrm((N, D_MODEL, D_FF), D_MODEL ** -0.5),
        'ffn1_w_down': nrm((N, D_FF, D_MODEL), D_FF ** -0.5 * BETA),
        'ln1_g': gain((N, D_MODEL)),
        'ln1_b': nrm((N, D_MODEL), 0.02),
        'w_in': nrm((N, D_MODEL, IN_COLS), D_MODEL ** -0.5),
        'w_o': nrm((N, D_MIX, D_MODEL), D_MIX ** -0.5 * BETA),
        'da_lam_q1': nrm((N, DA_QK_DIM), 0.1),
        'da_lam_k1': nrm((N, DA_QK_DIM), 0.1),
        'da_lam_q2': nrm((N, DA_QK_DIM), 0.1),
        'da_lam_k2': nrm((N, DA_QK_DIM), 0.1),
        'da_subln_g': gain((N, DA_V_DIM)),
        'ssm_lam_re': -0.5 + nrm((N, SSM_GROUPS, SSM_STATE), 0.01),
        'ssm_lam_im': jnp.pi * n_idx + nrm((N, SSM_GROUPS, SSM_STATE), 0.01),
        'ssm_log_dt': log_dt,
        'ssm_b_re': nrm((N, SSM_GROUPS, SSM_STATE, SSM_GROUP), (2.0 * SSM_GROUP) ** -0.5),
        'ssm_b_im': nrm((N, SSM_GROUPS, SSM_STATE, SSM_GROUP), (2.0 * SSM_GROUP) ** -0.5),
        'ssm_c_re': nrm((N, SSM_GROUPS, SSM_GROUP, SSM_STATE), SSM_STATE ** -0.5),
        'ssm_c_im': nrm((N, SSM_GROUPS, SSM_GROUP, SSM_STATE), SSM_STATE ** -0.5),
        'ssm_d': nrm((N, SSM_WIDTH), 1.0),
        'ssm_w_glu': nrm((N, SSM_WIDTH, SSM_WIDTH), SSM_WIDTH ** -0.5),
        'ln2_g': gain((N, D_MODEL)),
        'ln2_b': nrm((N, D_MODEL), 0.02),
        'ffn2_w_gate': nrm((N, D_MODEL, D_FF), D_MODEL ** -0.5),
        'ffn2_w_up': nrm((N, D_MODEL, D_FF), D_MODEL ** -0.5),
        'ffn2_w_down': nrm((N, D_FF, D_MODEL), D_FF ** -0.5 * BETA),
        'ple_w_proj': nrm((N, PLE_DIM, D_MODEL), PLE_DIM ** -0.5 * BETA),
        'ple_w_gate': nrm((N, D_MODEL, D_MODEL), D_MODEL ** -0.5),
        'ln3_g': gain((N, D_MODEL)),
        'ln3_b': nrm((N, D_MODEL), 0.02),
    }

def reference(x, p, rel_bias, ffn1_w_gate, ffn1_w_up, ffn1_w_down, ln1_g, ln1_b,
              w_in, w_o, da_lam_q1, da_lam_k1, da_lam_q2, da_lam_k2, da_subln_g,
              ssm_lam_re, ssm_lam_im, ssm_log_dt, ssm_b_re, ssm_b_im, ssm_c_re, ssm_c_im,
              ssm_d, ssm_w_glu, ln2_g, ln2_b, ffn2_w_gate, ffn2_w_up, ffn2_w_down,
              ple_w_proj, ple_w_gate, ln3_g, ln3_b):
    for i in range(DEPTH):
        lam_init = 0.8 - 0.6 * math.exp(-0.3 * i)
        x = layer_norm(ALPHA * x + 0.5 * swiglu(x, ffn1_w_gate[i], ffn1_w_up[i], ffn1_w_down[i]),
                       ln1_g[i], ln1_b[i])
        mix = hybrid_mixer(x, w_in[i], w_o[i], da_lam_q1[i], da_lam_k1[i], da_lam_q2[i], da_lam_k2[i],
                           lam_init, da_subln_g[i], ssm_lam_re[i], ssm_lam_im[i], ssm_log_dt[i],
                           ssm_b_re[i], ssm_b_im[i], ssm_c_re[i], ssm_c_im[i], ssm_d[i], ssm_w_glu[i],
                           rel_bias)
        x = layer_norm(ALPHA * x + mix, ln2_g[i], ln2_b[i])
        ple = (p[i] @ ple_w_proj[i]) * jax.nn.sigmoid(x @ ple_w_gate[i])
        x = layer_norm(ALPHA * x + 0.5 * swiglu(x, ffn2_w_gate[i], ffn2_w_up[i], ffn2_w_down[i]) + ple,
                       ln3_g[i], ln3_b[i])
    return x


_drawn_inputs = setup_inputs


def setup_inputs(seed=0):
    import zlib

    import numpy as np

    out = dict(_drawn_inputs(seed))
    spreads = {}
    factors = {'da_lam_q1': 4.231,
     'da_lam_k1': 3.547,
     'da_lam_q2': 4.954,
     'da_lam_k2': 5.105,
     'da_subln_g': 8.0,
     'ssm_lam_re': 64.0,
     'ssm_lam_im': 58.896,
     'ssm_log_dt': 60.728,
     'ssm_b_re': 64.0,
     'ssm_b_im': 64.0,
     'ssm_c_re': 64.0,
     'ssm_c_im': 64.0,
     'ssm_w_glu': 3.283}
    for name, (base, spread) in spreads.items():
        noise = np.random.default_rng([zlib.crc32(name.encode()), seed]).standard_normal(out[name].shape)
        drawn = base * np.exp(spread * noise) if base else spread * noise
        out[name] = __import__('jax').numpy.asarray(drawn.astype(out[name].dtype))
    for name, factor in factors.items():
        out[name] = (out[name] * factor).astype(out[name].dtype)
    return out
```

```python
import math
from contextlib import ExitStack

import numpy as np

import concourse.bass as bass
from concourse import mybir
from concourse.alu_op_type import AluOpType as ALU

F32 = mybir.dt.float32
F32R = mybir.dt.float32r
ACT = mybir.ActivationFunctionType
AX = mybir.AxisListType

P = 128
D_MODEL, SEQ, DEPTH = 1024, 256, 2
PLE_DIM, D_FF = 256, 2816
KT = D_MODEL // P
NT = SEQ // P
DA_HEADS, DA_QK, DA_V = 4, 64, 128
SSM_GROUP, SSM_WIDTH, SSM_GROUPS, SSM_STATE = 16, 256, 16, 64
SA_HEADS, SA_DIM = 4, 64
IDX_HEADS, IDX_DIM = 8, 32
TOPK = SEQ // 4
REL_BUCKETS, REL_MAX_DIST = 32, 128
N_ATT = DA_HEADS + SA_HEADS
ALPHA = (2 * DEPTH) ** 0.25
LN_EPS = 1e-5
IN_SIZES = (512, 512, 512, SSM_WIDTH, 256, 64, 64, 256, 32, 8)
IN_COLS = sum(IN_SIZES)
C_Q, C_K, C_V, C_U, C_SQ, C_SK, C_SV, C_IQ, C_IK, C_IW = (sum(IN_SIZES[:i]) for i in range(10))

CHUNK = 256
CHUNKS = D_FF // CHUNK
WIN_GROUPS = 6
WIN_COLS = IN_COLS // WIN_GROUPS
assert CHUNKS * CHUNK == D_FF and WIN_COLS * WIN_GROUPS == IN_COLS and WIN_COLS % 2 == 0

A_FFN1, A_WIN = 0, CHUNKS
A_WO = A_WIN + WIN_GROUPS
A_GATE = A_WO + 2
A_FFN2 = A_GATE + 2
A_GROUPS = A_FFN2 + CHUNKS
B_FFN1, B_PROJ = 0, CHUNKS
B_FFN2 = B_PROJ + 1
B_GROUPS = B_FFN2 + CHUNKS
A_UNITS, B_UNITS = 4, 2
A_ALL, B_ALL = A_GROUPS * A_UNITS, B_GROUPS * B_UNITS

NEG = -1e30
TAKEN = -3e38
STATE_TILES = SSM_GROUPS // 2
UNITS = DA_HEADS * NT

R_G1, R_B1, R_G2, R_B2, R_RE, R_IM, R_DT, R_D, R_SUB = 0, 16, 32, 48, 64, 80, 96, 112, 116
ROWS = 118
Q_G1, Q_B1, Q_G2, Q_B2, Q_MAG, Q_COS, Q_SIN, Q_FRE, Q_FIM, Q_MISC, NQ = range(11)
M_D, M_SUB, M_NLAM = 0, 2, 3

TWO_PI = 2 * math.pi
PI_A = 6.28125
PI_B = float(np.float32(round((TWO_PI - PI_A) * 2 ** 21) / 2 ** 21))
PI_C = float(np.float32(TWO_PI - PI_A - PI_B))
ROUND = 1.5 * 2 ** 23


def lam_init(layer):
    return 0.8 - 0.6 * math.exp(-0.3 * layer)


def bucket_selector():
    n = np.maximum(255 - np.arange(3 * P), 0)
    exact = REL_BUCKETS // 2
    nf = np.maximum(n, 1).astype(np.float32)
    large = exact + (np.log(nf / np.float32(exact)) / np.float32(math.log(REL_MAX_DIST / exact))
                     * np.float32(REL_BUCKETS - exact)).astype(np.int32)
    b = np.where(n < exact, n, np.minimum(large, REL_BUCKETS - 1))
    return (b[None, :] == np.arange(REL_BUCKETS)[:, None]).astype(np.float32)


def build(nc, a):
    ctx = ExitStack()
    with ctx:
        def sb(name, shape, dt=F32):
            return ctx.enter_context(nc.sbuf_tensor(name, shape, dt))

        def sem(name):
            return ctx.enter_context(nc.semaphore(name))

        raw_a = sb("raw_a", [P, 8, 512])
        raw_b = sb("raw_b", [P, 2, 1024])
        hi_a, lo_a = sb("hi_a", [P, 8, 512], F32R), sb("lo_a", [P, 8, 512], F32R)
        hi_b, lo_b = sb("hi_b", [P, 2, 1024], F32R), sb("lo_b", [P, 2, 1024], F32R)
        actT_hi, actT_lo = sb("actT_hi", [P, KT, SEQ], F32R), sb("actT_lo", [P, KT, SEQ], F32R)
        hT_hi, hT_lo = sb("hT_hi", [P, 2, SEQ], F32R), sb("hT_lo", [P, 2, SEQ], F32R)
        pT_hi, pT_lo = sb("pT_hi", [P, 2, SEQ], F32R), sb("pT_lo", [P, 2, SEQ], F32R)
        x = sb("x", [P, NT, D_MODEL])
        z = sb("z", [P, NT, D_MODEL])
        gb = sb("gb", [P, 2, D_MODEL])
        hp = sb("hp", [P, NT, IN_COLS])
        h = sb("h", [P, NT, CHUNK])
        bias = sb("bias", [P, N_ATT, SEQ])
        causal = sb("causal", [P, SEQ])
        ident, flip = sb("ident", [P, P]), sb("flip", [P, P])
        tw_re, tw_im = sb("tw_re", [P, STATE_TILES, SEQ]), sb("tw_im", [P, STATE_TILES, SEQ])
        qT, kT = sb("qT", [P, DA_HEADS, SEQ]), sb("kT", [P, DA_HEADS, SEQ])
        saqT, iqT = sb("saqT", [P, 2, SEQ]), sb("iqT", [P, 2, SEQ])
        ksT = sb("ksT", [P, 2, SEQ])
        uT = sb("uT", [P, 2, SEQ])
        inT = sb("inT", [P, 2, 2, P])
        outT = sb("outT", [P, STATE_TILES, 3, 32])
        b_exp = sb("b_exp", [P, 2, STATE_TILES, 32])
        parity = sb("parity", [P, 2])
        glu = sb("glu", [P, 2, SSM_WIDTH])
        dt_row = sb("dt_row", [P, 2])
        prmT = sb("prmT", [P, ROWS])
        par = sb("par", [P, NQ, DEPTH, 8])
        lp = sb("lp", [P, NQ, 8])
        small = sb("small", [P, 12, 16])
        lams = sb("lams", [P, 2, DEPTH])
        stats = sb("stats", [P, NT, 2, 6])
        mv = sb("mv", [P, NT, 2])
        var, rstd = sb("var", [P, NT]), sb("rstd", [P, NT])
        mhalf = sb("mhalf", [P, 8])
        isc, work = sb("isc", [P, SEQ]), sb("work", [P, SEQ])
        top8 = sb("top8", [P, 8])
        sel = sb("sel", [P, NT, SEQ])
        wis = sb("wis", [P, NT, IDX_HEADS])
        da_e = sb("da_e", [P, 2, 2, SEQ])
        da_nm = sb("da_nm", [P, 2, 2])
        da_sum, da_r = sb("da_sum", [P, UNITS, 2]), sb("da_r", [P, UNITS, 2])
        aT = sb("aT", [P, 2, SEQ])
        junk = sb("junk", [P, P])
        ss, rms = sb("ss", [P, NT, DA_HEADS]), sb("rms", [P, NT, DA_HEADS])
        sa_nm, sa_sum = sb("sa_nm", [P, NT, SA_HEADS]), sb("sa_sum", [P, NT, SA_HEADS])
        hp_flat = hp[:, :, :].rearrange("p a c -> p (a c)")
        lnT = hp_flat[:, 0:2048].rearrange("p (k t) -> p k t", k=KT)
        p_nat = hp_flat[:, 2048:2560].rearrange("p (t d) -> p t d", t=NT)
        c_nat = hp_flat[:, 2560:2816].rearrange("p (r t d) -> p r t d", r=2, t=2)
        b_nat = hp_flat[:, 2816:3072].rearrange("p (r j c) -> p r j c", r=2, j=STATE_TILES)
        b_tmp = hp_flat[:, 3072:3328].rearrange("p (r j c) -> p r j c", r=2, j=STATE_TILES)
        c_exp = hp_flat[:, 3328:3840].rearrange("p (r t q d) -> p r t q d", r=2, t=2, q=2)
        lamv = hp_flat[:, 3840:4352].rearrange("p (i l d) -> p i l d", i=4, l=DEPTH)
        rows = hp_flat[:, 4352:4480]
        rot = z[:, 0, :].rearrange("p (a c t) -> p a c t", a=2, c=2)
        ys = z[:, 1, :].rearrange("p (a c t) -> p a c t", a=2, c=2)
        prod = gb[:, :, :].rearrange("p a (b c t) -> p a b c t", b=2, c=2)
        derot = h
        kdup = h
        relu_w = raw_b[:, :, :].rearrange("p a (h s) -> p (a h) s", s=SEQ)
        sa_e = raw_b[:, 0, :].rearrange("p (h s) -> p h s", s=SEQ)
        sa_aT = raw_b[:, 1, :]
        ys2 = raw_b[:, 0, :].rearrange("p (v a t) -> p v a t", v=2, a=2)
        ysg = raw_b[:, 1, 0:512].rearrange("p (a t) -> p a t", a=2)

        ps = ctx.enter_context(nc.psum_tensor("ps", [P, 8, 512], F32))
        GU, ACC, TR, MISC = 0, 2, 6, 7
        LN_BANKS = (0, 1, 6, 7)

        a_loaded = [sem(f"a_loaded{i}") for i in range(2)]
        b_loaded = [sem(f"b_loaded{i}") for i in range(2)]
        a_hi, a_lo, a_used = sem("a_hi"), sem("a_lo"), sem("a_used")
        b_hi, b_lo, b_used = sem("b_hi"), sem("b_lo"), sem("b_used")
        names = """x_loaded rows_loaded dtrow_loaded lamv_loaded sel_loaded ssm_loaded glu_loaded p_loaded
            gb_loaded gb_used consts_set dt_expanded rows_turned prm_out table_turned table_out table_stored
            bias_loaded bias_flipped bias_out bias_read dt_exp mag_ready sin_in sin_out lam_in lam_exp par_ready lp_ready
            x_ready x_half turned lnT_scaled lnT_act actT_hi_ready actT_ready p_turned pT_hi_ready pT_ready
            gate_act h_ready h_turned hT_hi_ready hT_ready ffn_done acc_read var_ready rs_ready z_ready
            twiddles b_ready c_ready bc_turned in_out c_out x_updated
            win_done hp_ready kdup_ready ix_turned ix_out qk_turned qk_out ixs_done ixs_read sel_ready
            bu_done bu_read y_ready prod_ready c_done
            das_done das_read da_max da_exp da_a da_turned da_aT da_o da_o_out ss_scaled rms_ready mix_da
            sas_done sas_read sa_max sa_exp sa_turned sa_aT_ready sa_o mix_sa
            y_full gelu_done glu_done glu_act ssm_out mix_turned mixT_hi wo_done
            proj_done gate_done gate_sig ple_done stored""".split()
        s = {n: sem(n) for n in names}

        block = ctx.enter_context(nc.Block())

        def mm3(pe, out, act_hi, act_lo, w_hi, w_lo, first, last):
            pe.matmul(out, act_hi, w_hi, start=first, stop=False)
            pe.matmul(out, act_hi, w_lo, start=False, stop=False)
            return pe.matmul(out, act_lo, w_hi, start=False, stop=last)

        def bc(ap, n):
            return ap.unsqueeze(ap.ndim).broadcast_to([*ap.shape, n])

        def rep(ap, n):
            return ap.unsqueeze(1).broadcast_to([ap.shape[0], n, *ap.shape[1:]])

        @block.sync
        def _(sp):
            def load(dst, src, done):
                return sp.dma_start(dst, src).then_inc(done, 16)

            def load_a(L, n, k, srcs):
                for half in range(2):
                    sp.wait_ge(a_lo, L * A_ALL + n * A_UNITS + (k * A_UNITS + 2 * half + 2))
                    for dst, src in srcs(4 * half):
                        load(dst, src, a_loaded[half])

            def load_b(L, m, k, src):
                for half in range(2):
                    sp.wait_ge(b_lo, L * B_ALL + m * B_UNITS + (k * B_UNITS + half + 1))
                    load(raw_b[:, half, :], src(half), b_loaded[half])

            def ffn(L, gate, up, down, a0, b0):
                with sp.Fori(0, CHUNKS) as c:
                    col = sp.snap(c * CHUNK)
                    def srcs(k0):
                        for i, w in enumerate((gate, up)):
                            yield (raw_a[:, k0:k0 + 4, i * CHUNK:(i + 1) * CHUNK],
                                   w[L, k0 * P:(k0 + 4) * P, bass.ds(col, CHUNK)]
                                   .rearrange("(k p) f -> p k f", p=P))
                    load_a(L, c, a0, srcs)
                    load_b(L, c, b0, lambda half: down[L, bass.ds(col + half * P, P), :])

            def wide(w, L, c0, cols):
                def srcs(k0):
                    for k in (k0 + 2, k0):
                        yield (raw_a[:, k:k + 2, 0:cols],
                               w[L, k * P:(k + 2) * P, c0:c0 + cols].rearrange("(k p) f -> p k f", p=P))
                return srcs

            def load_norm(L, g, b):
                load(gb[:, 0, :], g[bass.ds(L, 1), :].broadcast_to([P, D_MODEL]), s["gb_loaded"])
                load(gb[:, 1, :], b[bass.ds(L, 1), :].broadcast_to([P, D_MODEL]), s["gb_loaded"])

            load(x[:, :, :], a["x"][0].rearrange("(t p) d -> p t d", p=P), s["x_loaded"])
            for r, name in ((R_G1, "ln1_g"), (R_B1, "ln1_b"), (R_G2, "ln2_g"), (R_B2, "ln2_b")):
                load(rows[r:r + 16, :], a[name].rearrange("l (r c) -> (l r) c", c=P), s["rows_loaded"])
            for r, name in ((R_RE, "ssm_lam_re"), (R_IM, "ssm_lam_im")):
                load(rows[r:r + 16, :], a[name].rearrange("l (j g) p -> (l j) (g p)", g=2), s["rows_loaded"])
            load(rows[R_D:R_D + 4, :], a["ssm_d"].rearrange("l (r c) -> (l r) c", c=P), s["rows_loaded"])
            load(rows[R_SUB:R_SUB + 2, :], a["da_subln_g"], s["rows_loaded"])
            load(dt_row[R_DT:R_DT + 16, :], a["ssm_log_dt"].rearrange("l (j g) -> (l j) g", g=2), s["dtrow_loaded"])
            for i, name in enumerate(("da_lam_q1", "da_lam_k1", "da_lam_q2", "da_lam_k2")):
                load(lamv[:, i, :, :].rearrange("p l d -> p (l d)"),
                     a[name].rearrange("l d -> (l d)").unsqueeze(0).broadcast_to([P, DEPTH * DA_QK]), s["lamv_loaded"])
            load(tw_re[0:REL_BUCKETS, 0, 0:N_ATT], a["rel_bias"], s["sel_loaded"])
            load(tw_im[0:REL_BUCKETS, 0:2, :].rearrange("p a t -> p (a t)")[:, 0:3 * P], a["selector"], s["sel_loaded"])

            with sp.Fori(0, DEPTH) as L:
                sp.wait_ge(s["gb_used"], L * 3)
                load_norm(L, a["ln1_g"], a["ln1_b"])
                for i, name in enumerate(("ssm_b_re", "ssm_b_im")):
                    load(b_nat[:, i, :, :], a[name][L].rearrange("(j g) p c -> (g p) j c", g=2), s["ssm_loaded"])
                for i, name in enumerate(("ssm_c_re", "ssm_c_im")):
                    load(c_nat[:, i, :, :], a[name][L].rearrange("(t g) c p -> (g c) t p", t=2), s["ssm_loaded"])
                load(glu[:, :, :], a["ssm_w_glu"][L].rearrange("(t p) c -> p t c", p=P), s["glu_loaded"])
                load(p_nat[:, :, :], a["p"][L, 0].rearrange("(t p) d -> p t d", p=P), s["p_loaded"])
                ffn(L, a["ffn1_w_gate"], a["ffn1_w_up"], a["ffn1_w_down"], A_FFN1, B_FFN1)
                for i in range(WIN_GROUPS):
                    load_a(L, 0, A_WIN + i, wide(a["w_in"], L, (WIN_GROUPS - 1 - i) * WIN_COLS, WIN_COLS))
                for i in range(2):
                    load_a(L, 0, A_WO + i, wide(a["w_o"], L, i * 512, 512))
                sp.wait_ge(s["mixT_hi"], L * 4 + 4)
                sp.wait_ge(s["actT_ready"], L * 16 + 12)
                load_norm(L, a["ln2_g"], a["ln2_b"])
                load_b(L, 0, B_PROJ, lambda half: a["ple_w_proj"][L, half * P:(half + 1) * P, :])
                for i in range(2):
                    load_a(L, 0, A_GATE + i, wide(a["ple_w_gate"], L, i * 512, 512))
                sp.wait_ge(s["gb_used"], L * 3 + 2)
                load_norm(L, a["ln3_g"], a["ln3_b"])
                ffn(L, a["ffn2_w_gate"], a["ffn2_w_up"], a["ffn2_w_down"], A_FFN2, B_FFN2)

            sp.wait_ge(s["x_ready"], DEPTH)
            sp.wait_ge(s["x_half"], DEPTH)
            load(a["out"][0].rearrange("(t p) d -> p t d", p=P), x[:, :, :], s["stored"])
            sp.wait_ge(s["stored"], 16)

        @block.gpsimd
        def _(pool):
            TT, MUL, ADD, SUB = pool.tensor_tensor, ALU.mult, ALU.add, ALU.subtract
            pool.memset(ident[:, :], 0.0)
            pool.memset(flip[:, :], 0.0)
            pool.memset(causal[:, :], 0.0)
            pool.memset(parity[:, :], 1.0)
            pool.memset(mhalf[:, :], -0.5)
            pool.memset(b_exp[:, :, :, :], 0.0)
            pool.drain()
            pool.affine_select(out=ident[:, :], in_=ident[:, :], compare_op=ALU.not_equal, fill=1.0, base=0,
                               pattern=[[-1, P]], channel_multiplier=1)
            pool.affine_select(out=flip[:, :], in_=flip[:, :], compare_op=ALU.not_equal, fill=1.0, base=1 - P,
                               pattern=[[1, P]], channel_multiplier=1)
            pool.affine_select(out=causal[:, :], in_=causal[:, :], compare_op=ALU.is_ge, fill=NEG, base=P,
                               pattern=[[-1, SEQ]], channel_multiplier=1)
            for g in range(P // SSM_GROUP):
                q = 1 - g % 2
                pool.drain()
                pool.affine_select(out=junk[:, 0:1], in_=mhalf[:, 0:1], compare_op=ALU.is_ge, fill=0.0,
                                   base=-SSM_GROUP * g, pattern=[[0, 1]], channel_multiplier=1)
                pool.drain()
                pool.affine_select(out=junk[:, 0:1], in_=junk[:, 0:1], compare_op=ALU.is_ge, fill=0.0,
                                   base=SSM_GROUP * (g + 1) - 1, pattern=[[0, 1]], channel_multiplier=-1)
                pool.drain()
                TT(parity[:, q:q + 1], parity[:, q:q + 1], junk[:, 0:1], ADD)
                pool.drain()
                TT(parity[:, q:q + 1], parity[:, q:q + 1], junk[:, 0:1], ADD)
            pool.drain().then_inc(s["consts_set"], 1)
            pool.wait_ge(s["table_out"], 1)
            pool.dma_start(a["table"], z[0:N_ATT, 0, 0:3 * P]).then_inc(s["table_stored"], 16)
            pool.wait_ge(s["table_stored"], 16)
            pool.dma_start(z[:, :, :].rearrange("p a (h t) -> p (a h) t", t=SEQ),
                           a["table_rows"]).then_inc(s["bias_loaded"], 16)

            def power(L, k):
                for t in range(NT):
                    pool.wait_ge(s["var_ready"], L * 6 + 2 * k + t + 1)
                    TT(rstd[:, t:t + 1], var[:, t:t + 1], mhalf[:, 0:1], ALU.pow).then_inc(s["rs_ready"], 1)

            def update_x(L, k):
                pool.wait_ge(s["gb_loaded"], L * 96 + 32 * (k + 1))
                for t in range(NT):
                    pool.wait_ge(s["z_ready"], L * 6 + 2 * k + t + 1)
                    TT(x[:, t, :], z[:, t, :], gb[:, 0, :], MUL)
                pool.drain()
                for t in range(NT):
                    ins = TT(x[:, t, :], x[:, t, :], gb[:, 1, :], ADD)
                pool.drain().then_inc(s["x_updated"], 1)
                pool.sem_inc(s["gb_used"], 1)

            with pool.Fori(0, DEPTH) as L:
                pool.wait_ge(s["lp_ready"], L + 1)
                pool.wait_ge(s["ssm_loaded"], L * 64 + 64)
                fre, fim = bc(lp[:, Q_FRE, :], SSM_GROUP), bc(lp[:, Q_FIM, :], SSM_GROUP)
                pool.wait_ge(s["bias_read"], 1)
                pool.wait_ge(s["x_ready"], L)
                for part, (f0, f1, op) in enumerate(((fre, fim, SUB), (fim, fre, ADD))):
                    TT(b_tmp[:, 0, :, :], b_nat[:, 0, :, :], f0, MUL)
                    TT(b_tmp[:, 1, :, :], b_nat[:, 1, :, :], f1, MUL)
                    pool.drain()
                    for g in range(2):
                        q = slice(64 * g, 64 * g + 64)
                        TT(b_exp[q, part, :, 16 * g:16 * g + 16], b_tmp[q, 0, :, :], b_tmp[q, 1, :, :], op)
                    pool.drain()
                pool.drain().then_inc(s["b_ready"], 1)
                for part in range(2):
                    for q in range(2):
                        TT(c_exp[:, part, :, q, :], c_nat[:, part, :, :],
                           parity[:, q:q + 1].unsqueeze(2).broadcast_to([P, 2, SSM_STATE]), MUL)
                pool.drain().then_inc(s["c_ready"], 1)
                pool.memset(tw_re[:, :, 0:1], 1.0)
                pool.memset(tw_im[:, :, 0:1], 0.0)
                pool.tensor_copy(tw_re[:, :, 1:2], lp[:, Q_COS, :].unsqueeze(2))
                pool.tensor_copy(tw_im[:, :, 1:2], lp[:, Q_SIN, :].unsqueeze(2))
                pool.drain()

                k = 1
                while k < SEQ:
                    for c0 in range(0, min(k, SEQ - 1 - k), 64):
                        m = min(64, k - c0, SEQ - 1 - k - c0)
                        src, dst = slice(1 + c0, 1 + c0 + m), slice(k + 1 + c0, k + 1 + c0 + m)
                        tmp = [z[:, i // 2, (i % 2) * 512:(i % 2) * 512 + STATE_TILES * m]
                               .rearrange("p (j t) -> p j t", j=STATE_TILES) for i in range(4)]
                        wr = tw_re[:, :, k:k + 1].broadcast_to([P, STATE_TILES, m])
                        wi = tw_im[:, :, k:k + 1].broadcast_to([P, STATE_TILES, m])
                        TT(tmp[0], tw_re[:, :, src], wr, MUL)
                        TT(tmp[1], tw_im[:, :, src], wi, MUL)
                        TT(tmp[2], tw_re[:, :, src], wi, MUL)
                        TT(tmp[3], tw_im[:, :, src], wr, MUL)
                        pool.drain()
                        TT(tw_re[:, :, dst], tmp[0], tmp[1], SUB)
                        TT(tw_im[:, :, dst], tmp[2], tmp[3], ADD)
                        pool.drain()
                    k *= 2
                pool.drain().then_inc(s["twiddles"], 1)

                power(L, 0)
                update_x(L, 0)
                for j in range(STATE_TILES):
                    pool.wait_ge(s["y_ready"], L * 8 + j + 1)
                    if j >= 2:
                        pool.wait_ge(s["c_done"], L * 8 + j - 1)
                    for i, tw in enumerate((tw_re, tw_im)):
                        TT(prod[:, j % 2, i, :, :], ys[:, j % 2, :, :], rep(tw[:, j, :], 2), MUL)
                    pool.drain().then_inc(s["prod_ready"], 1)
                pool.wait_ge(s["ss_scaled"], L + 1)
                TT(rms[:, :, :].rearrange("p t h -> p (t h)"), ss[:, :, :].rearrange("p t h -> p (t h)"),
                   mhalf[:, :], ALU.pow).then_inc(s["rms_ready"], 1)
                power(L, 1)
                update_x(L, 1)
                power(L, 2)
                pool.wait_ge(s["gb_loaded"], L * 96 + 96)
                pool.wait_ge(s["z_ready"], L * 6 + 6)
                TT(x[:, 1, :], z[:, 1, :], gb[:, 0, :], MUL)
                pool.drain()
                TT(x[:, 1, :], x[:, 1, :], gb[:, 1, :], ADD)
                pool.drain().then_inc(s["x_half"], 1)
                pool.wait_ge(s["x_ready"], L + 1)
                pool.sem_inc(s["gb_used"], 1)

        @block.scalar
        def _(act):
            def hi_unit(L, n, k, p):
                act.wait_ge(a_loaded[p // 2], L * (A_GROUPS * 32) + n * 32 + (k + 1) * 32)
                act.wait_ge(a_used, L * A_ALL + n * A_UNITS + (k * A_UNITS + p + 1))
                act.activation(hi_a[:, 2 * p:2 * p + 2, :], raw_a[:, 2 * p:2 * p + 2, :], ACT.Copy).then_inc(a_hi, 1)

            def hi_b_unit(L, m, k, u):
                act.wait_ge(b_loaded[u], L * (B_GROUPS * 16) + m * 16 + (k + 1) * 16)
                act.wait_ge(b_used, L * B_ALL + m * B_UNITS + (k * B_UNITS + u + 1))
                act.activation(hi_b[:, u, :], raw_b[:, u, :], ACT.Copy).then_inc(b_hi, 1)

            def evict(bank, dst, turned, count, done, scale=None):
                act.wait_ge(s[turned], count)
                act.activation(dst, bank, ACT.Copy).then_inc(s[done], 1)

            def ffn(L, a0, b0, f, following):
                base = f * CHUNKS

                def hidden(c, k):
                    act.wait_ge(a_used, L * A_ALL + c * A_UNITS + (A_UNITS + (a0 + k) * A_UNITS + A_UNITS))
                    act.wait_ge(s["h_turned"], L * 2 * CHUNKS + c + (base + k))
                    for t in range(NT):
                        act.activation(h[:, t, :], ps[:, GU + t, 0:CHUNK], ACT.Sigmoid).then_inc(s["gate_act"], 1)

                def hidden_hi(c, k):
                    act.wait_ge(s["h_turned"], L * 2 * CHUNKS + c + (base + k + 1))
                    act.activation(hT_hi[:, :, :].rearrange("p a t -> p (a t)"), ps[:, TR, :],
                                   ACT.Copy).then_inc(s["hT_hi_ready"], 1)

                for p in range(3):
                    hi_unit(L, 0, a0 + 1, p)
                hidden(0, 0)
                hi_unit(L, 0, a0 + 1, 3)
                for u in range(2):
                    hi_b_unit(L, 0, b0, u)
                with act.Fori(1, CHUNKS - 1) as c:
                    hi_unit(L, c, a0 + 1, 0)
                    hi_unit(L, c, a0 + 1, 1)
                    hidden_hi(c, -1)
                    hi_unit(L, c, a0 + 1, 2)
                    hidden(c, 0)
                    hi_unit(L, c, a0 + 1, 3)
                    for u in range(2):
                        hi_b_unit(L, c, b0, u)
                c = CHUNKS - 1
                if following:
                    hi_unit(L, 0, a0 + c + 1, 0)
                    hi_unit(L, 0, a0 + c + 1, 1)
                hidden_hi(0, c - 1)
                if following:
                    hi_unit(L, 0, a0 + c + 1, 2)
                hidden(0, c)
                if following:
                    hi_unit(L, 0, a0 + c + 1, 3)
                for u in range(2):
                    hi_b_unit(L, 0, b0 + c, u)
                hidden_hi(0, c)

            def act_hi(L, k, src, sem_in, count, scale=1.0):
                b = k % 4
                act.wait_ge(s[sem_in], count)
                act.activation(actT_hi[:, 2 * b:2 * b + 2, :].rearrange("p k t -> p (k t)"), src,
                               ACT.Copy).then_inc(s["actT_hi_ready"], 1)

            def norm_turned(L, k, g, b):
                for i in (2, 3):
                    act.wait_ge(s["turned"], L * 12 + 4 * (k + 1) + i + 1)
                    for kk in range(2):
                        c = 2 * i + kk
                        ins = act.activation(lnT[:, c, :], ps[:, LN_BANKS[i], kk * SEQ:(kk + 1) * SEQ], ACT.Identity,
                                             bias=lp[:, b, c:c + 1], scale=lp[:, g, c:c + 1])
                    ins.then_inc(s["lnT_act"], 1)
                for i in range(4):
                    if i < 2:
                        act.wait_ge(s["lnT_scaled"], L * 4 + 2 * k + i + 1)
                    else:
                        act.wait_ge(s["lnT_act"], L * 4 + 2 * k + i - 1)
                    act.activation(actT_hi[:, 2 * i:2 * i + 2, :], lnT[:, 2 * i:2 * i + 2, :],
                                   ACT.Copy).then_inc(s["actT_hi_ready"], 1)

            act.wait_ge(s["prm_out"], 1)
            act.activation(small[:, 0, :], prmT[:, R_DT:R_DT + 16], ACT.Exp).then_inc(s["dt_exp"], 1)
            act.wait_ge(s["lam_in"], 1)
            act.activation(lams[:, :, :], lams[:, :, :], ACT.Exp).then_inc(s["lam_exp"], 1)
            act.wait_ge(s["sin_in"], 1)
            act.activation(small[:, 3, :], small[:, 3, :], ACT.Exp).then_inc(s["mag_ready"], 1)
            act.activation(small[:, 5, :], small[:, 4, :], ACT.Sin)
            act.activation(small[:, 6, :], small[:, 4, :], ACT.Sin, scale=0.5).then_inc(s["sin_out"], 1)

            with act.Fori(0, DEPTH) as L:
                for p in range(4):
                    hi_unit(L, 0, A_FFN1, p)
                for i in range(4):
                    act.wait_ge(s["turned"], L * 12 + i + 1)
                    act.activation(actT_hi[:, 2 * i:2 * i + 2, :].rearrange("p k t -> p (k t)"),
                                   ps[:, LN_BANKS[i], :], ACT.Copy).then_inc(s["actT_hi_ready"], 1)
                evict(ps[:, ACC, :], pT_hi[:, :, :].rearrange("p a t -> p (a t)"), "p_turned", L + 1, "pT_hi_ready")
                ffn(L, A_FFN1, B_FFN1, 0, True)
                act.wait_ge(s["bc_turned"], L * 2 + 1)
                act.activation(inT[:, :, :, :].rearrange("p a r c -> p (a r c)"), ps[:, MISC, :],
                               ACT.Copy).then_inc(s["in_out"], 1)
                act.wait_ge(s["bc_turned"], L * 2 + 2)
                cT = ps[:, TR, :].rearrange("p (r j c) -> p r j c", r=2, c=32)
                for i, (r, sign) in enumerate(((0, 1.0), (0, -1.0), (1, -1.0))):
                    ins = act.activation(outT[:, :, i, :], cT[:, r, :, :], ACT.Copy, scale=sign)
                ins.then_inc(s["c_out"], 1)
                norm_turned(L, 0, Q_G1, Q_B1)
                for i in range(WIN_GROUPS):
                    for p in range(3):
                        hi_unit(L, 0, A_WIN + i + 1, p)
                    c0 = (WIN_GROUPS - 1 - i) * WIN_COLS
                    if i == 0:
                        act.wait_ge(s["actT_ready"], L * 16 + 8)
                    act.wait_ge(s["win_done"], L * WIN_GROUPS + i + 1)
                    for t in range(NT):
                        ins = act.activation(hp[:, t, c0:c0 + WIN_COLS], ps[:, 2 * (i % 2) + t, 0:WIN_COLS], ACT.Copy)
                    ins.then_inc(s["hp_ready"], 1)
                    hi_unit(L, 0, A_WIN + i + 1, 3)
                    if i == 3:
                        for n, (bank, dst) in enumerate(((6, iqT), (7, ksT), (4, saqT), (5, uT))):
                            act.wait_ge(s["ix_turned"], L * 4 + n + 1)
                            act.activation(dst[:, :, :].rearrange("p a t -> p (a t)"), ps[:, bank, :],
                                           ACT.Copy).then_inc(s["ix_out"], 1)
                for n in range(4):
                    dst = (qT, kT)[n // 2][:, 2 * (n % 2):2 * (n % 2) + 2, :]
                    act.wait_ge(s["qk_turned"], L * 4 + n + 1)
                    act.activation(dst.rearrange("p a t -> p (a t)"), ps[:, n, :], ACT.Copy).then_inc(s["qk_out"], 1)
                for i in range(UNITS + 1):
                    if i < UNITS:
                        N = P * (i % 2 + 1)
                        act.wait_ge(s["da_max"], L * UNITS + i + 1)
                        for c in range(2):
                            ins = act.activation(da_e[:, i % 2, c, 0:N], da_e[:, i % 2, c, 0:N], ACT.Exp,
                                                 bias=da_nm[:, i % 2, c:c + 1], accum_out=da_sum[:, i, c:c + 1])
                        ins.then_inc(s["da_exp"], 1)
                    if i >= 1:
                        u = i - 1
                        hd, qb = u // 2, u % 2
                        act.wait_ge(s["da_turned"], L * UNITS + u + 1)
                        act.activation(aT[:, u % 2, 0:P * (qb + 1)], ps[:, 6, 0:P * (qb + 1)],
                                       ACT.Copy).then_inc(s["da_aT"], 1)
                        act.wait_ge(s["da_o"], L * UNITS + u + 1)
                        act.activation(hp[:, qb, hd * DA_V:(hd + 1) * DA_V], ps[:, 7, 0:P], ACT.Copy)
                        act.activation(junk[:, :], ps[:, 7, 0:P], ACT.Square,
                                       accum_out=ss[:, qb, hd:hd + 1]).then_inc(s["da_o_out"], 1)
                for qb in range(NT):
                    N = P * (qb + 1)
                    act.wait_ge(s["sa_max"], L * 2 + qb + 1)
                    for hd in range(SA_HEADS):
                        ins = act.activation(sa_e[:, hd, 0:N], sa_e[:, hd, 0:N], ACT.Exp,
                                             bias=sa_nm[:, qb, hd:hd + 1], accum_out=sa_sum[:, qb, hd:hd + 1])
                    ins.then_inc(s["sa_exp"], 1)
                    for half in range(2):
                        act.wait_ge(s["sa_turned"], L * 4 + 2 * qb + half + 1)
                        w = 2 * N
                        act.activation(sa_aT[:, half * 512:half * 512 + w], ps[:, half, 0:w],
                                       ACT.Copy).then_inc(s["sa_aT_ready"], 1)
                act.wait_ge(s["y_full"], L + 1)
                act.activation(ys2[:, 1, :, :], ys2[:, 0, :, :], ACT.Gelu_apprx_tanh).then_inc(s["gelu_done"], 1)
                act.wait_ge(s["glu_done"], L + 1)
                act.activation(ysg.rearrange("p a t -> p (a t)"), ps[:, 2, :], ACT.Sigmoid).then_inc(s["glu_act"], 1)
                act.wait_ge(s["ssm_out"], L + 1)
                act.activation(actT_hi[:, 4:6, :], ysg, ACT.Copy).then_inc(s["mixT_hi"], 1)
                for n, b in enumerate((0, 1, 3)):
                    act.wait_ge(s["mix_turned"], L * 3 + n + 1)
                    if b < 2:
                        ins = act.activation(actT_hi[:, 2 * b:2 * b + 2, :].rearrange("p k t -> p (k t)"),
                                             ps[:, LN_BANKS[b], :], ACT.Copy, scale=lp[:, Q_MISC, M_SUB:M_SUB + 1])
                    else:
                        ins = act.activation(actT_hi[:, 2 * b:2 * b + 2, :].rearrange("p k t -> p (k t)"),
                                             ps[:, LN_BANKS[b], :], ACT.Copy)
                    ins.then_inc(s["mixT_hi"], 1)
                for p in range(4):
                    hi_unit(L, 0, A_WO + 1, p)
                for p in range(4):
                    hi_unit(L, 0, A_GATE, p)
                for u in range(2):
                    hi_b_unit(L, 0, B_PROJ, u)
                norm_turned(L, 1, Q_G2, Q_B2)
                for i in range(2):
                    for p in range(4):
                        hi_unit(L, 0, A_GATE + i + 1, p)
                    act.wait_ge(s["gate_done"], L * 2 + i + 1)
                    act.wait_ge(s["x_updated"], L * 2 + 2)
                    for t in range(NT):
                        act.activation(z[:, t, i * 512:(i + 1) * 512], ps[:, (GU, TR)[i] + t, :],
                                       ACT.Sigmoid).then_inc(s["gate_sig"], 1)
                ffn(L, A_FFN2, B_FFN2, 1, False)

        @block.vector
        def _(dve):
            TT, TS, STT = dve.tensor_tensor, dve.tensor_scalar, dve.scalar_tensor_tensor
            MUL, ADD, SUB, MAX = ALU.mult, ALU.add, ALU.subtract, ALU.max

            def lo_unit(L, n, k, p):
                dve.wait_ge(a_hi, L * A_ALL + n * A_UNITS + (k * A_UNITS + p + 1))
                q = slice(2 * p, 2 * p + 2)
                TT(lo_a[:, q, :], raw_a[:, q, :], hi_a[:, q, :].bitcast(F32), SUB).then_inc(a_lo, 1)

            def lo_b_unit(L, m, k, u):
                dve.wait_ge(b_hi, L * B_ALL + m * B_UNITS + (k * B_UNITS + u + 1))
                TT(lo_b[:, u, :], raw_b[:, u, :], hi_b[:, u, :].bitcast(F32), SUB).then_inc(b_lo, 1)

            def ffn(L, a0, b0, f, following):
                base = f * CHUNKS

                def hidden(c, k):
                    for t in range(NT):
                        dve.wait_ge(s["gate_act"], L * 4 * CHUNKS + c * 2 + (2 * (base + k) + t + 1))
                        TT(h[:, t, :], h[:, t, :], ps[:, GU + t, 0:CHUNK], MUL)
                    dve.drain()
                    for t in range(NT):
                        TT(h[:, t, :], h[:, t, :], ps[:, GU + t, CHUNK:2 * CHUNK], MUL).then_inc(s["h_ready"], 1)

                def hidden_lo(c, k):
                    dve.wait_ge(s["hT_hi_ready"], L * 2 * CHUNKS + c + (base + k + 1))
                    TT(hT_lo[:, :, :].rearrange("p a t -> p (a t)"), ps[:, TR, :],
                       hT_hi[:, :, :].rearrange("p a t -> p (a t)").bitcast(F32), SUB).then_inc(s["hT_ready"], 1)

                for p in range(3):
                    lo_unit(L, 0, a0 + 1, p)
                hidden(0, 0)
                lo_unit(L, 0, a0 + 1, 3)
                for u in range(2):
                    lo_b_unit(L, 0, b0, u)
                with dve.Fori(1, CHUNKS - 1) as c:
                    lo_unit(L, c, a0 + 1, 0)
                    lo_unit(L, c, a0 + 1, 1)
                    hidden_lo(c, -1)
                    lo_unit(L, c, a0 + 1, 2)
                    hidden(c, 0)
                    lo_unit(L, c, a0 + 1, 3)
                    for u in range(2):
                        lo_b_unit(L, c, b0, u)
                c = CHUNKS - 1
                if following:
                    lo_unit(L, 0, a0 + c + 1, 0)
                    lo_unit(L, 0, a0 + c + 1, 1)
                hidden_lo(0, c - 1)
                if following:
                    lo_unit(L, 0, a0 + c + 1, 2)
                hidden(0, c)
                if following:
                    lo_unit(L, 0, a0 + c + 1, 3)
                for u in range(2):
                    lo_b_unit(L, 0, b0 + c, u)
                hidden_lo(0, c)

            def norm(L, k, coef, eps):
                for t in range(NT):
                    dve.wait_ge(s["ffn_done"], L * 6 + 2 * k + t + 1)
                    for half in range(2):
                        q = slice(512 * half, 512 * half + 512)
                        STT(z[:, t, q], x[:, t, q], coef, ps[:, ACC + 2 * t + half, :], MUL, ADD)
                    dve.drain().then_inc(s["acc_read"], 1)
                    for half in range(2):
                        dve.bn_stats(stats[:, t, half, :], z[:, t, 512 * half:512 * half + 512])
                    dve.drain()
                    dve.bn_aggr(mv[:, t, :], stats[:, t, :, :].rearrange("p a b -> p (a b)"))
                    dve.drain()
                    TS(var[:, t:t + 1], mv[:, t, 1:2], eps, None, ADD).then_inc(s["var_ready"], 1)
                for t in range(NT):
                    dve.wait_ge(s["rs_ready"], L * 6 + 2 * k + t + 1)
                    TS(z[:, t, :], z[:, t, :], mv[:, t, 0:1], rstd[:, t:t + 1], SUB, MUL).then_inc(s["z_ready"], 1)

            def norm_turned(L, k, g, b):
                for i in (0, 1):
                    dve.wait_ge(s["turned"], L * 12 + 4 * (k + 1) + i + 1)
                    for kk in range(2):
                        c = 2 * i + kk
                        ins = TS(lnT[:, c, :], ps[:, LN_BANKS[i], kk * SEQ:(kk + 1) * SEQ],
                                 lp[:, g, c:c + 1], lp[:, b, c:c + 1], MUL, ADD)
                    ins.then_inc(s["lnT_scaled"], 1)
                base = (4, 8)[k]
                for i in range(4):
                    dve.wait_ge(s["actT_hi_ready"], L * 12 + base + i + 1)
                    q = slice(2 * i, 2 * i + 2)
                    TT(actT_lo[:, q, :], lnT[:, q, :], actT_hi[:, q, :].bitcast(F32), SUB).then_inc(s["actT_ready"], 1)

            def flat(t):
                return t.rearrange("p a t -> p (a t)")

            dve.sem_inc(a_lo, A_UNITS)
            dve.sem_inc(b_lo, B_UNITS)
            dve.wait_ge(s["dtrow_loaded"], 16)
            dve.tensor_copy(rows[R_DT:R_DT + 16, :].rearrange("p (g q) -> p g q", g=2),
                            bc(dt_row[R_DT:R_DT + 16, :], SSM_STATE)).then_inc(s["dt_expanded"], 1)
            dve.wait_ge(s["lamv_loaded"], 64)
            for i in range(2):
                TT(lamv[:, 2 * i, :, :], lamv[:, 2 * i, :, :], lamv[:, 2 * i + 1, :, :], MUL)
            dve.drain()
            dve.tensor_reduce(lams[:, 0, :], lamv[:, 0, :, :], AX.X, ADD)
            dve.tensor_reduce(lams[:, 1, :], lamv[:, 2, :, :], AX.X, ADD).then_inc(s["lam_in"], 1)
            dve.wait_ge(s["rows_turned"], 1)
            dve.tensor_copy(prmT[:, :], ps[:, 0, 0:ROWS]).then_inc(s["prm_out"], 1)
            dve.wait_ge(s["table_turned"], 1)
            dve.tensor_copy(z[0:N_ATT, 0, 0:3 * P], ps[0:N_ATT, 1, 0:3 * P]).then_inc(s["table_out"], 1)
            dve.memset(par[:, Q_MISC, :, :], 0.0)
            dve.drain()
            for i in range(4):
                dve.tensor_copy(par[:, Q_G1 + i, :, :].rearrange("p l k -> p (l k)"), prmT[:, 16 * i:16 * i + 16])
            for layer in range(DEPTH):
                dve.tensor_copy(par[:, Q_MISC, layer, M_D:M_D + 2], prmT[:, R_D + 2 * layer:R_D + 2 * layer + 2])
                TS(par[:, Q_MISC, layer, M_SUB:M_SUB + 1], prmT[:, R_SUB + layer:R_SUB + layer + 1],
                   1.0 - lam_init(layer), None, MUL)
            dve.wait_ge(s["lam_exp"], 1)
            for layer in range(DEPTH):
                out = par[:, Q_MISC, layer, M_NLAM:M_NLAM + 1]
                TT(out, lams[:, 1, layer:layer + 1], lams[:, 0, layer:layer + 1], SUB)
                dve.drain()
                TS(out, out, lam_init(layer), None, SUB)
            re, im = prmT[:, R_RE:R_RE + 16], prmT[:, R_IM:R_IM + 16]
            sm = [small[:, i, :] for i in range(12)]
            dve.wait_ge(s["dt_exp"], 1)
            TT(sm[3], re, sm[0], MUL)
            TT(sm[4], im, sm[0], MUL)
            dve.drain()
            TS(sm[1], sm[4], 1 / TWO_PI, ROUND, MUL, ADD)
            dve.drain()
            TS(sm[1], sm[1], ROUND, None, SUB)
            for part in (PI_A, PI_B, PI_C):
                dve.drain()
                STT(sm[4], sm[1], -part, sm[4], MUL, ADD)
            dve.drain()
            TS(sm[4], sm[4], 3.1415925, -3.1415925, ALU.min, MAX)
            dve.drain().then_inc(s["sin_in"], 1)
            dve.wait_ge(s["mag_ready"], 1)
            dve.wait_ge(s["sin_out"], 1)
            TT(sm[6], sm[6], sm[6], MUL)
            TT(sm[7], sm[3], sm[5], MUL)
            TT(sm[8], re, re, MUL)
            TT(sm[9], im, im, MUL)
            dve.drain()
            TS(sm[6], sm[6], -2.0, 1.0, MUL, ADD)
            TT(sm[8], sm[8], sm[9], ADD)
            dve.drain()
            dve.reciprocal(sm[8], sm[8])
            TT(sm[9], sm[3], sm[6], MUL)
            dve.drain()
            TS(sm[9], sm[9], -1.0, None, ADD)
            dve.drain()
            TT(sm[10], sm[9], re, MUL)
            TT(sm[11], sm[7], im, MUL)
            TT(sm[1], sm[7], re, MUL)
            TT(sm[2], sm[9], im, MUL)
            dve.drain()
            TT(sm[10], sm[10], sm[11], ADD)
            TT(sm[1], sm[1], sm[2], SUB)
            dve.drain()
            TT(sm[10], sm[10], sm[8], MUL)
            TT(sm[1], sm[1], sm[8], MUL)
            dve.drain()
            for q, src in ((Q_MAG, 3), (Q_COS, 6), (Q_SIN, 5), (Q_FRE, 10), (Q_FIM, 1)):
                dve.tensor_copy(par[:, q, :, :].rearrange("p l k -> p (l k)"), sm[src])
            dve.drain()
            dve.wait_ge(s["consts_set"], 1)
            for b in range(4):
                dve.wait_ge(s["bias_flipped"], b + 1)
                TT(bias[:, 2 * b:2 * b + 2, :], ps[:, ACC + b, :].rearrange("p (h t) -> p h t", h=2),
                   rep(causal[:, :], 2), ADD).then_inc(s["bias_out"], 1)
            dve.drain().then_inc(s["bias_read"], 1)

            with dve.Fori(0, DEPTH) as L:
                dve.tensor_copy(lp[:, :, :], par[:, :, bass.ds(L, 1), :].rearrange("p q l k -> p q (l k)"))\
                   .then_inc(s["lp_ready"], 1)
                for p in range(4):
                    lo_unit(L, 0, A_FFN1, p)
                for i in range(4):
                    dve.wait_ge(s["actT_hi_ready"], L * 12 + i + 1)
                    q = slice(2 * i, 2 * i + 2)
                    TT(flat(actT_lo[:, q, :]), ps[:, LN_BANKS[i], :], flat(actT_hi[:, q, :]).bitcast(F32),
                       SUB).then_inc(s["actT_ready"], 1)
                dve.wait_ge(s["pT_hi_ready"], L + 1)
                TT(flat(pT_lo[:, :, :]), ps[:, ACC, :], flat(pT_hi[:, :, :]).bitcast(F32), SUB).then_inc(s["pT_ready"], 1)
                ffn(L, A_FFN1, B_FFN1, 0, True)
                dve.wait_ge(s["twiddles"], L + 1)
                norm(L, 0, 2 * ALPHA, 4 * LN_EPS)
                norm_turned(L, 0, Q_G1, Q_B1)

                def index_scores(qb, n):
                    N = P * (qb + 1)
                    off = SEQ - N
                    dve.wait_ge(s["ixs_done"], L * 2 + n + 1)
                    for hh in range(2):
                        STT(relu_w[:, 4 * hh:4 * hh + 4, 0:N], ps[:, 4:8, hh * SEQ:hh * SEQ + N], 0.0,
                            bc(wis[:, qb, 4 * hh:4 * hh + 4], N), MAX, MUL)
                    dve.drain().then_inc(s["ixs_read"], 1)
                    dve.tensor_reduce(isc[:, 0:N], relu_w[:, :, 0:N].rearrange("p h s -> p s h"), AX.X, ADD)
                    dve.drain()
                    TT(work[:, 0:N], isc[:, 0:N], causal[:, off:SEQ], ADD)
                    for _ in range(TOPK // 8):
                        dve.drain()
                        dve.max(top8[:, :], work[:, 0:N])
                        dve.drain()
                        dve.match_replace(work[:, 0:N], top8[:, :], work[:, 0:N], TAKEN)
                    dve.drain()
                    TS(sel[:, qb, 0:N], work[:, 0:N], TAKEN, NEG, ALU.not_equal, MUL)
                    dve.drain()

                for i in range(WIN_GROUPS):
                    for p in range(4):
                        lo_unit(L, 0, A_WIN + i + 1, p)
                    if i == 2:
                        dve.wait_ge(s["hp_ready"], L * WIN_GROUPS + 2)
                        dve.tensor_copy(kdup[:, :, 0:P].rearrange("p t (r d) -> p t r d", r=4),
                                        hp[:, :, C_IK:C_IK + 32].unsqueeze(2).broadcast_to([P, NT, 4, 32]))
                        dve.tensor_copy(kdup[:, :, P:2 * P].rearrange("p t (r d) -> p t r d", r=2),
                                        hp[:, :, C_SK:C_SK + 64].unsqueeze(2).broadcast_to([P, NT, 2, 64]))
                        TS(wis[:, :, :], hp[:, :, C_IW:C_IW + 8], IDX_HEADS ** -0.5 * IDX_DIM ** -0.5, None, MUL)
                        dve.drain().then_inc(s["kdup_ready"], 1)
                    if i == 4:
                        index_scores(1, 0)
                    if i == 5:
                        index_scores(0, 1)

                dve.wait_ge(s["x_updated"], L * 2 + 1)
                for i in range(UNITS + 1):
                    if i < UNITS:
                        hd, qb = i // 2, i % 2
                        N = P * (qb + 1)
                        dve.wait_ge(s["das_done"], L * UNITS + i + 1)
                        STT(da_e[:, i % 2, :, 0:N], ps[:, 4:6, 0:N], DA_QK ** -0.5,
                            rep(bias[:, hd, SEQ - N:SEQ], 2), MUL, ADD)
                        dve.drain().then_inc(s["das_read"], 1)
                        dve.tensor_reduce(da_nm[:, i % 2, :], da_e[:, i % 2, :, 0:N], AX.X, MAX,
                                          negate=True).then_inc(s["da_max"], 1)
                        j = i
                        dve.wait_ge(s["bu_done"], L * 8 + j + 1)
                        bu = ps[:, j % 2, :].rearrange("p (c t) -> p c t", c=2)
                        TT(rot[:, 0, :, :], bu, rep(tw_re[:, j, :], 2), MUL)
                        TT(rot[:, 1, :, :], bu, rep(tw_im[:, j, :], 2), MUL)
                        dve.drain().then_inc(s["bu_read"], 1)
                        TT(derot[:, 0, :], rot[:, 0, 0, :], rot[:, 1, 1, :], ADD)
                        TT(derot[:, 1, :], rot[:, 0, 1, :], rot[:, 1, 0, :], SUB)
                        dve.drain()
                        if j >= 2:
                            dve.wait_ge(s["prod_ready"], L * 8 + j - 1)
                        for c in range(2):
                            ins = dve.tensor_tensor_scan(ys[:, j % 2, c, :],
                                                         lp[:, Q_MAG, j:j + 1].broadcast_to([P, SEQ]),
                                                         derot[:, c, :], 0.0, MUL, ADD)
                        dve.drain().then_inc(s["y_ready"], 1)
                    if i < UNITS:
                        u = i
                        dve.wait_ge(s["da_exp"], L * UNITS + u + 1)
                        dve.reciprocal(da_r[:, u, :], da_sum[:, u, :])
                        dve.drain()
                        TT(da_r[:, u, 1:2], da_r[:, u, 1:2], lp[:, Q_MISC, M_NLAM:M_NLAM + 1], MUL)
                        TS(da_e[:, u % 2, 0, 0:N], da_e[:, u % 2, 0, 0:N], da_r[:, u, 0:1], None, MUL)
                        dve.drain()
                        STT(da_e[:, u % 2, 0, 0:N], da_e[:, u % 2, 1, 0:N], da_r[:, u, 1:2],
                            da_e[:, u % 2, 0, 0:N], MUL, ADD)
                        dve.drain().then_inc(s["da_a"], 1)
                dve.wait_ge(s["da_o_out"], L * UNITS + UNITS)
                TS(ss[:, :, :], ss[:, :, :], 1.0 / DA_V, LN_EPS, MUL, ADD).then_inc(s["ss_scaled"], 1)
                dve.wait_ge(s["c_done"], L * 8 + 8)
                for qb in range(NT):
                    N = P * (qb + 1)
                    dve.wait_ge(s["sas_done"], L * 2 + qb + 1)
                    STT(sa_e[:, :, 0:N], ps[:, 4:8, 0:N], SA_DIM ** -0.5, bias[:, DA_HEADS:, SEQ - N:SEQ], MUL, ADD)
                    dve.drain().then_inc(s["sas_read"], 1)
                    TT(sa_e[:, :, 0:N], sa_e[:, :, 0:N], rep(sel[:, qb, 0:N], SA_HEADS), ADD)
                    dve.drain()
                    dve.tensor_reduce(sa_nm[:, qb, :], sa_e[:, :, 0:N], AX.X, MAX, negate=True).then_inc(s["sa_max"], 1)
                    if qb == 0:
                        dve.wait_ge(s["rms_ready"], L + 1)
                        for t in range(NT):
                            m = hp[:, t, 0:DA_HEADS * DA_V].rearrange("p (h e) -> p h e", h=DA_HEADS)
                            TT(m, m, bc(rms[:, t, :], DA_V), MUL)
                        dve.drain().then_inc(s["mix_da"], 1)
                    dve.wait_ge(s["sa_exp"], L * 2 + qb + 1)
                    dve.reciprocal(sa_sum[:, qb, :], sa_sum[:, qb, :])
                    dve.drain()
                    dve.wait_ge(s["sa_o"], L * 2 + qb + 1)
                    TT(hp[:, qb, 768:1024].rearrange("p (h e) -> p h e", h=SA_HEADS),
                       ps[:, 3, 0:256].rearrange("p (h e) -> p h e", h=SA_HEADS), bc(sa_sum[:, qb, :], SA_DIM),
                       MUL).then_inc(s["mix_sa"], 1)
                for t in range(2):
                    ins = STT(ys2[:, 0, t, :], uT[:, t, :], lp[:, Q_MISC, M_D + t:M_D + t + 1],
                              ps[:, 2, t * SEQ:(t + 1) * SEQ], MUL, ADD)
                ins.then_inc(s["y_full"], 1)
                dve.wait_ge(s["glu_act"], L + 1)
                TT(ysg, ysg, ys2[:, 1, :, :], MUL).then_inc(s["ssm_out"], 1)
                dve.wait_ge(s["mixT_hi"], L * 4 + 1)
                TT(actT_lo[:, 4:6, :], ysg, actT_hi[:, 4:6, :].bitcast(F32), SUB).then_inc(s["actT_ready"], 1)
                for n, b in enumerate((0, 1, 3)):
                    dve.wait_ge(s["mixT_hi"], L * 4 + n + 2)
                    q = slice(2 * b, 2 * b + 2)
                    bank, hi = ps[:, LN_BANKS[b], :], flat(actT_hi[:, q, :]).bitcast(F32)
                    if b < 2:
                        ins = STT(flat(actT_lo[:, q, :]), bank, lp[:, Q_MISC, M_SUB:M_SUB + 1], hi, MUL, SUB)
                    else:
                        ins = TT(flat(actT_lo[:, q, :]), bank, hi, SUB)
                    ins.then_inc(s["actT_ready"], 1)
                for p in range(4):
                    lo_unit(L, 0, A_WO + 1, p)
                for p in range(4):
                    lo_unit(L, 0, A_GATE, p)
                for u in range(2):
                    lo_b_unit(L, 0, B_PROJ, u)
                norm(L, 1, ALPHA, LN_EPS)
                norm_turned(L, 1, Q_G2, Q_B2)
                for i in range(2):
                    for p in range(4):
                        lo_unit(L, 0, A_GATE + i + 1, p)
                    for t in range(NT):
                        q = slice(512 * i, 512 * i + 512)
                        dve.wait_ge(s["gate_sig"], L * 4 + 2 * i + t + 1)
                        if i == 0 and t == 0:
                            dve.wait_ge(s["proj_done"], L * 2 + 2)
                        TT(z[:, t, q], z[:, t, q], ps[:, ACC + 2 * t + i, :], MUL)
                        dve.drain()
                        STT(x[:, t, q], x[:, t, q], ALPHA, z[:, t, q], MUL, ADD).then_inc(s["ple_done"], 1)
                ffn(L, A_FFN2, B_FFN2, 1, False)
                norm(L, 2, 2.0, 4 * LN_EPS)
                dve.drain()
                dve.wait_ge(s["gb_loaded"], L * 96 + 96)
                TT(x[:, 0, :], z[:, 0, :], gb[:, 0, :], MUL)
                dve.drain()
                TT(x[:, 0, :], x[:, 0, :], gb[:, 1, :], ADD)
                dve.drain().then_inc(s["x_ready"], 1)

        @block.tensor
        def _(pe):
            def turn(out, src):
                return pe.transpose(out, src, ident[:, :])

            def wait_a(L, n, k, p):
                pe.wait_ge(a_lo, L * A_ALL + n * A_UNITS + (A_UNITS + k * A_UNITS + p + 1))

            def group(L, n, k, bank, cols, middle=None):
                for p in range(A_UNITS):
                    wait_a(L, n, k, p)
                    for kt in (2 * p, 2 * p + 1):
                        for t in range(NT):
                            q = slice(t * P, (t + 1) * P)
                            ins = mm3(pe, ps[:, bank + t, 0:cols], actT_hi[:, kt, q], actT_lo[:, kt, q],
                                      hi_a[:, kt, 0:cols], lo_a[:, kt, 0:cols], kt == 0, kt == KT - 1)
                    ins.then_inc(a_used, 1)
                    if p == 1 and middle:
                        middle()

            def rows2(L, m, k, hi, lo, first, last, done=None):
                if not last:
                    for u in range(B_UNITS):
                        pe.wait_ge(b_lo, L * B_ALL + m * B_UNITS + (B_UNITS + k * B_UNITS + u + 1))
                        for t in range(NT):
                            for half in range(2):
                                q, w = slice(t * P, (t + 1) * P), slice(half * 512, half * 512 + 512)
                                ins = mm3(pe, ps[:, ACC + 2 * t + half, :], hi[:, u, q], lo[:, u, q],
                                          hi_b[:, u, w], lo_b[:, u, w], first and u == 0, False)
                        ins.then_inc(b_used, 1)
                    return
                pe.wait_ge(b_lo, L * B_ALL + m * B_UNITS + (B_UNITS + (k + 1) * B_UNITS))
                for t in range(NT):
                    for u in range(B_UNITS):
                        for half in range(2):
                            q, w = slice(t * P, (t + 1) * P), slice(half * 512, half * 512 + 512)
                            ins = mm3(pe, ps[:, ACC + 2 * t + half, :], hi[:, u, q], lo[:, u, q],
                                      hi_b[:, u, w], lo_b[:, u, w], first and u == 0, u == B_UNITS - 1)
                    ins.then_inc(s[done], 1)
                pe.drain().then_inc(b_used, 2)

            def ffn(L, a0, b0, f):
                base = f * CHUNKS

                def turn_h(c, k):
                    pe.wait_ge(s["h_ready"], L * 4 * CHUNKS + c * 2 + 2 * (base + k + 1))
                    for u in range(2):
                        for t in range(NT):
                            ins = turn(ps[:, TR, u * SEQ + t * P:u * SEQ + (t + 1) * P], h[:, t, u * P:(u + 1) * P])
                    ins.then_inc(s["h_turned"], 1)

                def gate_up(c, k, middle=None):
                    pe.wait_ge(s["h_ready"], L * 4 * CHUNKS + c * 2 + 2 * (base + k))
                    group(L, c, a0 + k, GU, 2 * CHUNK, middle)

                def down(c, k, first=False, last=False):
                    pe.wait_ge(s["hT_ready"], L * 2 * CHUNKS + c + (base + k + 1))
                    rows2(L, c, b0 + k, hT_hi, hT_lo, first, last, "ffn_done")

                gate_up(0, 0)
                gate_up(0, 1, lambda: turn_h(0, 0))
                down(0, 0, first=True)
                with pe.Fori(2, CHUNKS) as c:
                    gate_up(c, 0, lambda: turn_h(c, -1))
                    down(c, -1)
                turn_h(0, CHUNKS - 1)
                down(0, CHUNKS - 1, last=True)

            def turn_norm(L, k, src, ready):
                for t in range(NT):
                    ready(t)
                    for i in range(4):
                        for kk in range(2):
                            c = 2 * i + kk
                            ins = turn(ps[:, LN_BANKS[i], kk * SEQ + t * P:kk * SEQ + (t + 1) * P],
                                       src[:, t, c * P:(c + 1) * P])
                        if t == NT - 1:
                            ins.then_inc(s["turned"], 1)

            def wait_act(L, k):
                pe.wait_ge(s["actT_ready"], L * 16 + k)

            pe.sem_inc(a_used, A_UNITS)
            pe.sem_inc(b_used, B_UNITS)
            pe.wait_ge(s["consts_set"], 1)
            pe.wait_ge(s["rows_loaded"], 16 * 8)
            pe.wait_ge(s["dt_expanded"], 1)
            pe.transpose(ps[:, 0, 0:ROWS], rows[0:ROWS, :], ident[0:ROWS, 0:ROWS]).then_inc(s["rows_turned"], 1)
            pe.wait_ge(s["sel_loaded"], 32)
            pe.matmul(ps[0:N_ATT, 1, 0:3 * P], tw_re[0:REL_BUCKETS, 0, 0:N_ATT],
                      tw_im[0:REL_BUCKETS, 0:2, :].rearrange("p a t -> p (a t)")[:, 0:3 * P],
                      start=True, stop=True).then_inc(s["table_turned"], 1)
            pe.wait_ge(s["bias_loaded"], 16)
            for b in range(4):
                pe.matmul(ps[:, ACC + b, :], flip[:, :], z[:, b // 2, (b % 2) * 512:(b % 2) * 512 + 512],
                          start=True, stop=True).then_inc(s["bias_flipped"], 1)
            pe.wait_ge(s["prm_out"], 1)
            pe.wait_ge(s["table_out"], 1)
            pe.wait_ge(s["x_loaded"], 16)

            with pe.Fori(0, DEPTH) as L:
                def input_ready(t):
                    pe.wait_ge(s["x_ready" if t == 0 else "x_half"], L)
                turn_norm(L, 0, x, input_ready)
                pe.wait_ge(s["bias_read"], 1)
                pe.wait_ge(s["p_loaded"], L * 16 + 16)
                for u in range(2):
                    for t in range(NT):
                        ins = turn(ps[:, ACC, u * SEQ + t * P:u * SEQ + (t + 1) * P], p_nat[:, t, u * P:(u + 1) * P])
                ins.then_inc(s["p_turned"], 1)
                wait_act(L, 4)
                pe.wait_ge(s["pT_ready"], L + 1)
                ffn(L, A_FFN1, B_FFN1, 0)
                pe.wait_ge(s["b_ready"], L + 1)
                for half in range(2):
                    for part in range(2):
                        ins = turn(ps[:, MISC, (2 * half + part) * P:(2 * half + part + 1) * P],
                                   b_exp[:, part, 4 * half:4 * half + 4, :].rearrange("p j c -> p (j c)"))
                ins.then_inc(s["bc_turned"], 1)
                pe.wait_ge(s["c_ready"], L + 1)
                pe.wait_ge(s["hT_ready"], L * 2 * CHUNKS + CHUNKS)
                for part in range(2):
                    for half in range(2):
                        ins = turn(ps[:, TR, (2 * part + half) * P:(2 * part + half + 1) * P],
                                   c_exp[:, part, half, :, :].rearrange("p q d -> p (q d)"))
                ins.then_inc(s["bc_turned"], 1)
                pe.wait_ge(s["in_out"], L + 1)
                pe.wait_ge(s["c_out"], L + 1)
                turn_norm(L, 1, z, lambda t: pe.wait_ge(s["z_ready"], L * 6 + t + 1))
                for i in range(WIN_GROUPS):
                    if i >= 2:
                        pe.wait_ge(s["hp_ready"], L * WIN_GROUPS + i - 1)
                    if i == 0:
                        wait_act(L, 8)
                    group(L, 0, A_WIN + i, 2 * (i % 2), WIN_COLS)
                    pe.drain().then_inc(s["win_done"], 1)
                    if i == 3:
                        pe.wait_ge(s["hp_ready"], L * WIN_GROUPS + 3)
                        pe.wait_ge(s["kdup_ready"], L + 1)
                        for bank, src, c0 in ((6, hp, C_IQ), (7, kdup, 0), (4, hp, C_SQ), (5, hp, C_U)):
                            for u in range(2):
                                for t in range(NT):
                                    ins = turn(ps[:, bank, u * SEQ + t * P:u * SEQ + (t + 1) * P],
                                               src[:, t, c0 + u * P:c0 + (u + 1) * P])
                            ins.then_inc(s["ix_turned"], 1)
                    if i >= 4:
                        qb = 5 - i
                        N = P * (qb + 1)
                        pe.wait_ge(s["ix_out"], L * 4 + 4)
                        if i == 5:
                            pe.wait_ge(s["ixs_read"], L * 2 + 1)
                        for hd in range(IDX_HEADS):
                            r = 32 * (hd % 4)
                            ins = pe.matmul(ps[:, 4 + hd % 4, (hd // 4) * SEQ:(hd // 4) * SEQ + N],
                                            iqT[r:r + 32, hd // 4, qb * P:(qb + 1) * P], ksT[r:r + 32, 0, 0:N],
                                            start=True, stop=True)
                        pe.drain().then_inc(s["ixs_done"], 1)
                pe.wait_ge(s["hp_ready"], L * WIN_GROUPS + WIN_GROUPS)
                for n in range(4):
                    for u in range(2):
                        for t in range(NT):
                            c0 = (2 * n + u) * P
                            ins = turn(ps[:, n, u * SEQ + t * P:u * SEQ + (t + 1) * P], hp[:, t, c0:c0 + P])
                    ins.then_inc(s["qk_turned"], 1)
                pe.wait_ge(s["qk_out"], L * 4 + 4)
                pe.wait_ge(s["ixs_read"], L * 2 + 2)
                for i in range(UNITS + 2):
                    if i < UNITS:
                        hd, qb = i // 2, i % 2
                        N = P * (qb + 1)
                        if i >= 1:
                            pe.wait_ge(s["das_read"], L * UNITS + i)
                        for c in range(2):
                            r = slice(64 * c, 64 * c + 64)
                            ins = pe.matmul(ps[:, 4 + c, 0:N], qT[r, hd, qb * P:(qb + 1) * P], kT[r, hd, 0:N],
                                            start=True, stop=True)
                        pe.drain().then_inc(s["das_done"], 1)
                        j = i
                        if j >= 2:
                            pe.wait_ge(s["bu_read"], L * 8 + j - 1)
                        r = slice(32 * (j % 4), 32 * (j % 4) + 32)
                        for part in range(2):
                            ins = pe.matmul(ps[:, j % 2, part * SEQ:(part + 1) * SEQ], inT[r, j // 4, part, :],
                                            uT[r, j // 4, :], start=True, stop=True)
                        ins.then_inc(s["bu_done"], 1)
                    if 1 <= i <= UNITS:
                        u = i - 1
                        hd, qb = u // 2, u % 2
                        pe.wait_ge(s["da_a"], L * UNITS + u + 1)
                        if u >= 1:
                            pe.wait_ge(s["da_aT"], L * UNITS + u)
                        for kb in range(qb + 1):
                            ins = turn(ps[:, 6, kb * P:(kb + 1) * P], da_e[:, u % 2, 0, kb * P:(kb + 1) * P])
                        ins.then_inc(s["da_turned"], 1)
                        pe.wait_ge(s["da_aT"], L * UNITS + u + 1)
                        if u >= 1:
                            pe.wait_ge(s["da_o_out"], L * UNITS + u)
                        for kb in range(qb + 1):
                            ins = pe.matmul(ps[:, 7, 0:P], aT[:, u % 2, kb * P:(kb + 1) * P],
                                            hp[:, kb, C_V + hd * DA_V:C_V + (hd + 1) * DA_V],
                                            start=kb == 0, stop=kb == qb)
                        ins.then_inc(s["da_o"], 1)
                    if i >= 2:
                        j = i - 2
                        pe.wait_ge(s["prod_ready"], L * 8 + j + 1)
                        r = slice(32 * (j % 4), 32 * (j % 4) + 32)
                        for n, (w, tw, part) in enumerate(((0, 0, 0), (1, 1, 1), (2, 1, 0), (2, 0, 1))):
                            ins = pe.matmul(ps[r, 2, (j // 4) * SEQ:(j // 4 + 1) * SEQ], outT[:, j, w, :],
                                            prod[:, j % 2, tw, part, :], start=n == 0, stop=n == 3)
                        ins.then_inc(s["c_done"], 1)
                pe.wait_ge(s["da_o_out"], L * UNITS + UNITS)
                for qb in range(NT):
                    N = P * (qb + 1)
                    if qb:
                        pe.wait_ge(s["sas_read"], L * 2 + 1)
                    for hd in range(SA_HEADS):
                        r = slice(64 * (hd % 2), 64 * (hd % 2) + 64)
                        ins = pe.matmul(ps[:, 4 + hd, 0:N], saqT[r, hd // 2, qb * P:(qb + 1) * P], ksT[r, 1, 0:N],
                                        start=True, stop=True)
                    pe.drain().then_inc(s["sas_done"], 1)
                    pe.wait_ge(s["sa_exp"], L * 2 + qb + 1)
                    if qb:
                        pe.wait_ge(s["sa_aT_ready"], L * 4 + 2)
                        pe.wait_ge(s["mix_sa"], L * 2 + 1)
                    for half in range(2):
                        for b in range(2 * (qb + 1)):
                            hd, kb = 2 * half + b // (qb + 1), b % (qb + 1)
                            ins = turn(ps[:, half, b * P:(b + 1) * P], sa_e[:, hd, kb * P:(kb + 1) * P])
                        ins.then_inc(s["sa_turned"], 1)
                    pe.wait_ge(s["sa_aT_ready"], L * 4 + 2 * qb + 2)
                    for hd in range(SA_HEADS):
                        for kb in range(qb + 1):
                            c0 = (hd // 2) * 512 + ((hd % 2) * (qb + 1) + kb) * P
                            ins = pe.matmul(ps[:, 3, hd * SA_DIM:(hd + 1) * SA_DIM], sa_aT[:, c0:c0 + P],
                                            hp[:, kb, C_SV:C_SV + SA_DIM], start=kb == 0, stop=kb == qb)
                    ins.then_inc(s["sa_o"], 1)
                pe.wait_ge(s["gelu_done"], L + 1)
                pe.wait_ge(s["glu_loaded"], L * 16 + 16)
                for o in range(2):
                    for t in range(2):
                        ins = pe.matmul(ps[:, 2, o * SEQ:(o + 1) * SEQ], glu[:, t, o * P:(o + 1) * P],
                                        ys2[:, 1, t, :], start=t == 0, stop=t == 1)
                ins.then_inc(s["glu_done"], 1)
                pe.wait_ge(s["mix_da"], L + 1)
                pe.wait_ge(s["mix_sa"], L * 2 + 2)
                for b, c0 in ((0, 0), (1, 256), (3, 768)):
                    for u in range(2):
                        for t in range(NT):
                            ins = turn(ps[:, LN_BANKS[b], u * SEQ + t * P:u * SEQ + (t + 1) * P],
                                       hp[:, t, c0 + u * P:c0 + (u + 1) * P])
                    ins.then_inc(s["mix_turned"], 1)
                wait_act(L, 12)
                for i in range(2):
                    for p in range(A_UNITS):
                        wait_a(L, 0, A_WO + i, p)
                        for kt in (2 * p, 2 * p + 1):
                            for t in range(NT):
                                q = slice(t * P, (t + 1) * P)
                                ins = mm3(pe, ps[:, ACC + 2 * t + i, :], actT_hi[:, kt, q], actT_lo[:, kt, q],
                                          hi_a[:, kt, :], lo_a[:, kt, :], kt == 0, kt == KT - 1)
                        ins.then_inc(a_used, 1)
                pe.drain().then_inc(s["ffn_done"], 2)
                turn_norm(L, 2, z, lambda t: pe.wait_ge(s["z_ready"], L * 6 + 2 + t + 1))
                pe.wait_ge(s["acc_read"], L * 6 + 4)
                rows2(L, 0, B_PROJ, pT_hi, pT_lo, True, True, "proj_done")
                wait_act(L, 16)
                for i in range(2):
                    group(L, 0, A_GATE + i, (GU, TR)[i], 512)
                    pe.drain().then_inc(s["gate_done"], 1)
                pe.wait_ge(s["ple_done"], L * 4 + 4)
                ffn(L, A_FFN2, B_FFN2, 1)


INS = ["x", "p", "rel_bias", "ffn1_w_gate", "ffn1_w_up", "ffn1_w_down", "ln1_g", "ln1_b", "w_in", "w_o",
       "da_lam_q1", "da_lam_k1", "da_lam_q2", "da_lam_k2", "da_subln_g", "ssm_lam_re", "ssm_lam_im", "ssm_log_dt",
       "ssm_b_re", "ssm_b_im", "ssm_c_re", "ssm_c_im", "ssm_d", "ssm_w_glu", "ln2_g", "ln2_b", "ffn2_w_gate",
       "ffn2_w_up", "ffn2_w_down", "ple_w_proj", "ple_w_gate", "ln3_g", "ln3_b"]


def kernel(**inputs):
    import concourse.bacc as bacc
    from concourse.bass_utils import run_bass_kernel_spmd

    nc = bacc.Bacc("TRN2", target_bir_lowering=False, num_devices=1)
    arrays, args = {}, {}
    for name in INS + ["selector"]:
        v = np.ascontiguousarray(inputs[name]) if name != "selector" else bucket_selector()
        arrays[f"in_{name}"] = v
        args[name] = nc.dram_tensor(f"in_{name}", v.shape, mybir.dt.from_np(v.dtype), kind="ExternalInput").ap()
    args["out"] = nc.dram_tensor("out_x", (1, SEQ, D_MODEL), F32, kind="ExternalOutput").ap()
    table = nc.dram_tensor("bias_table", (N_ATT, 3 * P), F32).ap()
    args["table"] = table
    args["table_rows"] = bass.AP(table.tensor, 0, [[1, P], [3 * P, N_ATT], [1, SEQ]])
    build(nc, args)
    r = run_bass_kernel_spmd(nc, [arrays], core_ids=[0])
    return r.results[0]["out_x"]
```

```python
import math
from contextlib import ExitStack

import numpy as np

import concourse.bass as bass
from concourse import mybir
from concourse.alu_op_type import AluOpType as ALU

F32 = mybir.dt.float32
F32R = mybir.dt.float32r
ACT = mybir.ActivationFunctionType
AX = mybir.AxisListType

P = 128
D_MODEL, SEQ, DEPTH = 1024, 256, 2
PLE_DIM, D_FF = 256, 2816
KT = D_MODEL // P
NT = SEQ // P
DA_HEADS, DA_QK, DA_V = 4, 64, 128
SSM_GROUP, SSM_WIDTH, SSM_GROUPS, SSM_STATE = 16, 256, 16, 64
SA_HEADS, SA_DIM = 4, 64
IDX_HEADS, IDX_DIM = 8, 32
TOPK = SEQ // 4
REL_BUCKETS, REL_MAX_DIST = 32, 128
N_ATT = DA_HEADS + SA_HEADS
ALPHA = (2 * DEPTH) ** 0.25
LN_EPS = 1e-5
IN_SIZES = (512, 512, 512, SSM_WIDTH, 256, 64, 64, 256, 32, 8)
IN_COLS = sum(IN_SIZES)
C_Q, C_K, C_V, C_U, C_SQ, C_SK, C_SV, C_IQ, C_IK, C_IW = (sum(IN_SIZES[:i]) for i in range(10))

CHUNK = 256
CHUNKS = D_FF // CHUNK
WIN_GROUPS = 6
WIN_COLS = IN_COLS // WIN_GROUPS
assert CHUNKS * CHUNK == D_FF and WIN_COLS * WIN_GROUPS == IN_COLS and WIN_COLS % 2 == 0

A_FFN1, A_WIN = 0, CHUNKS
A_WO = A_WIN + WIN_GROUPS
A_GATE = A_WO + 2
A_FFN2 = A_GATE + 2
A_GROUPS = A_FFN2 + CHUNKS
B_FFN1, B_PROJ = 0, CHUNKS
B_FFN2 = B_PROJ + 1
B_GROUPS = B_FFN2 + CHUNKS
A_UNITS, B_UNITS = 4, 2
A_ALL, B_ALL = A_GROUPS * A_UNITS, B_GROUPS * B_UNITS

NEG = -1e30
TAKEN = -3e38
STATE_TILES = SSM_GROUPS // 2
UNITS = DA_HEADS * NT

R_DT, R_G1, R_B1, R_G2, R_B2, R_RE, R_IM, R_D, R_SUB, ROWS = 0, 8, 16, 24, 32, 40, 48, 56, 58, 59
Q_G1, Q_B1, Q_G2, Q_B2, Q_MAG, Q_COS, Q_SIN, Q_FRE, Q_FIM, Q_MISC, NQ = range(11)
M_D, M_SUB, M_NLAM = 0, 2, 3

TWO_PI = 2 * math.pi
PI_A = 6.28125
PI_B = float(np.float32(round((TWO_PI - PI_A) * 2 ** 21) / 2 ** 21))
PI_C = float(np.float32(TWO_PI - PI_A - PI_B))
ROUND = 1.5 * 2 ** 23


def lam_init(layer):
    return 0.8 - 0.6 * math.exp(-0.3 * layer)


def bucket_selector():
    n = np.maximum(255 - np.arange(3 * P), 0)
    exact = REL_BUCKETS // 2
    nf = np.maximum(n, 1).astype(np.float32)
    large = exact + (np.log(nf / np.float32(exact)) / np.float32(math.log(REL_MAX_DIST / exact))
                     * np.float32(REL_BUCKETS - exact)).astype(np.int32)
    b = np.where(n < exact, n, np.minimum(large, REL_BUCKETS - 1))
    return (b[None, :] == np.arange(REL_BUCKETS)[:, None]).astype(np.float32)


def build(nc, a):
    ctx = ExitStack()
    with ctx:
        def sb(name, shape, dt=F32):
            return ctx.enter_context(nc.sbuf_tensor(name, shape, dt))

        def sem(name):
            return ctx.enter_context(nc.semaphore(name))

        raw_a = sb("raw_a", [P, 8, 512])
        raw_b = sb("raw_b", [P, 2, 1024])
        hi_a, lo_a = sb("hi_a", [P, 8, 512], F32R), sb("lo_a", [P, 8, 512], F32R)
        hi_b, lo_b = sb("hi_b", [P, 2, 1024], F32R), sb("lo_b", [P, 2, 1024], F32R)
        actT_hi, actT_lo = sb("actT_hi", [P, KT, SEQ], F32R), sb("actT_lo", [P, KT, SEQ], F32R)
        hT_hi, hT_lo = sb("hT_hi", [P, 2, SEQ], F32R), sb("hT_lo", [P, 2, SEQ], F32R)
        pT_hi, pT_lo = sb("pT_hi", [P, 2, SEQ], F32R), sb("pT_lo", [P, 2, SEQ], F32R)
        x = sb("x", [P, NT, D_MODEL])
        z = sb("z", [P, NT, D_MODEL])
        gb = sb("gb", [P, 2, D_MODEL])
        hp = sb("hp", [P, NT, IN_COLS])
        h = sb("h", [P, NT, CHUNK])
        bias = sb("bias", [P, N_ATT, SEQ])
        causal = sb("causal", [P, SEQ])
        ident = sb("ident", [P, P])
        tw_re, tw_im = sb("tw_re", [P, STATE_TILES, SEQ]), sb("tw_im", [P, STATE_TILES, SEQ])
        qT, kT = sb("qT", [P, DA_HEADS, SEQ]), sb("kT", [P, DA_HEADS, SEQ])
        saqT, iqT = sb("saqT", [P, 2, SEQ]), sb("iqT", [P, 2, SEQ])
        ksT = sb("ksT", [P, 2, SEQ])
        uT = sb("uT", [P, 2, SEQ])
        inT = sb("inT", [P, 2, 2, P])
        outT = sb("outT", [P, STATE_TILES, 3, 32])
        b_exp = sb("b_exp", [P, 2, STATE_TILES, 32])
        parity = sb("parity", [P, 2])
        glu = sb("glu", [P, 2, SSM_WIDTH])
        dt_row = sb("dt_row", [P, 2])
        prmT = sb("prmT", [P, ROWS])
        lp = sb("lp", [P, NQ, 8])
        small = sb("small", [P, 8, 8])
        lams = sb("lams", [P, 2])
        lam_consts = sb("lam_consts", [P, 2, DEPTH])
        stats = sb("stats", [P, NT, 2, 6])
        mv = sb("mv", [P, NT, 2])
        var, rstd = sb("var", [P, NT]), sb("rstd", [P, NT])
        mhalf = sb("mhalf", [P, 8])
        isc, work = sb("isc", [P, SEQ]), sb("work", [P, SEQ])
        top8 = sb("top8", [P, 8])
        sel = sb("sel", [P, NT, SEQ])
        wis = sb("wis", [P, NT, IDX_HEADS])
        da_e = sb("da_e", [P, 2, 2, SEQ])
        da_nm = sb("da_nm", [P, 2, 2])
        da_sum, da_r = sb("da_sum", [P, UNITS, 2]), sb("da_r", [P, UNITS, 2])
        aT = sb("aT", [P, 2, SEQ])
        junk = sb("junk", [P, P])
        ss, rms = sb("ss", [P, NT, DA_HEADS]), sb("rms", [P, NT, DA_HEADS])
        sa_nm, sa_sum = sb("sa_nm", [P, NT, SA_HEADS]), sb("sa_sum", [P, NT, SA_HEADS])
        hp_flat = hp[:, :, :].rearrange("p a c -> p (a c)")
        lnT = hp_flat[:, 0:2048].rearrange("p (k t) -> p k t", k=KT)
        p_nat = hp_flat[:, 2048:2560].rearrange("p (t d) -> p t d", t=NT)
        c_nat = hp_flat[:, 2560:2816].rearrange("p (r t d) -> p r t d", r=2, t=2)
        b_nat = hp_flat[:, 2816:3072].rearrange("p (r j c) -> p r j c", r=2, j=STATE_TILES)
        b_tmp = hp_flat[:, 3072:3328].rearrange("p (r j c) -> p r j c", r=2, j=STATE_TILES)
        c_exp = hp_flat[:, 3328:3840].rearrange("p (r t q d) -> p r t q d", r=2, t=2, q=2)
        lamv = hp_flat[:, 3840:4096].rearrange("p (i d) -> p i d", i=4)
        rows = hp_flat[:, 4096:4224]
        rot = z[:, 0, :].rearrange("p (a c t) -> p a c t", a=2, c=2)
        ys = z[:, 1, :].rearrange("p (a c t) -> p a c t", a=2, c=2)
        prod = gb[:, :, :].rearrange("p a (b c t) -> p a b c t", b=2, c=2)
        derot = h
        kdup = h
        relu_w = raw_b[:, :, :].rearrange("p a (h s) -> p (a h) s", s=SEQ)
        sa_e = raw_b[:, 0, :].rearrange("p (h s) -> p h s", s=SEQ)
        sa_aT = raw_b[:, 1, :]
        ys2 = raw_b[:, 0, :].rearrange("p (v a t) -> p v a t", v=2, a=2)
        ysg = raw_b[:, 1, 0:512].rearrange("p (a t) -> p a t", a=2)

        ps = ctx.enter_context(nc.psum_tensor("ps", [P, 8, 512], F32))
        GU, ACC, TR, MISC = 0, 2, 6, 7
        LN_BANKS = (0, 1, 6, 7)

        a_loaded = [sem(f"a_loaded{i}") for i in range(2)]
        b_loaded = [sem(f"b_loaded{i}") for i in range(2)]
        a_hi, a_lo, a_used = sem("a_hi"), sem("a_lo"), sem("a_used")
        b_hi, b_lo, b_used = sem("b_hi"), sem("b_lo"), sem("b_used")
        names = """x_loaded rows_loaded dtrow_loaded lamv_loaded sel_loaded ssm_loaded glu_loaded p_loaded
            gb_loaded gb_used ident_set causal_set dt_expanded rows_turned prm_out table_turned table_out table_stored
            bias_loaded bias_ready dt_exp mag_ready sin_in sin_out lam_in lam_exp par_ready lp_ready
            x_ready x_half turned lnT_scaled lnT_act actT_hi_ready actT_ready p_turned pT_hi_ready pT_ready
            gate_act h_ready h_turned hT_hi_ready hT_ready ffn_done acc_read var_ready rs_ready z_ready
            twiddles b_ready c_ready bc_turned in_out c_out x_updated
            win_done hp_ready kdup_ready ix_turned ix_out qk_turned qk_out ixs_done ixs_read sel_ready
            bu_done bu_read y_ready prod_ready c_done
            das_done das_read da_max da_exp da_a da_turned da_aT da_o da_o_out ss_scaled rms_ready mix_da
            sas_done sas_read sa_max sa_exp sa_turned sa_aT_ready sa_o mix_sa
            y_full gelu_done glu_done glu_act ssm_out mix_turned mixT_hi wo_done
            proj_done gate_done gate_sig ple_done stored""".split()
        s = {n: sem(n) for n in names}

        block = ctx.enter_context(nc.Block())

        def mm3(pe, out, act_hi, act_lo, w_hi, w_lo, first, last):
            pe.matmul(out, act_hi, w_hi, start=first, stop=False)
            pe.matmul(out, act_hi, w_lo, start=False, stop=False)
            return pe.matmul(out, act_lo, w_hi, start=False, stop=last)

        def bc(ap, n):
            return ap.unsqueeze(ap.ndim).broadcast_to([*ap.shape, n])

        def rep(ap, n):
            return ap.unsqueeze(1).broadcast_to([ap.shape[0], n, *ap.shape[1:]])

        @block.sync
        def _(sp):
            def load(dst, src, done):
                return sp.dma_start(dst, src).then_inc(done, 16)

            def load_a(L, n, k, srcs):
                for half in range(2):
                    sp.wait_ge(a_lo, L * A_ALL + n * A_UNITS + (k * A_UNITS + 2 * half + 2))
                    for dst, src in srcs(4 * half):
                        load(dst, src, a_loaded[half])

            def load_b(L, m, k, src):
                for half in range(2):
                    sp.wait_ge(b_lo, L * B_ALL + m * B_UNITS + (k * B_UNITS + half + 1))
                    load(raw_b[:, half, :], src(half), b_loaded[half])

            def ffn(L, gate, up, down, a0, b0, small_loads=None):
                def gate_up(n, k, col):
                    def srcs(k0):
                        for i, w in enumerate((gate, up)):
                            yield (raw_a[:, k0:k0 + 4, i * CHUNK:(i + 1) * CHUNK],
                                   w[L, k0 * P:(k0 + 4) * P, bass.ds(col, CHUNK)]
                                   .rearrange("(k p) f -> p k f", p=P))
                    load_a(L, n, k, srcs)

                def down_rows(n, k, col):
                    load_b(L, n, k, lambda half: down[L, bass.ds(col + half * P, P), :])

                gate_up(0, a0, 0)
                if small_loads:
                    small_loads()
                with sp.Fori(0, CHUNKS - 1) as c:
                    col = sp.snap(c * CHUNK)
                    gate_up(c, a0 + 1, col + CHUNK)
                    down_rows(c, b0, col)
                down_rows(0, b0 + CHUNKS - 1, D_FF - CHUNK)

            def wide(w, L, c0, cols):
                def srcs(k0):
                    for k in (k0 + 2, k0):
                        yield (raw_a[:, k:k + 2, 0:cols],
                               w[L, k * P:(k + 2) * P, c0:c0 + cols].rearrange("(k p) f -> p k f", p=P))
                return srcs

            def load_norm(L, g, b):
                load(gb[:, 0, :], g[bass.ds(L, 1), :].broadcast_to([P, D_MODEL]), s["gb_loaded"])
                load(gb[:, 1, :], b[bass.ds(L, 1), :].broadcast_to([P, D_MODEL]), s["gb_loaded"])

            load(x[:, :, :], a["x"][0].rearrange("(t p) d -> p t d", p=P), s["x_loaded"])

            with sp.Fori(0, DEPTH) as L:
                def small_loads():
                    load(p_nat[:, :, :], a["p"][L, 0].rearrange("(t p) d -> p t d", p=P), s["p_loaded"])
                    load(dt_row[R_DT:R_DT + 8, :], a["ssm_log_dt"][L].rearrange("(j g) -> j g", g=2), s["dtrow_loaded"])
                    for r, name in ((R_G1, "ln1_g"), (R_B1, "ln1_b"), (R_G2, "ln2_g"), (R_B2, "ln2_b")):
                        load(rows[r:r + 8, :], a[name][L].rearrange("(r c) -> r c", c=P), s["rows_loaded"])
                    for r, name in ((R_RE, "ssm_lam_re"), (R_IM, "ssm_lam_im")):
                        load(rows[r:r + 8, :], a[name][L].rearrange("(j g) p -> j (g p)", g=2), s["rows_loaded"])
                    load(rows[R_D:R_D + 2, :], a["ssm_d"][L].rearrange("(r c) -> r c", c=P), s["rows_loaded"])
                    load(rows[R_SUB:R_SUB + 1, :], a["da_subln_g"][bass.ds(L, 1), :], s["rows_loaded"])
                    for i, name in enumerate(("da_lam_q1", "da_lam_k1", "da_lam_q2", "da_lam_k2")):
                        load(lamv[:, i, :], a[name][bass.ds(L, 1), :].broadcast_to([P, DA_QK]), s["lamv_loaded"])
                    for i, name in enumerate(("ssm_b_re", "ssm_b_im")):
                        load(b_nat[:, i, :, :], a[name][L].rearrange("(j g) p c -> (g p) j c", g=2), s["ssm_loaded"])
                    for i, name in enumerate(("ssm_c_re", "ssm_c_im")):
                        load(c_nat[:, i, :, :], a[name][L].rearrange("(t g) c p -> (g c) t p", t=2), s["ssm_loaded"])
                    load(glu[:, :, :], a["ssm_w_glu"][L].rearrange("(t p) c -> p t c", p=P), s["glu_loaded"])
                ffn(L, a["ffn1_w_gate"], a["ffn1_w_up"], a["ffn1_w_down"], A_FFN1, B_FFN1, small_loads)
                sp.wait_ge(s["gb_used"], L * 3)
                load_norm(L, a["ln1_g"], a["ln1_b"])
                for i in range(WIN_GROUPS):
                    load_a(L, 0, A_WIN + i, wide(a["w_in"], L, (WIN_GROUPS - 1 - i) * WIN_COLS, WIN_COLS))
                for i in range(2):
                    load_a(L, 0, A_WO + i, wide(a["w_o"], L, i * 512, 512))
                sp.wait_ge(s["actT_ready"], L * 16 + 12)
                load_norm(L, a["ln2_g"], a["ln2_b"])
                load_b(L, 0, B_PROJ, lambda half: a["ple_w_proj"][L, half * P:(half + 1) * P, :])
                for i in range(2):
                    load_a(L, 0, A_GATE + i, wide(a["ple_w_gate"], L, i * 512, 512))
                sp.wait_ge(s["gb_used"], L * 3 + 2)
                load_norm(L, a["ln3_g"], a["ln3_b"])
                ffn(L, a["ffn2_w_gate"], a["ffn2_w_up"], a["ffn2_w_down"], A_FFN2, B_FFN2)

            sp.wait_ge(s["x_ready"], DEPTH)
            sp.wait_ge(s["x_half"], DEPTH)
            load(a["out"][0].rearrange("(t p) d -> p t d", p=P), x[:, :, :], s["stored"])
            sp.wait_ge(s["stored"], 16)

        @block.gpsimd
        def _(pool):
            TT, MUL, ADD, SUB = pool.tensor_tensor, ALU.mult, ALU.add, ALU.subtract
            def load_setup(dst, src, done):
                pool.dma_start(dst, src).then_inc(done, 16)

            pool.memset(ident[:, :], 0.0)
            pool.drain()
            pool.affine_select(out=ident[:, :], in_=ident[:, :], compare_op=ALU.not_equal, fill=1.0, base=0,
                               pattern=[[-1, P]], channel_multiplier=1)
            pool.drain().then_inc(s["ident_set"], 1)
            load_setup(tw_re[0:REL_BUCKETS, 0, 0:N_ATT], a["rel_bias"], s["sel_loaded"])
            load_setup(tw_im[0:REL_BUCKETS, 0:2, :].rearrange("p a t -> p (a t)")[:, 0:3 * P], a["selector"], s["sel_loaded"])
            pool.memset(causal[:, :], 0.0)
            pool.memset(mhalf[:, :], -0.5)
            for layer in range(DEPTH):
                pool.memset(lam_consts[:, 0, layer:layer + 1], lam_init(layer))
                pool.memset(lam_consts[:, 1, layer:layer + 1], 1.0 - lam_init(layer))
            pool.memset(b_exp[:, :, :, :], 0.0)
            pool.drain()
            pool.affine_select(out=causal[:, :], in_=causal[:, :], compare_op=ALU.is_ge, fill=NEG, base=P,
                               pattern=[[-1, SEQ]], channel_multiplier=1)
            pool.drain().then_inc(s["causal_set"], 1)
            pool.wait_ge(s["table_out"], 1)
            pool.dma_start(a["table"], z[0:N_ATT, 0, 0:3 * P].unsqueeze(1).broadcast_to([N_ATT, P, 3 * P]))\
                .then_inc(s["table_stored"], 16)
            pool.wait_ge(s["table_stored"], 16)
            pool.dma_start(bias[:, :, :], a["table_rows"]).then_inc(s["bias_loaded"], 16)
            pool.wait_ge(s["bias_loaded"], 16)
            TT(bias[:, :, :], bias[:, :, :], rep(causal[:, :], N_ATT), ADD)
            pool.drain().then_inc(s["bias_ready"], 1)

            def power(L, k):
                for t in range(NT):
                    pool.wait_ge(s["var_ready"], L * 6 + 2 * k + t + 1)
                    TT(rstd[:, t:t + 1], var[:, t:t + 1], mhalf[:, 0:1], ALU.pow).then_inc(s["rs_ready"], 1)

            def update_x(L, k):
                pool.wait_ge(s["gb_loaded"], L * 96 + 32 * (k + 1))
                for t in range(NT):
                    pool.wait_ge(s["z_ready"], L * 6 + 2 * k + t + 1)
                    TT(x[:, t, :], z[:, t, :], gb[:, 0, :], MUL)
                pool.drain()
                for t in range(NT):
                    ins = TT(x[:, t, :], x[:, t, :], gb[:, 1, :], ADD)
                pool.drain().then_inc(s["x_updated"], 1)
                pool.sem_inc(s["gb_used"], 1)

            with pool.Fori(0, DEPTH) as L:
                pool.wait_ge(s["lp_ready"], L + 1)
                pool.wait_ge(s["ssm_loaded"], L * 64 + 64)
                fre, fim = bc(lp[:, Q_FRE, :], SSM_GROUP), bc(lp[:, Q_FIM, :], SSM_GROUP)
                pool.wait_ge(s["x_ready"], L)
                for part, (f0, f1, op) in enumerate(((fre, fim, SUB), (fim, fre, ADD))):
                    TT(b_tmp[:, 0, :, :], b_nat[:, 0, :, :], f0, MUL)
                    TT(b_tmp[:, 1, :, :], b_nat[:, 1, :, :], f1, MUL)
                    pool.drain()
                    for g in range(2):
                        q = slice(64 * g, 64 * g + 64)
                        TT(b_exp[q, part, :, 16 * g:16 * g + 16], b_tmp[q, 0, :, :], b_tmp[q, 1, :, :], op)
                    pool.drain()
                pool.drain().then_inc(s["b_ready"], 1)
                for part in range(2):
                    for q in range(2):
                        TT(c_exp[:, part, :, q, :], c_nat[:, part, :, :],
                           parity[:, q:q + 1].unsqueeze(2).broadcast_to([P, 2, SSM_STATE]), MUL)
                pool.drain().then_inc(s["c_ready"], 1)
                pool.memset(tw_re[:, :, 0:1], 1.0)
                pool.memset(tw_im[:, :, 0:1], 0.0)
                pool.tensor_copy(tw_re[:, :, 1:2], lp[:, Q_COS, :].unsqueeze(2))
                pool.tensor_copy(tw_im[:, :, 1:2], lp[:, Q_SIN, :].unsqueeze(2))
                pool.drain()

                k = 1
                while k < SEQ:
                    for c0 in range(0, min(k, SEQ - 1 - k), 64):
                        m = min(64, k - c0, SEQ - 1 - k - c0)
                        src, dst = slice(1 + c0, 1 + c0 + m), slice(k + 1 + c0, k + 1 + c0 + m)
                        tmp = [z[:, i // 2, (i % 2) * 512:(i % 2) * 512 + STATE_TILES * m]
                               .rearrange("p (j t) -> p j t", j=STATE_TILES) for i in range(4)]
                        wr = tw_re[:, :, k:k + 1].broadcast_to([P, STATE_TILES, m])
                        wi = tw_im[:, :, k:k + 1].broadcast_to([P, STATE_TILES, m])
                        TT(tmp[0], tw_re[:, :, src], wr, MUL)
                        TT(tmp[1], tw_im[:, :, src], wi, MUL)
                        TT(tmp[2], tw_re[:, :, src], wi, MUL)
                        TT(tmp[3], tw_im[:, :, src], wr, MUL)
                        pool.drain()
                        TT(tw_re[:, :, dst], tmp[0], tmp[1], SUB)
                        TT(tw_im[:, :, dst], tmp[2], tmp[3], ADD)
                        pool.drain()
                    k *= 2
                pool.drain().then_inc(s["twiddles"], 1)

                power(L, 0)
                update_x(L, 0)
                for j in range(STATE_TILES):
                    pool.wait_ge(s["y_ready"], L * 8 + j + 1)
                    if j >= 2:
                        pool.wait_ge(s["c_done"], L * 8 + j - 1)
                    for i, tw in enumerate((tw_re, tw_im)):
                        TT(prod[:, j % 2, i, :, :], ys[:, j % 2, :, :], rep(tw[:, j, :], 2), MUL)
                    pool.drain().then_inc(s["prod_ready"], 1)
                pool.wait_ge(s["ss_scaled"], L + 1)
                TT(rms[:, :, :].rearrange("p t h -> p (t h)"), ss[:, :, :].rearrange("p t h -> p (t h)"),
                   mhalf[:, :], ALU.pow).then_inc(s["rms_ready"], 1)
                power(L, 1)
                update_x(L, 1)
                power(L, 2)
                pool.wait_ge(s["gb_loaded"], L * 96 + 96)
                pool.wait_ge(s["z_ready"], L * 6 + 6)
                TT(x[:, 1, :], z[:, 1, :], gb[:, 0, :], MUL)
                pool.drain()
                TT(x[:, 1, :], x[:, 1, :], gb[:, 1, :], ADD)
                pool.drain().then_inc(s["x_half"], 1)
                pool.wait_ge(s["x_ready"], L + 1)
                pool.sem_inc(s["gb_used"], 1)

        @block.scalar
        def _(act):
            def hi_unit(L, n, k, p):
                act.wait_ge(a_loaded[p // 2], L * (A_GROUPS * 32) + n * 32 + (k + 1) * 32)
                act.wait_ge(a_used, L * A_ALL + n * A_UNITS + (k * A_UNITS + p + 1))
                act.activation(hi_a[:, 2 * p:2 * p + 2, :], raw_a[:, 2 * p:2 * p + 2, :], ACT.Copy).then_inc(a_hi, 1)

            def hi_b_unit(L, m, k, u):
                act.wait_ge(b_loaded[u], L * (B_GROUPS * 16) + m * 16 + (k + 1) * 16)
                act.wait_ge(b_used, L * B_ALL + m * B_UNITS + (k * B_UNITS + u + 1))
                act.activation(hi_b[:, u, :], raw_b[:, u, :], ACT.Copy).then_inc(b_hi, 1)

            def evict(bank, dst, turned, count, done, scale=None):
                act.wait_ge(s[turned], count)
                act.activation(dst, bank, ACT.Copy).then_inc(s[done], 1)

            def parameters(L):
                act.wait_ge(s["lam_in"], L + 1)
                act.activation(lams[:, :], lams[:, :], ACT.Exp).then_inc(s["lam_exp"], 1)
                act.wait_ge(s["prm_out"], L + 1)
                act.activation(small[:, 0, :], prmT[:, R_DT:R_DT + 8], ACT.Exp).then_inc(s["dt_exp"], 1)
                act.wait_ge(s["sin_in"], L + 1)
                act.activation(lp[:, Q_MAG, :], lp[:, Q_MAG, :], ACT.Exp)
                act.activation(lp[:, Q_SIN, :], small[:, 1, :], ACT.Sin)
                act.activation(lp[:, Q_COS, :], small[:, 1, :], ACT.Sin, scale=0.5).then_inc(s["sin_out"], 1)

            def ffn(L, a0, b0, f, following):
                base = f * CHUNKS

                def hidden(c, k):
                    act.wait_ge(a_used, L * A_ALL + c * A_UNITS + (A_UNITS + (a0 + k) * A_UNITS + A_UNITS))
                    act.wait_ge(s["h_turned"], L * 2 * CHUNKS + c + (base + k))
                    for t in range(NT):
                        act.activation(h[:, t, :], ps[:, GU + t, 0:CHUNK], ACT.Sigmoid).then_inc(s["gate_act"], 1)

                def hidden_hi(c, k, dst=hT_hi[:, :, :]):
                    act.wait_ge(s["h_turned"], L * 2 * CHUNKS + c + (base + k + 1))
                    act.activation(dst.rearrange("p a t -> p (a t)"), ps[:, TR, :],
                                   ACT.Copy).then_inc(s["hT_hi_ready"], 1)

                for p in range(3):
                    hi_unit(L, 0, a0 + 1, p)
                hidden(0, 0)
                if not f:
                    evict(ps[:, ACC, :], pT_hi[:, :, :].rearrange("p a t -> p (a t)"), "p_turned", L + 1, "pT_hi_ready")
                hi_unit(L, 0, a0 + 1, 3)
                for u in range(2):
                    hi_b_unit(L, 0, b0, u)
                if not f:
                    parameters(L)
                with act.Fori(1, CHUNKS - 1) as c:
                    hi_unit(L, c, a0 + 1, 0)
                    hidden_hi(c, -1)
                    hi_unit(L, c, a0 + 1, 1)
                    hi_unit(L, c, a0 + 1, 2)
                    hidden(c, 0)
                    hi_unit(L, c, a0 + 1, 3)
                    for u in range(2):
                        hi_b_unit(L, c, b0, u)
                c = CHUNKS - 1
                if following:
                    hi_unit(L, 0, a0 + c + 1, 0)
                hidden_hi(0, c - 1)
                if following:
                    hi_unit(L, 0, a0 + c + 1, 1)
                    hi_unit(L, 0, a0 + c + 1, 2)
                hidden(0, c)
                if following:
                    hi_unit(L, 0, a0 + c + 1, 3)
                hidden_hi(0, c, actT_hi[:, 0:2, :])
                for u in range(2):
                    hi_b_unit(L, 0, b0 + c, u)

            def act_hi(L, k, src, sem_in, count, scale=1.0):
                b = k % 4
                act.wait_ge(s[sem_in], count)
                act.activation(actT_hi[:, 2 * b:2 * b + 2, :].rearrange("p k t -> p (k t)"), src,
                               ACT.Copy).then_inc(s["actT_hi_ready"], 1)

            def norm_turned(L, k, g, b):
                def scaled(i):
                    act.wait_ge(s["turned"], L * 12 + 4 * (k + 1) + i + 1)
                    for kk in range(2):
                        c = 2 * i + kk
                        ins = act.activation(lnT[:, c, :], ps[:, LN_BANKS[i], kk * SEQ:(kk + 1) * SEQ], ACT.Identity,
                                             bias=lp[:, b, c:c + 1], scale=lp[:, g, c:c + 1])
                    ins.then_inc(s["lnT_act"], 1)

                for i in range(4):
                    if i < 2:
                        act.wait_ge(s["lnT_scaled"], L * 4 + 2 * k + i + 1)
                    else:
                        act.wait_ge(s["lnT_act"], L * 4 + 2 * k + i - 1)
                    if i + 2 < 4:
                        scaled(i + 2)
                    act.activation(actT_hi[:, 2 * i:2 * i + 2, :], lnT[:, 2 * i:2 * i + 2, :],
                                   ACT.Copy).then_inc(s["actT_hi_ready"], 1)

            with act.Fori(0, DEPTH) as L:
                for p in range(2):
                    hi_unit(L, 0, A_FFN1, p)
                for i in range(4):
                    act.wait_ge(s["turned"], L * 12 + i + 1)
                    act.activation(actT_hi[:, 2 * i:2 * i + 2, :].rearrange("p k t -> p (k t)"),
                                   ps[:, LN_BANKS[i], :], ACT.Copy).then_inc(s["actT_hi_ready"], 1)
                for p in range(2, 4):
                    hi_unit(L, 0, A_FFN1, p)
                ffn(L, A_FFN1, B_FFN1, 0, True)
                act.wait_ge(s["bc_turned"], L * 2 + 1)
                act.activation(inT[:, :, :, :].rearrange("p a r c -> p (a r c)"), ps[:, MISC, :],
                               ACT.Copy).then_inc(s["in_out"], 1)
                act.wait_ge(s["bc_turned"], L * 2 + 2)
                cT = ps[:, TR, :].rearrange("p (r j c) -> p r j c", r=2, c=32)
                for i, (r, sign) in enumerate(((0, 1.0), (0, -1.0), (1, -1.0))):
                    ins = act.activation(outT[:, :, i, :], cT[:, r, :, :], ACT.Copy, scale=sign)
                ins.then_inc(s["c_out"], 1)
                norm_turned(L, 0, Q_G1, Q_B1)
                for i in range(WIN_GROUPS):
                    for p in range(3):
                        hi_unit(L, 0, A_WIN + i + 1, p)
                    c0 = (WIN_GROUPS - 1 - i) * WIN_COLS
                    if i == 0:
                        act.wait_ge(s["actT_ready"], L * 16 + 8)
                    act.wait_ge(s["win_done"], L * WIN_GROUPS + i + 1)
                    for t in range(NT):
                        ins = act.activation(hp[:, t, c0:c0 + WIN_COLS], ps[:, 2 * (i % 2) + t, 0:WIN_COLS], ACT.Copy)
                    ins.then_inc(s["hp_ready"], 1)
                    hi_unit(L, 0, A_WIN + i + 1, 3)
                    if i == 3:
                        for n, (bank, dst) in enumerate(((6, iqT), (7, ksT), (4, saqT), (5, uT))):
                            act.wait_ge(s["ix_turned"], L * 4 + n + 1)
                            act.activation(dst[:, :, :].rearrange("p a t -> p (a t)"), ps[:, bank, :],
                                           ACT.Copy).then_inc(s["ix_out"], 1)
                for n in range(4):
                    dst = (qT, kT)[n // 2][:, 2 * (n % 2):2 * (n % 2) + 2, :]
                    act.wait_ge(s["qk_turned"], L * 4 + n + 1)
                    act.activation(dst.rearrange("p a t -> p (a t)"), ps[:, n, :], ACT.Copy).then_inc(s["qk_out"], 1)
                for i in range(UNITS + 1):
                    if i < UNITS:
                        N = P * (i % 2 + 1)
                        act.wait_ge(s["da_max"], L * UNITS + i + 1)
                        for c in range(2):
                            ins = act.activation(da_e[:, i % 2, c, 0:N], da_e[:, i % 2, c, 0:N], ACT.Exp,
                                                 bias=da_nm[:, i % 2, c:c + 1], accum_out=da_sum[:, i, c:c + 1])
                        ins.then_inc(s["da_exp"], 1)
                    if i >= 1:
                        u = i - 1
                        hd, qb = u // 2, u % 2
                        act.wait_ge(s["da_turned"], L * UNITS + u + 1)
                        act.activation(aT[:, u % 2, 0:P * (qb + 1)], ps[:, 6, 0:P * (qb + 1)],
                                       ACT.Copy).then_inc(s["da_aT"], 1)
                        act.wait_ge(s["da_o"], L * UNITS + u + 1)
                        act.activation(hp[:, qb, hd * DA_V:(hd + 1) * DA_V], ps[:, 7, 0:P], ACT.Copy)
                        act.activation(junk[:, :], ps[:, 7, 0:P], ACT.Square,
                                       accum_out=ss[:, qb, hd:hd + 1]).then_inc(s["da_o_out"], 1)
                for qb in range(NT):
                    N = P * (qb + 1)
                    act.wait_ge(s["sa_max"], L * 2 + qb + 1)
                    for hd in range(SA_HEADS):
                        ins = act.activation(sa_e[:, hd, 0:N], sa_e[:, hd, 0:N], ACT.Exp,
                                             bias=sa_nm[:, qb, hd:hd + 1], accum_out=sa_sum[:, qb, hd:hd + 1])
                    ins.then_inc(s["sa_exp"], 1)
                    for half in range(2):
                        act.wait_ge(s["sa_turned"], L * 4 + 2 * qb + half + 1)
                        w = 2 * N
                        act.activation(sa_aT[:, half * 512:half * 512 + w], ps[:, half, 0:w],
                                       ACT.Copy).then_inc(s["sa_aT_ready"], 1)
                act.wait_ge(s["y_full"], L + 1)
                act.activation(ys2[:, 1, :, :], ys2[:, 0, :, :], ACT.Gelu_apprx_tanh).then_inc(s["gelu_done"], 1)
                act.wait_ge(s["glu_done"], L + 1)
                act.activation(ysg.rearrange("p a t -> p (a t)"), ps[:, 2, :], ACT.Sigmoid).then_inc(s["glu_act"], 1)
                act.wait_ge(s["ssm_out"], L + 1)
                act.activation(actT_hi[:, 4:6, :], ysg, ACT.Copy).then_inc(s["mixT_hi"], 1)
                for n, b in enumerate((0, 1, 3)):
                    act.wait_ge(s["mix_turned"], L * 3 + n + 1)
                    if b < 2:
                        ins = act.activation(actT_hi[:, 2 * b:2 * b + 2, :].rearrange("p k t -> p (k t)"),
                                             ps[:, LN_BANKS[b], :], ACT.Copy, scale=lp[:, Q_MISC, M_SUB:M_SUB + 1])
                    else:
                        ins = act.activation(actT_hi[:, 2 * b:2 * b + 2, :].rearrange("p k t -> p (k t)"),
                                             ps[:, LN_BANKS[b], :], ACT.Copy)
                    ins.then_inc(s["mixT_hi"], 1)
                for p in range(4):
                    hi_unit(L, 0, A_WO + 1, p)
                for u in range(2):
                    hi_b_unit(L, 0, B_PROJ, u)
                for p in range(4):
                    hi_unit(L, 0, A_GATE, p)
                norm_turned(L, 1, Q_G2, Q_B2)
                for i in range(2):
                    for p in range(4):
                        hi_unit(L, 0, A_GATE + i + 1, p)
                    act.wait_ge(s["gate_done"], L * 2 + i + 1)
                    act.wait_ge(s["x_updated"], L * 2 + 2)
                    for t in range(NT):
                        act.activation(z[:, t, i * 512:(i + 1) * 512], ps[:, (GU, TR)[i] + t, :],
                                       ACT.Sigmoid).then_inc(s["gate_sig"], 1)
                ffn(L, A_FFN2, B_FFN2, 1, False)

        @block.vector
        def _(dve):
            TT, TS, STT = dve.tensor_tensor, dve.tensor_scalar, dve.scalar_tensor_tensor
            MUL, ADD, SUB, MAX = ALU.mult, ALU.add, ALU.subtract, ALU.max

            def flat(t):
                return t.rearrange("p a t -> p (a t)")

            def lo_unit(L, n, k, p):
                dve.wait_ge(a_hi, L * A_ALL + n * A_UNITS + (k * A_UNITS + p + 1))
                q = slice(2 * p, 2 * p + 2)
                TT(lo_a[:, q, :], raw_a[:, q, :], hi_a[:, q, :].bitcast(F32), SUB).then_inc(a_lo, 1)

            def lo_b_unit(L, m, k, u):
                dve.wait_ge(b_hi, L * B_ALL + m * B_UNITS + (k * B_UNITS + u + 1))
                TT(lo_b[:, u, :], raw_b[:, u, :], hi_b[:, u, :].bitcast(F32), SUB).then_inc(b_lo, 1)

            re, im = prmT[:, R_RE:R_RE + 8], prmT[:, R_IM:R_IM + 8]
            sm = [small[:, i, :] for i in range(8)]

            def parameters_in(L):
                dve.wait_ge(s["lamv_loaded"], L * 64 + 64)
                for i in range(2):
                    TT(lamv[:, 2 * i, :], lamv[:, 2 * i, :], lamv[:, 2 * i + 1, :], MUL)
                dve.memset(lp[:, Q_MISC, :], 0.0)
                dve.drain()
                dve.tensor_reduce(lams[:, 0:1], lamv[:, 0, :], AX.X, ADD)
                dve.tensor_reduce(lams[:, 1:2], lamv[:, 2, :], AX.X, ADD).then_inc(s["lam_in"], 1)
                dve.tensor_copy(lp[:, Q_G1:Q_B2 + 1, :], prmT[:, R_G1:R_B2 + 8].rearrange("p (q k) -> p q k", k=8))
                dve.tensor_copy(lp[:, Q_MISC, M_D:M_D + 2], prmT[:, R_D:R_D + 2])

            def parameters(L):
                dve.wait_ge(s["dt_exp"], L + 1)
                TT(lp[:, Q_MAG, :], re, sm[0], MUL)
                TT(sm[1], im, sm[0], MUL)
                dve.wait_ge(s["lam_exp"], L + 1)
                TT(lams[:, 0:1], lams[:, 1:2], lams[:, 0:1], SUB)
                dve.drain()
                TT(lp[:, Q_MISC, M_NLAM:M_NLAM + 1], lams[:, 0:1],
                   lam_consts[:, 0, bass.ds(L, 1)], SUB)
                TT(lp[:, Q_MISC, M_SUB:M_SUB + 1], prmT[:, R_SUB:R_SUB + 1],
                   lam_consts[:, 1, bass.ds(L, 1)], MUL)
                TS(sm[2], sm[1], 1 / TWO_PI, ROUND, MUL, ADD)
                dve.drain()
                TS(sm[2], sm[2], ROUND, None, SUB)
                for part in (PI_A, PI_B, PI_C):
                    dve.drain()
                    STT(sm[1], sm[2], -part, sm[1], MUL, ADD)
                dve.drain()
                TS(sm[1], sm[1], 3.1415925, -3.1415925, ALU.min, MAX)
                TT(sm[3], re, re, MUL)
                TT(sm[4], im, im, MUL)
                dve.drain().then_inc(s["sin_in"], 1)
                TT(sm[3], sm[3], sm[4], ADD)
                dve.drain()
                dve.reciprocal(sm[3], sm[3])
                dve.wait_ge(s["sin_out"], L + 1)
                mag, cos, sin = lp[:, Q_MAG, :], lp[:, Q_COS, :], lp[:, Q_SIN, :]
                TT(cos, cos, cos, MUL)
                TT(sm[4], mag, sin, MUL)
                dve.drain()
                TS(cos, cos, -2.0, 1.0, MUL, ADD)
                dve.drain()
                TT(sm[5], mag, cos, MUL)
                dve.drain()
                TS(sm[5], sm[5], -1.0, None, ADD)
                dve.drain()
                TT(sm[0], sm[5], re, MUL)
                TT(sm[1], sm[4], im, MUL)
                TT(sm[6], sm[4], re, MUL)
                TT(sm[7], sm[5], im, MUL)
                dve.drain()
                TT(sm[0], sm[0], sm[1], ADD)
                TT(sm[6], sm[6], sm[7], SUB)
                dve.drain()
                TT(lp[:, Q_FRE, :], sm[0], sm[3], MUL)
                TT(lp[:, Q_FIM, :], sm[6], sm[3], MUL)
                dve.drain().then_inc(s["lp_ready"], 1)

            def ffn(L, a0, b0, f, following):
                base = f * CHUNKS

                def hidden(c, k):
                    for t in range(NT):
                        dve.wait_ge(s["gate_act"], L * 4 * CHUNKS + c * 2 + (2 * (base + k) + t + 1))
                        TT(h[:, t, :], h[:, t, :], ps[:, GU + t, 0:CHUNK], MUL)
                    dve.drain()
                    for t in range(NT):
                        TT(h[:, t, :], h[:, t, :], ps[:, GU + t, CHUNK:2 * CHUNK], MUL).then_inc(s["h_ready"], 1)

                def hidden_lo(c, k, hi=hT_hi[:, :, :], lo=hT_lo[:, :, :]):
                    dve.wait_ge(s["hT_hi_ready"], L * 2 * CHUNKS + c + (base + k + 1))
                    TT(flat(lo), ps[:, TR, :], flat(hi).bitcast(F32), SUB).then_inc(s["hT_ready"], 1)

                for p in range(3):
                    lo_unit(L, 0, a0 + 1, p)
                hidden(0, 0)
                if not f:
                    dve.wait_ge(s["rows_turned"], L + 1)
                    dve.tensor_copy(prmT[:, :], ps[:, ACC + 1, 0:ROWS]).then_inc(s["prm_out"], 1)
                    dve.wait_ge(s["pT_hi_ready"], L + 1)
                    TT(flat(pT_lo[:, :, :]), ps[:, ACC, :], flat(pT_hi[:, :, :]).bitcast(F32), SUB)\
                        .then_inc(s["pT_ready"], 1)
                    parameters_in(L)
                lo_unit(L, 0, a0 + 1, 3)
                for u in range(2):
                    lo_b_unit(L, 0, b0, u)
                if not f:
                    parameters(L)
                with dve.Fori(1, CHUNKS - 1) as c:
                    lo_unit(L, c, a0 + 1, 0)
                    hidden_lo(c, -1)
                    lo_unit(L, c, a0 + 1, 1)
                    lo_unit(L, c, a0 + 1, 2)
                    hidden(c, 0)
                    lo_unit(L, c, a0 + 1, 3)
                    for u in range(2):
                        lo_b_unit(L, c, b0, u)
                c = CHUNKS - 1
                if following:
                    lo_unit(L, 0, a0 + c + 1, 0)
                hidden_lo(0, c - 1)
                if following:
                    lo_unit(L, 0, a0 + c + 1, 1)
                    lo_unit(L, 0, a0 + c + 1, 2)
                hidden(0, c)
                if following:
                    lo_unit(L, 0, a0 + c + 1, 3)
                hidden_lo(0, c, actT_hi[:, 0:2, :], actT_lo[:, 0:2, :])
                for u in range(2):
                    lo_b_unit(L, 0, b0 + c, u)

            def norm(L, k, coef, eps):
                def normalise(t):
                    dve.wait_ge(s["rs_ready"], L * 6 + 2 * k + t + 1)
                    TS(z[:, t, :], z[:, t, :], mv[:, t, 0:1], rstd[:, t:t + 1], SUB, MUL).then_inc(s["z_ready"], 1)

                for t in range(NT):
                    dve.wait_ge(s["ffn_done"], L * 6 + 2 * k + t + 1)
                    for half in range(2):
                        q = slice(512 * half, 512 * half + 512)
                        STT(z[:, t, q], x[:, t, q], coef, ps[:, ACC + 2 * t + half, :], MUL, ADD)
                    dve.drain().then_inc(s["acc_read"], 1)
                    if t == 1:
                        normalise(0)
                    for half in range(2):
                        dve.bn_stats(stats[:, t, half, :], z[:, t, 512 * half:512 * half + 512])
                    dve.drain()
                    dve.bn_aggr(mv[:, t, :], stats[:, t, :, :].rearrange("p a b -> p (a b)"))
                    dve.drain()
                    TS(var[:, t:t + 1], mv[:, t, 1:2], eps, None, ADD).then_inc(s["var_ready"], 1)
                normalise(1)

            def norm_turned(L, k, g, b):
                for i in (0, 1):
                    dve.wait_ge(s["turned"], L * 12 + 4 * (k + 1) + i + 1)
                    for kk in range(2):
                        c = 2 * i + kk
                        ins = TS(lnT[:, c, :], ps[:, LN_BANKS[i], kk * SEQ:(kk + 1) * SEQ],
                                 lp[:, g, c:c + 1], lp[:, b, c:c + 1], MUL, ADD)
                    ins.then_inc(s["lnT_scaled"], 1)
                base = (4, 8)[k]
                for i in range(4):
                    dve.wait_ge(s["actT_hi_ready"], L * 12 + base + i + 1)
                    q = slice(2 * i, 2 * i + 2)
                    TT(actT_lo[:, q, :], lnT[:, q, :], actT_hi[:, q, :].bitcast(F32), SUB).then_inc(s["actT_ready"], 1)

            dve.sem_inc(a_lo, A_UNITS)
            dve.sem_inc(b_lo, B_UNITS)
            dve.wait_ge(s["ident_set"], 1)
            dve.tensor_reduce(parity[:, :], ident[:, :].rearrange("p (g q d) -> p q g d", q=2, d=SSM_GROUP),
                              AX.XY, ADD)
            dve.wait_ge(s["causal_set"], 1)
            dve.wait_ge(s["table_turned"], 1)
            dve.tensor_copy(z[0:N_ATT, 0, 0:3 * P], ps[0:N_ATT, 5, 0:3 * P]).then_inc(s["table_out"], 1)

            with dve.Fori(0, DEPTH) as L:
                for p in range(2):
                    lo_unit(L, 0, A_FFN1, p)
                for i in range(4):
                    dve.wait_ge(s["actT_hi_ready"], L * 12 + i + 1)
                    q = slice(2 * i, 2 * i + 2)
                    TT(flat(actT_lo[:, q, :]), ps[:, LN_BANKS[i], :], flat(actT_hi[:, q, :]).bitcast(F32),
                       SUB).then_inc(s["actT_ready"], 1)
                for p in range(2, 4):
                    lo_unit(L, 0, A_FFN1, p)
                dve.wait_ge(s["dtrow_loaded"], L * 16 + 16)
                dve.tensor_copy(rows[R_DT:R_DT + 8, :].rearrange("p (g q) -> p g q", g=2),
                                bc(dt_row[R_DT:R_DT + 8, :], SSM_STATE)).then_inc(s["dt_expanded"], 1)
                ffn(L, A_FFN1, B_FFN1, 0, True)
                dve.wait_ge(s["twiddles"], L + 1)
                norm(L, 0, 2 * ALPHA, 4 * LN_EPS)
                norm_turned(L, 0, Q_G1, Q_B1)

                def index_scores(qb, n):
                    N = P * (qb + 1)
                    off = SEQ - N
                    dve.wait_ge(s["ixs_done"], L * 2 + n + 1)
                    for hh in range(2):
                        STT(relu_w[:, 4 * hh:4 * hh + 4, 0:N], ps[:, 4:8, hh * SEQ:hh * SEQ + N], 0.0,
                            bc(wis[:, qb, 4 * hh:4 * hh + 4], N), MAX, MUL)
                    dve.drain().then_inc(s["ixs_read"], 1)
                    dve.tensor_reduce(isc[:, 0:N], relu_w[:, :, 0:N].rearrange("p h s -> p s h"), AX.X, ADD)
                    dve.drain()
                    TT(work[:, 0:N], isc[:, 0:N], causal[:, off:SEQ], ADD)
                    for _ in range(TOPK // 8):
                        dve.drain()
                        dve.max(top8[:, :], work[:, 0:N])
                        dve.drain()
                        dve.match_replace(work[:, 0:N], top8[:, :], work[:, 0:N], TAKEN)
                    dve.drain()
                    TS(sel[:, qb, 0:N], work[:, 0:N], TAKEN, NEG, ALU.not_equal, MUL)
                    dve.drain()

                for i in range(WIN_GROUPS):
                    for p in range(4):
                        lo_unit(L, 0, A_WIN + i + 1, p)
                    if i == 2:
                        dve.wait_ge(s["hp_ready"], L * WIN_GROUPS + 2)
                        dve.tensor_copy(kdup[:, :, 0:P].rearrange("p t (r d) -> p t r d", r=4),
                                        hp[:, :, C_IK:C_IK + 32].unsqueeze(2).broadcast_to([P, NT, 4, 32]))
                        dve.tensor_copy(kdup[:, :, P:2 * P].rearrange("p t (r d) -> p t r d", r=2),
                                        hp[:, :, C_SK:C_SK + 64].unsqueeze(2).broadcast_to([P, NT, 2, 64]))
                        TS(wis[:, :, :], hp[:, :, C_IW:C_IW + 8], IDX_HEADS ** -0.5 * IDX_DIM ** -0.5, None, MUL)
                        dve.drain().then_inc(s["kdup_ready"], 1)
                    if i == 4:
                        index_scores(1, 0)
                    if i == 5:
                        index_scores(0, 1)

                dve.wait_ge(s["bias_ready"], 1)
                dve.wait_ge(s["x_updated"], L * 2 + 1)
                for i in range(UNITS + 1):
                    if i < UNITS:
                        hd, qb = i // 2, i % 2
                        N = P * (qb + 1)
                        dve.wait_ge(s["das_done"], L * UNITS + i + 1)
                        STT(da_e[:, i % 2, :, 0:N], ps[:, 4:6, 0:N], DA_QK ** -0.5,
                            rep(bias[:, hd, SEQ - N:SEQ], 2), MUL, ADD)
                        dve.drain().then_inc(s["das_read"], 1)
                        dve.tensor_reduce(da_nm[:, i % 2, :], da_e[:, i % 2, :, 0:N], AX.X, MAX,
                                          negate=True).then_inc(s["da_max"], 1)
                        j = i
                        dve.wait_ge(s["bu_done"], L * 8 + j + 1)
                        bu = ps[:, j % 2, :].rearrange("p (c t) -> p c t", c=2)
                        TT(rot[:, 0, :, :], bu, rep(tw_re[:, j, :], 2), MUL)
                        TT(rot[:, 1, :, :], bu, rep(tw_im[:, j, :], 2), MUL)
                        dve.drain().then_inc(s["bu_read"], 1)
                        TT(derot[:, 0, :], rot[:, 0, 0, :], rot[:, 1, 1, :], ADD)
                        TT(derot[:, 1, :], rot[:, 0, 1, :], rot[:, 1, 0, :], SUB)
                        dve.drain()
                        if j >= 2:
                            dve.wait_ge(s["prod_ready"], L * 8 + j - 1)
                        for c in range(2):
                            ins = dve.tensor_tensor_scan(ys[:, j % 2, c, :],
                                                         lp[:, Q_MAG, j:j + 1].broadcast_to([P, SEQ]),
                                                         derot[:, c, :], 0.0, MUL, ADD)
                        dve.drain().then_inc(s["y_ready"], 1)
                    if i < UNITS:
                        u = i
                        dve.wait_ge(s["da_exp"], L * UNITS + u + 1)
                        dve.reciprocal(da_r[:, u, :], da_sum[:, u, :])
                        dve.drain()
                        TT(da_r[:, u, 1:2], da_r[:, u, 1:2], lp[:, Q_MISC, M_NLAM:M_NLAM + 1], MUL)
                        TS(da_e[:, u % 2, 0, 0:N], da_e[:, u % 2, 0, 0:N], da_r[:, u, 0:1], None, MUL)
                        dve.drain()
                        STT(da_e[:, u % 2, 0, 0:N], da_e[:, u % 2, 1, 0:N], da_r[:, u, 1:2],
                            da_e[:, u % 2, 0, 0:N], MUL, ADD)
                        dve.drain().then_inc(s["da_a"], 1)
                dve.wait_ge(s["da_o_out"], L * UNITS + UNITS)
                TS(ss[:, :, :], ss[:, :, :], 1.0 / DA_V, LN_EPS, MUL, ADD).then_inc(s["ss_scaled"], 1)
                dve.wait_ge(s["c_done"], L * 8 + 8)
                for qb in range(NT):
                    N = P * (qb + 1)
                    dve.wait_ge(s["sas_done"], L * 2 + qb + 1)
                    STT(sa_e[:, :, 0:N], ps[:, 4:8, 0:N], SA_DIM ** -0.5, bias[:, DA_HEADS:, SEQ - N:SEQ], MUL, ADD)
                    dve.drain().then_inc(s["sas_read"], 1)
                    TT(sa_e[:, :, 0:N], sa_e[:, :, 0:N], rep(sel[:, qb, 0:N], SA_HEADS), ADD)
                    dve.drain()
                    dve.tensor_reduce(sa_nm[:, qb, :], sa_e[:, :, 0:N], AX.X, MAX, negate=True).then_inc(s["sa_max"], 1)
                    if qb == 0:
                        dve.wait_ge(s["rms_ready"], L + 1)
                        for t in range(NT):
                            m = hp[:, t, 0:DA_HEADS * DA_V].rearrange("p (h e) -> p h e", h=DA_HEADS)
                            TT(m, m, bc(rms[:, t, :], DA_V), MUL)
                        dve.drain().then_inc(s["mix_da"], 1)
                    dve.wait_ge(s["sa_exp"], L * 2 + qb + 1)
                    dve.reciprocal(sa_sum[:, qb, :], sa_sum[:, qb, :])
                    dve.drain()
                    dve.wait_ge(s["sa_o"], L * 2 + qb + 1)
                    TT(hp[:, qb, 768:1024].rearrange("p (h e) -> p h e", h=SA_HEADS),
                       ps[:, 3, 0:256].rearrange("p (h e) -> p h e", h=SA_HEADS), bc(sa_sum[:, qb, :], SA_DIM),
                       MUL).then_inc(s["mix_sa"], 1)
                for t in range(2):
                    ins = STT(ys2[:, 0, t, :], uT[:, t, :], lp[:, Q_MISC, M_D + t:M_D + t + 1],
                              ps[:, 2, t * SEQ:(t + 1) * SEQ], MUL, ADD)
                ins.then_inc(s["y_full"], 1)
                dve.wait_ge(s["glu_act"], L + 1)
                TT(ysg, ysg, ys2[:, 1, :, :], MUL).then_inc(s["ssm_out"], 1)
                dve.wait_ge(s["mixT_hi"], L * 4 + 1)
                TT(actT_lo[:, 4:6, :], ysg, actT_hi[:, 4:6, :].bitcast(F32), SUB).then_inc(s["actT_ready"], 1)
                for n, b in enumerate((0, 1, 3)):
                    dve.wait_ge(s["mixT_hi"], L * 4 + n + 2)
                    q = slice(2 * b, 2 * b + 2)
                    bank, hi = ps[:, LN_BANKS[b], :], flat(actT_hi[:, q, :]).bitcast(F32)
                    if b < 2:
                        ins = STT(flat(actT_lo[:, q, :]), bank, lp[:, Q_MISC, M_SUB:M_SUB + 1], hi, MUL, SUB)
                    else:
                        ins = TT(flat(actT_lo[:, q, :]), bank, hi, SUB)
                    ins.then_inc(s["actT_ready"], 1)
                for p in range(4):
                    lo_unit(L, 0, A_WO + 1, p)
                for u in range(2):
                    lo_b_unit(L, 0, B_PROJ, u)
                norm(L, 1, ALPHA, LN_EPS)
                for p in range(2):
                    lo_unit(L, 0, A_GATE, p)
                norm_turned(L, 1, Q_G2, Q_B2)
                for p in range(2, 4):
                    lo_unit(L, 0, A_GATE, p)
                for i in range(2):
                    for p in range(4):
                        lo_unit(L, 0, A_GATE + i + 1, p)
                    for t in range(NT):
                        q = slice(512 * i, 512 * i + 512)
                        dve.wait_ge(s["gate_sig"], L * 4 + 2 * i + t + 1)
                        if i == 0 and t == 0:
                            dve.wait_ge(s["proj_done"], L * 2 + 2)
                        TT(z[:, t, q], z[:, t, q], ps[:, ACC + 2 * t + i, :], MUL)
                        dve.drain()
                        STT(x[:, t, q], x[:, t, q], ALPHA, z[:, t, q], MUL, ADD).then_inc(s["ple_done"], 1)
                ffn(L, A_FFN2, B_FFN2, 1, False)
                norm(L, 2, 2.0, 4 * LN_EPS)
                dve.drain()
                dve.wait_ge(s["gb_loaded"], L * 96 + 96)
                TT(x[:, 0, :], z[:, 0, :], gb[:, 0, :], MUL)
                dve.drain()
                TT(x[:, 0, :], x[:, 0, :], gb[:, 1, :], ADD)
                dve.drain().then_inc(s["x_ready"], 1)

        @block.tensor
        def _(pe):
            def turn(out, src):
                return pe.transpose(out, src, ident[:, :])

            def wait_a(L, n, k, p):
                pe.wait_ge(a_lo, L * A_ALL + n * A_UNITS + (A_UNITS + k * A_UNITS + p + 1))

            def group(L, n, k, bank, cols, middle=None, acts=None):
                for p in range(A_UNITS):
                    wait_a(L, n, k, p)
                    if acts is not None:
                        wait_act(L, acts + max(p + 1, 2))
                    for kt in (2 * p, 2 * p + 1):
                        for t in range(NT):
                            q = slice(t * P, (t + 1) * P)
                            ins = mm3(pe, ps[:, bank + t, 0:cols], actT_hi[:, kt, q], actT_lo[:, kt, q],
                                      hi_a[:, kt, 0:cols], lo_a[:, kt, 0:cols], kt == 0, kt == KT - 1)
                    ins.then_inc(a_used, 1)
                    if p == 1 and middle:
                        middle()

            def rows2(L, m, k, hi, lo, first, last, done=None, middle=None):
                if not last:
                    for u in range(B_UNITS):
                        pe.wait_ge(b_lo, L * B_ALL + m * B_UNITS + (B_UNITS + k * B_UNITS + u + 1))
                        for t in range(NT):
                            for half in range(2):
                                q, w = slice(t * P, (t + 1) * P), slice(half * 512, half * 512 + 512)
                                ins = mm3(pe, ps[:, ACC + 2 * t + half, :], hi[:, u, q], lo[:, u, q],
                                          hi_b[:, u, w], lo_b[:, u, w], first and u == 0, False)
                        ins.then_inc(b_used, 1)
                        if u == 0 and middle:
                            middle()
                    return
                for u in range(B_UNITS):
                    pe.wait_ge(b_lo, L * B_ALL + m * B_UNITS + (B_UNITS + k * B_UNITS + u + 1))
                    for t in range(NT):
                        for half in range(2):
                            q, w = slice(t * P, (t + 1) * P), slice(half * 512, half * 512 + 512)
                            ins = mm3(pe, ps[:, ACC + 2 * t + half, :], hi[:, u, q], lo[:, u, q],
                                      hi_b[:, u, w], lo_b[:, u, w], first and u == 0, u == B_UNITS - 1)
                        if u == B_UNITS - 1:
                            ins.then_inc(s[done], 1)
                pe.drain().then_inc(b_used, 2)

            def ffn(L, a0, b0, f, before_down, after_first=None, acts=None):
                base = f * CHUNKS

                def turn_h(c, k):
                    pe.wait_ge(s["h_ready"], L * 4 * CHUNKS + c * 2 + 2 * (base + k + 1))
                    for u in range(2):
                        for t in range(NT):
                            ins = turn(ps[:, TR, u * SEQ + t * P:u * SEQ + (t + 1) * P], h[:, t, u * P:(u + 1) * P])
                    ins.then_inc(s["h_turned"], 1)

                def gate_up(c, k, middle=None, acts=None):
                    pe.wait_ge(s["h_ready"], L * 4 * CHUNKS + c * 2 + 2 * (base + k))
                    group(L, c, a0 + k, GU, 2 * CHUNK, middle, acts)

                def down(c, k, hi=hT_hi, lo=hT_lo, first=False, last=False, middle=None):
                    pe.wait_ge(s["hT_ready"], L * 2 * CHUNKS + c + (base + k + 1))
                    rows2(L, c, b0 + k, hi, lo, first, last, "ffn_done", middle)

                gate_up(0, 0, acts=acts)
                if after_first:
                    after_first()
                gate_up(0, 1, lambda: turn_h(0, 0))
                before_down()
                down(0, 0, first=True)
                with pe.Fori(2, CHUNKS - 1) as c:
                    gate_up(c, 0, lambda: turn_h(c, -1))
                    down(c, -1)
                c = CHUNKS - 1
                gate_up(0, c, lambda: turn_h(0, c - 1))
                down(0, c - 1, middle=lambda: turn_h(0, c))
                down(0, c, actT_hi, actT_lo, last=True)

            def turn_norm(L, k, src, ready):
                for t in range(NT):
                    ready(t)
                    for i in range(4):
                        for kk in range(2):
                            c = 2 * i + kk
                            ins = turn(ps[:, LN_BANKS[i], kk * SEQ + t * P:kk * SEQ + (t + 1) * P],
                                       src[:, t, c * P:(c + 1) * P])
                        if t == NT - 1:
                            ins.then_inc(s["turned"], 1)

            def wait_act(L, k):
                pe.wait_ge(s["actT_ready"], L * 16 + k)

            pe.sem_inc(a_used, A_UNITS)
            pe.sem_inc(b_used, B_UNITS)
            pe.wait_ge(s["ident_set"], 1)
            pe.wait_ge(s["sel_loaded"], 32)
            pe.matmul(ps[0:N_ATT, 5, 0:3 * P], tw_re[0:REL_BUCKETS, 0, 0:N_ATT],
                      tw_im[0:REL_BUCKETS, 0:2, :].rearrange("p a t -> p (a t)")[:, 0:3 * P],
                      start=True, stop=True).then_inc(s["table_turned"], 1)
            pe.wait_ge(s["x_loaded"], 16)
            pe.wait_ge(s["table_out"], 1)

            with pe.Fori(0, DEPTH) as L:
                def input_ready(t):
                    pe.wait_ge(s["x_ready" if t == 0 else "x_half"], L)
                turn_norm(L, 0, x, input_ready)

                def turn_small():
                    pe.wait_ge(s["rows_loaded"], L * 128 + 128)
                    pe.wait_ge(s["dt_expanded"], L + 1)
                    pe.wait_ge(s["p_loaded"], L * 16 + 16)
                    for u in range(2):
                        for t in range(NT):
                            ins = turn(ps[:, ACC, u * SEQ + t * P:u * SEQ + (t + 1) * P], p_nat[:, t, u * P:(u + 1) * P])
                    ins.then_inc(s["p_turned"], 1)
                    pe.transpose(ps[:, ACC + 1, 0:ROWS], rows[0:ROWS, :], ident[0:ROWS, 0:ROWS])\
                        .then_inc(s["rows_turned"], 1)

                def small_out():
                    pe.wait_ge(s["prm_out"], L + 1)
                    pe.wait_ge(s["pT_ready"], L + 1)

                ffn(L, A_FFN1, B_FFN1, 0, small_out, turn_small, acts=0)
                pe.wait_ge(s["b_ready"], L + 1)
                for half in range(2):
                    for part in range(2):
                        ins = turn(ps[:, MISC, (2 * half + part) * P:(2 * half + part + 1) * P],
                                   b_exp[:, part, 4 * half:4 * half + 4, :].rearrange("p j c -> p (j c)"))
                ins.then_inc(s["bc_turned"], 1)
                pe.wait_ge(s["c_ready"], L + 1)
                pe.wait_ge(s["hT_ready"], L * 2 * CHUNKS + CHUNKS)
                for part in range(2):
                    for half in range(2):
                        ins = turn(ps[:, TR, (2 * part + half) * P:(2 * part + half + 1) * P],
                                   c_exp[:, part, half, :, :].rearrange("p q d -> p (q d)"))
                ins.then_inc(s["bc_turned"], 1)
                pe.wait_ge(s["in_out"], L + 1)
                pe.wait_ge(s["c_out"], L + 1)
                turn_norm(L, 1, z, lambda t: pe.wait_ge(s["z_ready"], L * 6 + t + 1))
                for i in range(WIN_GROUPS):
                    if i >= 2:
                        pe.wait_ge(s["hp_ready"], L * WIN_GROUPS + i - 1)
                    group(L, 0, A_WIN + i, 2 * (i % 2), WIN_COLS, acts=4 if i == 0 else None)
                    pe.drain().then_inc(s["win_done"], 1)
                    if i == 3:
                        pe.wait_ge(s["hp_ready"], L * WIN_GROUPS + 3)
                        pe.wait_ge(s["kdup_ready"], L + 1)
                        for bank, src, c0 in ((6, hp, C_IQ), (7, kdup, 0), (4, hp, C_SQ), (5, hp, C_U)):
                            for u in range(2):
                                for t in range(NT):
                                    ins = turn(ps[:, bank, u * SEQ + t * P:u * SEQ + (t + 1) * P],
                                               src[:, t, c0 + u * P:c0 + (u + 1) * P])
                            ins.then_inc(s["ix_turned"], 1)
                    if i >= 4:
                        qb = 5 - i
                        N = P * (qb + 1)
                        pe.wait_ge(s["ix_out"], L * 4 + 4)
                        if i == 5:
                            pe.wait_ge(s["ixs_read"], L * 2 + 1)
                        for hd in range(IDX_HEADS):
                            r = 32 * (hd % 4)
                            ins = pe.matmul(ps[:, 4 + hd % 4, (hd // 4) * SEQ:(hd // 4) * SEQ + N],
                                            iqT[r:r + 32, hd // 4, qb * P:(qb + 1) * P], ksT[r:r + 32, 0, 0:N],
                                            start=True, stop=True)
                        pe.drain().then_inc(s["ixs_done"], 1)
                pe.wait_ge(s["hp_ready"], L * WIN_GROUPS + WIN_GROUPS)
                for n in range(4):
                    for u in range(2):
                        for t in range(NT):
                            c0 = (2 * n + u) * P
                            ins = turn(ps[:, n, u * SEQ + t * P:u * SEQ + (t + 1) * P], hp[:, t, c0:c0 + P])
                    ins.then_inc(s["qk_turned"], 1)
                pe.wait_ge(s["qk_out"], L * 4 + 4)
                pe.wait_ge(s["ixs_read"], L * 2 + 2)
                for i in range(UNITS + 2):
                    if i < UNITS:
                        hd, qb = i // 2, i % 2
                        N = P * (qb + 1)
                        if i >= 1:
                            pe.wait_ge(s["das_read"], L * UNITS + i)
                        for c in range(2):
                            r = slice(64 * c, 64 * c + 64)
                            ins = pe.matmul(ps[:, 4 + c, 0:N], qT[r, hd, qb * P:(qb + 1) * P], kT[r, hd, 0:N],
                                            start=True, stop=True)
                        pe.drain().then_inc(s["das_done"], 1)
                        j = i
                        if j >= 2:
                            pe.wait_ge(s["bu_read"], L * 8 + j - 1)
                        r = slice(32 * (j % 4), 32 * (j % 4) + 32)
                        for part in range(2):
                            ins = pe.matmul(ps[:, j % 2, part * SEQ:(part + 1) * SEQ], inT[r, j // 4, part, :],
                                            uT[r, j // 4, :], start=True, stop=True)
                        ins.then_inc(s["bu_done"], 1)
                    if 1 <= i <= UNITS:
                        u = i - 1
                        hd, qb = u // 2, u % 2
                        pe.wait_ge(s["da_a"], L * UNITS + u + 1)
                        if u >= 1:
                            pe.wait_ge(s["da_aT"], L * UNITS + u)
                        for kb in range(qb + 1):
                            ins = turn(ps[:, 6, kb * P:(kb + 1) * P], da_e[:, u % 2, 0, kb * P:(kb + 1) * P])
                        ins.then_inc(s["da_turned"], 1)
                        pe.wait_ge(s["da_aT"], L * UNITS + u + 1)
                        if u >= 1:
                            pe.wait_ge(s["da_o_out"], L * UNITS + u)
                        for kb in range(qb + 1):
                            ins = pe.matmul(ps[:, 7, 0:P], aT[:, u % 2, kb * P:(kb + 1) * P],
                                            hp[:, kb, C_V + hd * DA_V:C_V + (hd + 1) * DA_V],
                                            start=kb == 0, stop=kb == qb)
                        ins.then_inc(s["da_o"], 1)
                    if i >= 2:
                        j = i - 2
                        pe.wait_ge(s["prod_ready"], L * 8 + j + 1)
                        r = slice(32 * (j % 4), 32 * (j % 4) + 32)
                        for n, (w, tw, part) in enumerate(((0, 0, 0), (1, 1, 1), (2, 1, 0), (2, 0, 1))):
                            ins = pe.matmul(ps[r, 2, (j // 4) * SEQ:(j // 4 + 1) * SEQ], outT[:, j, w, :],
                                            prod[:, j % 2, tw, part, :], start=n == 0, stop=n == 3)
                        ins.then_inc(s["c_done"], 1)
                pe.wait_ge(s["da_o_out"], L * UNITS + UNITS)
                for qb in range(NT):
                    N = P * (qb + 1)
                    if qb:
                        pe.wait_ge(s["sas_read"], L * 2 + 1)
                    for hd in range(SA_HEADS):
                        r = slice(64 * (hd % 2), 64 * (hd % 2) + 64)
                        ins = pe.matmul(ps[:, 4 + hd, 0:N], saqT[r, hd // 2, qb * P:(qb + 1) * P], ksT[r, 1, 0:N],
                                        start=True, stop=True)
                    pe.drain().then_inc(s["sas_done"], 1)
                    pe.wait_ge(s["sa_exp"], L * 2 + qb + 1)
                    if qb:
                        pe.wait_ge(s["sa_aT_ready"], L * 4 + 2)
                        pe.wait_ge(s["mix_sa"], L * 2 + 1)
                    for half in range(2):
                        for b in range(2 * (qb + 1)):
                            hd, kb = 2 * half + b // (qb + 1), b % (qb + 1)
                            ins = turn(ps[:, half, b * P:(b + 1) * P], sa_e[:, hd, kb * P:(kb + 1) * P])
                        ins.then_inc(s["sa_turned"], 1)
                    pe.wait_ge(s["sa_aT_ready"], L * 4 + 2 * qb + 2)
                    for hd in range(SA_HEADS):
                        for kb in range(qb + 1):
                            c0 = (hd // 2) * 512 + ((hd % 2) * (qb + 1) + kb) * P
                            ins = pe.matmul(ps[:, 3, hd * SA_DIM:(hd + 1) * SA_DIM], sa_aT[:, c0:c0 + P],
                                            hp[:, kb, C_SV:C_SV + SA_DIM], start=kb == 0, stop=kb == qb)
                    ins.then_inc(s["sa_o"], 1)
                pe.wait_ge(s["gelu_done"], L + 1)
                pe.wait_ge(s["glu_loaded"], L * 16 + 16)
                for o in range(2):
                    for t in range(2):
                        ins = pe.matmul(ps[:, 2, o * SEQ:(o + 1) * SEQ], glu[:, t, o * P:(o + 1) * P],
                                        ys2[:, 1, t, :], start=t == 0, stop=t == 1)
                ins.then_inc(s["glu_done"], 1)
                pe.wait_ge(s["mix_da"], L + 1)
                pe.wait_ge(s["mix_sa"], L * 2 + 2)
                for b, c0 in ((0, 0), (1, 256), (3, 768)):
                    for u in range(2):
                        for t in range(NT):
                            ins = turn(ps[:, LN_BANKS[b], u * SEQ + t * P:u * SEQ + (t + 1) * P],
                                       hp[:, t, c0 + u * P:c0 + (u + 1) * P])
                    ins.then_inc(s["mix_turned"], 1)
                def project(i, kt, t):
                    q = slice(t * P, (t + 1) * P)
                    return mm3(pe, ps[:, ACC + 2 * t + i, :], actT_hi[:, kt, q], actT_lo[:, kt, q],
                               hi_a[:, kt, :], lo_a[:, kt, :], kt == 0, kt == KT - 1)

                wait_act(L, 12)
                for p in range(A_UNITS):
                    wait_a(L, 0, A_WO, p)
                    for kt in (2 * p, 2 * p + 1):
                        for t in range(NT):
                            ins = project(0, kt, t)
                    ins.then_inc(a_used, 1)
                for t in range(NT):
                    for kt in range(KT):
                        if t == 0 and kt % 2 == 0:
                            wait_a(L, 0, A_WO + 1, kt // 2)
                        ins = project(1, kt, t)
                        if t == NT - 1 and kt % 2 and kt < KT - 1:
                            ins.then_inc(a_used, 1)
                    ins.then_inc(s["ffn_done"], 1)
                pe.drain().then_inc(a_used, 1)
                turn_norm(L, 2, z, lambda t: pe.wait_ge(s["z_ready"], L * 6 + 2 + t + 1))
                pe.wait_ge(s["acc_read"], L * 6 + 4)
                rows2(L, 0, B_PROJ, pT_hi, pT_lo, True, True, "proj_done")
                for i in range(2):
                    group(L, 0, A_GATE + i, (GU, TR)[i], 512, acts=12 if i == 0 else None)
                    pe.drain().then_inc(s["gate_done"], 1)
                pe.wait_ge(s["gate_sig"], L * 4 + 2)
                ffn(L, A_FFN2, B_FFN2, 1, lambda: pe.wait_ge(s["ple_done"], L * 4 + 4))


INS = ["x", "p", "rel_bias", "ffn1_w_gate", "ffn1_w_up", "ffn1_w_down", "ln1_g", "ln1_b", "w_in", "w_o",
       "da_lam_q1", "da_lam_k1", "da_lam_q2", "da_lam_k2", "da_subln_g", "ssm_lam_re", "ssm_lam_im", "ssm_log_dt",
       "ssm_b_re", "ssm_b_im", "ssm_c_re", "ssm_c_im", "ssm_d", "ssm_w_glu", "ln2_g", "ln2_b", "ffn2_w_gate",
       "ffn2_w_up", "ffn2_w_down", "ple_w_proj", "ple_w_gate", "ln3_g", "ln3_b"]


def kernel(**inputs):
    import concourse.bacc as bacc
    from concourse.bass_utils import run_bass_kernel_spmd

    nc = bacc.Bacc("TRN2", target_bir_lowering=False, num_devices=1)
    arrays, args = {}, {}
    for name in INS + ["selector"]:
        v = np.ascontiguousarray(inputs[name]) if name != "selector" else bucket_selector()
        arrays[f"in_{name}"] = v
        args[name] = nc.dram_tensor(f"in_{name}", v.shape, mybir.dt.from_np(v.dtype), kind="ExternalInput").ap()
    args["out"] = nc.dram_tensor("out_x", (1, SEQ, D_MODEL), F32, kind="ExternalOutput").ap()
    table = nc.dram_tensor("bias_table", (N_ATT, P, 3 * P), F32).ap()
    args["table"] = table
    args["table_rows"] = bass.AP(table.tensor, P - 1, [[3 * P - 1, P], [P * 3 * P, N_ATT], [1, SEQ]])
    build(nc, args)
    r = run_bass_kernel_spmd(nc, [arrays], core_ids=[0])
    return r.results[0]["out_x"]
```

```python
import math
from contextlib import ExitStack

import numpy as np

import concourse.bass as bass
from concourse import mybir
from concourse.alu_op_type import AluOpType as ALU

F32 = mybir.dt.float32
F32R = mybir.dt.float32r
ACT = mybir.ActivationFunctionType
AX = mybir.AxisListType

P = 128
D_MODEL, SEQ, DEPTH = 1024, 256, 2
PLE_DIM, D_FF = 256, 2816
KT = D_MODEL // P
NT = SEQ // P
DA_HEADS, DA_QK, DA_V = 4, 64, 128
SSM_GROUP, SSM_WIDTH, SSM_GROUPS, SSM_STATE = 16, 256, 16, 64
SA_HEADS, SA_DIM = 4, 64
IDX_HEADS, IDX_DIM = 8, 32
TOPK = SEQ // 4
REL_BUCKETS, REL_MAX_DIST = 32, 128
N_ATT = DA_HEADS + SA_HEADS
ALPHA = (2 * DEPTH) ** 0.25
LN_EPS = 1e-5
IN_SIZES = (512, 512, 512, SSM_WIDTH, 256, 64, 64, 256, 32, 8)
IN_COLS = sum(IN_SIZES)
C_Q, C_K, C_V, C_U, C_SQ, C_SK, C_SV, C_IQ, C_IK, C_IW = (sum(IN_SIZES[:i]) for i in range(10))

CHUNK = 256
CHUNKS = D_FF // CHUNK
WIN_GROUPS = 6
WIN_COLS = IN_COLS // WIN_GROUPS
assert CHUNKS * CHUNK == D_FF and WIN_COLS * WIN_GROUPS == IN_COLS and WIN_COLS % 2 == 0

A_FFN1, A_WIN = 0, CHUNKS
A_WO = A_WIN + WIN_GROUPS
A_GATE = A_WO + 2
A_FFN2 = A_GATE + 2
A_GROUPS = A_FFN2 + CHUNKS
B_FFN1, B_PROJ = 0, CHUNKS
B_FFN2 = B_PROJ + 1
B_GROUPS = B_FFN2 + CHUNKS
A_UNITS, B_UNITS = 4, 2
A_ALL, B_ALL = A_GROUPS * A_UNITS, B_GROUPS * B_UNITS

NEG = -1e30
TAKEN = -3e38
STATE_TILES = SSM_GROUPS // 2
UNITS = DA_HEADS * NT
TILE_ORDER = [*range(STATE_TILES // 2, STATE_TILES), *range(STATE_TILES // 2)]
MIX_ROWS = (0, 6, 2, 4)
SA_SCORES, SA_TURN, SA_OUT, SA_SCALE = {1: 1, 5: 0}, {3: 1, 7: 0}, {4: 1, 8: 0}, {5: 1, 9: 0}
BU_LATE, SCAN_LATE, C_LATE = {1: 7}, {1: 5, 3: 6, 5: 7}, {0: 3, 2: 4, 4: 5, 6: 6, 8: 7}

R_DT, R_G1, R_B1, R_G2, R_B2, R_RE, R_IM, R_D, R_SUB, ROWS = 0, 8, 16, 24, 32, 40, 48, 56, 58, 59
Q_G1, Q_B1, Q_G2, Q_B2, Q_MAG, Q_COS, Q_SIN, Q_FRE, Q_FIM, Q_MISC, NQ = range(11)
M_D, M_SUB, M_NLAM = 0, 2, 3

TWO_PI = 2 * math.pi
PI_A = 6.28125
PI_B = float(np.float32(round((TWO_PI - PI_A) * 2 ** 21) / 2 ** 21))
PI_C = float(np.float32(TWO_PI - PI_A - PI_B))
ROUND = 1.5 * 2 ** 23


def lam_init(layer):
    return 0.8 - 0.6 * math.exp(-0.3 * layer)


def bucket_selector():
    n = np.maximum(255 - np.arange(3 * P), 0)
    exact = REL_BUCKETS // 2
    nf = np.maximum(n, 1).astype(np.float32)
    large = exact + (np.log(nf / np.float32(exact)) / np.float32(math.log(REL_MAX_DIST / exact))
                     * np.float32(REL_BUCKETS - exact)).astype(np.int32)
    b = np.where(n < exact, n, np.minimum(large, REL_BUCKETS - 1))
    return (b[None, :] == np.arange(REL_BUCKETS)[:, None]).astype(np.float32)


def build(nc, a):
    ctx = ExitStack()
    with ctx:
        def sb(name, shape, dt=F32):
            return ctx.enter_context(nc.sbuf_tensor(name, shape, dt))

        def sem(name):
            return ctx.enter_context(nc.semaphore(name))

        raw_a = sb("raw_a", [P, 8, 512])
        raw_b = sb("raw_b", [P, 2, 1024])
        hi_a, lo_a = sb("hi_a", [P, 8, 512], F32R), sb("lo_a", [P, 8, 512], F32R)
        hi_b, lo_b = sb("hi_b", [P, 2, 1024], F32R), sb("lo_b", [P, 2, 1024], F32R)
        actT_hi, actT_lo = sb("actT_hi", [P, KT, SEQ], F32R), sb("actT_lo", [P, KT, SEQ], F32R)
        hT_hi, hT_lo = sb("hT_hi", [P, 2, SEQ], F32R), sb("hT_lo", [P, 2, SEQ], F32R)
        pT_hi, pT_lo = sb("pT_hi", [P, 2, SEQ], F32R), sb("pT_lo", [P, 2, SEQ], F32R)
        x = sb("x", [P, NT, D_MODEL])
        z = sb("z", [P, NT, D_MODEL])
        gb = sb("gb", [P, 2, D_MODEL])
        hp = sb("hp", [P, NT, IN_COLS])
        h = sb("h", [P, NT, CHUNK])
        bias = sb("bias", [P, N_ATT, SEQ])
        causal = sb("causal", [P, SEQ])
        ident = sb("ident", [P, P])
        tw_re, tw_im = sb("tw_re", [P, STATE_TILES, SEQ]), sb("tw_im", [P, STATE_TILES, SEQ])
        qT, kT = sb("qT", [P, DA_HEADS, SEQ]), sb("kT", [P, DA_HEADS, SEQ])
        saqT, iqT = sb("saqT", [P, 2, SEQ]), sb("iqT", [P, 2, SEQ])
        ksT = sb("ksT", [P, 2, SEQ])
        uT = sb("uT", [P, 2, SEQ])
        inT = sb("inT", [P, 2, 2, P])
        outT = sb("outT", [P, STATE_TILES, 2, 32])
        b_exp = sb("b_exp", [P, 2, STATE_TILES, 32])
        parity = sb("parity", [P, 2])
        bu_sb = sb("bu_sb", [P, 2, 2, SEQ])
        glu = sb("glu", [P, 2, SSM_WIDTH])
        dt_row = sb("dt_row", [P, 2])
        prmT = sb("prmT", [P, ROWS])
        lp = sb("lp", [P, NQ, 8])
        small = sb("small", [P, 8, 8])
        lams = sb("lams", [P, 2])
        lam_consts = sb("lam_consts", [P, 2, DEPTH])
        stats = sb("stats", [P, NT, 2, 6])
        mv = sb("mv", [P, NT, 2])
        var, rstd = sb("var", [P, NT]), sb("rstd", [P, NT])
        shift = sb("shift", [P, 2])
        mhalf = sb("mhalf", [P, 8])
        isc = sb("isc", [P, NT, SEQ])
        top8 = sb("top8", [P, NT, 8])
        sel = sb("sel", [P, NT, SEQ])
        wis = sb("wis", [P, NT, IDX_HEADS])
        da_e = sb("da_e", [P, 2, 2, SEQ])
        da_nm = sb("da_nm", [P, 2, 2])
        da_sum, da_r = sb("da_sum", [P, UNITS, 2]), sb("da_r", [P, UNITS, 2])
        aT = sb("aT", [P, 2, SEQ])
        junk = isc[:, 0, 0:P]
        ss, rms = sb("ss", [P, NT, DA_HEADS]), sb("rms", [P, NT, DA_HEADS])
        sa_nm, sa_sum = sb("sa_nm", [P, NT, SA_HEADS]), sb("sa_sum", [P, NT, SA_HEADS])
        hp_flat = hp[:, :, :].rearrange("p a c -> p (a c)")
        lnT = hp_flat[:, 0:2048].rearrange("p (k t) -> p k t", k=KT)
        p_nat = hp_flat[:, 2048:2560].rearrange("p (t d) -> p t d", t=NT)
        c_nat = hp_flat[:, 2560:2816].rearrange("p (r t d) -> p r t d", r=2, t=2)
        b_nat = hp_flat[:, 2816:3072].rearrange("p (r j c) -> p r j c", r=2, j=STATE_TILES)
        b_tmp = hp_flat[:, 3072:3328].rearrange("p (r j c) -> p r j c", r=2, j=STATE_TILES)
        c_exp = hp_flat[:, 3328:3840].rearrange("p (r t q d) -> p r t q d", r=2, t=2, q=2)
        lamv = hp_flat[:, 3840:4096].rearrange("p (i d) -> p i d", i=4)
        rows = hp_flat[:, 4096:4224]
        rot = z[:, 0, :].rearrange("p (a c t) -> p a c t", a=2, c=2)
        ys = z[:, 1, :].rearrange("p (a c t) -> p a c t", a=2, c=2)
        prod = gb[:, :, :].rearrange("p a (b c t) -> p a b c t", b=2, c=2)
        ys2 = z[:, 0, :].rearrange("p (v a t) -> p v a t", v=2, a=2)
        ysg = z[:, 1, 0:512].rearrange("p (a t) -> p a t", a=2)
        derot = h
        kdup = da_e[:, 0, :, :]
        relu_w = raw_b[:, :, :].rearrange("p a (h s) -> p (a h) s", s=SEQ)
        sa_e = raw_b[:, 0, :].rearrange("p (h s) -> p h s", s=SEQ)
        sa_aT = raw_b[:, 1, :]

        ps = ctx.enter_context(nc.psum_tensor("ps", [P, 8, 512], F32))
        GU, ACC, TR, MISC = 0, 2, 6, 7
        LN_BANKS = (0, 1, 6, 7)

        a_loaded = [sem(f"a_loaded{i}") for i in range(2)]
        b_loaded = [sem(f"b_loaded{i}") for i in range(2)]
        a_hi, a_lo, a_used = sem("a_hi"), sem("a_lo"), sem("a_used")
        b_hi, b_lo, b_used = sem("b_hi"), sem("b_lo"), sem("b_used")
        names = """x_loaded rows_loaded dtrow_loaded lamv_loaded sel_loaded ssm_loaded glu_loaded p_loaded
            gb_loaded gb_used ident_set causal_set dt_expanded rows_turned prm_out table_turned table_out table_stored
            bias_loaded bias_ready dt_exp sin_in sin_out lam_in lam_exp lp_ready
            x_ready turned lnT_scaled lnT_act actT_hi_ready actT_ready p_turned pT_hi_ready pT_ready
            gate_act h_ready h_turned hT_hi_ready hT_ready ffn_done acc_read var_ready rs_ready shift_ready z0_ready z1_ready
            twiddles b_ready c_ready bc_turned in_out c_out x_updated
            win_done hp_ready kdup_ready ix_turned ix_out qk_turned qk_out ixs_done ixs_read
            bu_done bu_out bu_used derot_ready y_ready prod_ready c_done
            das_done das_read da_max da_exp da_a da_turned da_aT da_o da_o_out ss_scaled rms_ready mix_da
            sas_done sas_read sa_max sa_exp sa_turned sa_aT_ready sa_o mix_sa
            y_full gelu_done glu_done glu_act ssm_out mix_turned mixT_hi
            proj_done gate_done gate_sig ple_done stored""".split()
        s = {n: sem(n) for n in names}

        block = ctx.enter_context(nc.Block())

        def mm3(pe, out, act_hi, act_lo, w_hi, w_lo, first, last):
            pe.matmul(out, act_hi, w_hi, start=first, stop=False)
            pe.matmul(out, act_hi, w_lo, start=False, stop=False)
            return pe.matmul(out, act_lo, w_hi, start=False, stop=last)

        def bc(ap, n):
            return ap.unsqueeze(ap.ndim).broadcast_to([*ap.shape, n])

        def rep(ap, n):
            return ap.unsqueeze(1).broadcast_to([ap.shape[0], n, *ap.shape[1:]])

        @block.sync
        def _(sp):
            def load(dst, src, done):
                return sp.dma_start(dst, src).then_inc(done, 16)

            def load_a(L, n, k, srcs):
                for half in range(2):
                    sp.wait_ge(a_lo, L * A_ALL + n * A_UNITS + (k * A_UNITS + 2 * half + 2))
                    for dst, src in srcs(4 * half):
                        load(dst, src, a_loaded[half])

            def load_b(L, m, k, src):
                for half in range(2):
                    sp.wait_ge(b_lo, L * B_ALL + m * B_UNITS + (k * B_UNITS + half + 1))
                    load(raw_b[:, half, :], src(half), b_loaded[half])

            def ffn(L, gate, up, down, a0, b0, small_loads=None, following=None):
                def gate_up(n, k, col):
                    def srcs(k0):
                        for i, w in enumerate((gate, up)):
                            yield (raw_a[:, k0:k0 + 4, i * CHUNK:(i + 1) * CHUNK],
                                   w[L, k0 * P:(k0 + 4) * P, bass.ds(col, CHUNK)]
                                   .rearrange("(k p) f -> p k f", p=P))
                    load_a(L, n, k, srcs)

                def down_rows(n, k, col):
                    load_b(L, n, k, lambda half: down[L, bass.ds(col + half * P, P), :])

                gate_up(0, a0, 0)
                if small_loads:
                    small_loads()
                with sp.Fori(0, CHUNKS - 1) as c:
                    col = sp.snap(c * CHUNK)
                    gate_up(c, a0 + 1, col + CHUNK)
                    down_rows(c, b0, col)
                if following:
                    following()
                down_rows(0, b0 + CHUNKS - 1, D_FF - CHUNK)

            def wide(w, L, c0, cols, pairs=(0, 2, 4, 6)):
                def srcs(k0):
                    for k in (k0 + 2, k0):
                        r = pairs[k // 2]
                        yield (raw_a[:, k:k + 2, 0:cols],
                               w[L, r * P:(r + 2) * P, c0:c0 + cols].rearrange("(k p) f -> p k f", p=P))
                return srcs

            def load_norm(L, g, b):
                load(gb[:, 0, :], g[bass.ds(L, 1), :].broadcast_to([P, D_MODEL]), s["gb_loaded"])
                load(gb[:, 1, :], b[bass.ds(L, 1), :].broadcast_to([P, D_MODEL]), s["gb_loaded"])

            load(x[:, :, :], a["x"][0].rearrange("(t p) d -> p t d", p=P), s["x_loaded"])

            with sp.Fori(0, DEPTH) as L:
                def small_loads():
                    load(p_nat[:, :, :], a["p"][L, 0].rearrange("(t p) d -> p t d", p=P), s["p_loaded"])
                    load(dt_row[R_DT:R_DT + 8, :], a["ssm_log_dt"][L].rearrange("(j g) -> j g", g=2), s["dtrow_loaded"])
                    for r, name in ((R_G1, "ln1_g"), (R_B1, "ln1_b"), (R_G2, "ln2_g"), (R_B2, "ln2_b")):
                        load(rows[r:r + 8, :], a[name][L].rearrange("(r c) -> r c", c=P), s["rows_loaded"])
                    for r, name in ((R_RE, "ssm_lam_re"), (R_IM, "ssm_lam_im")):
                        load(rows[r:r + 8, :], a[name][L].rearrange("(j g) p -> j (g p)", g=2), s["rows_loaded"])
                    load(rows[R_D:R_D + 2, :], a["ssm_d"][L].rearrange("(r c) -> r c", c=P), s["rows_loaded"])
                    load(rows[R_SUB:R_SUB + 1, :], a["da_subln_g"][bass.ds(L, 1), :], s["rows_loaded"])
                    for i, name in enumerate(("da_lam_q1", "da_lam_k1", "da_lam_q2", "da_lam_k2")):
                        load(lamv[:, i, :], a[name][bass.ds(L, 1), :].broadcast_to([P, DA_QK]), s["lamv_loaded"])
                    for i, name in enumerate(("ssm_b_re", "ssm_b_im")):
                        load(b_nat[:, i, :, :], a[name][L].rearrange("(j g) p c -> (g p) j c", g=2), s["ssm_loaded"])
                    for i, name in enumerate(("ssm_c_re", "ssm_c_im")):
                        load(c_nat[:, i, :, :], a[name][L].rearrange("(t g) c p -> (g c) t p", t=2), s["ssm_loaded"])
                    load(glu[:, :, :], a["ssm_w_glu"][L].rearrange("(t p) c -> p t c", p=P), s["glu_loaded"])
                def load_w_in(i):
                    load_a(L, 0, A_WIN + i, wide(a["w_in"], L, (WIN_GROUPS - 1 - i) * WIN_COLS, WIN_COLS))

                ffn(L, a["ffn1_w_gate"], a["ffn1_w_up"], a["ffn1_w_down"], A_FFN1, B_FFN1, small_loads,
                    lambda: load_w_in(0))
                sp.wait_ge(s["gb_used"], L * 3)
                load_norm(L, a["ln1_g"], a["ln1_b"])
                for i in range(1, WIN_GROUPS):
                    load_w_in(i)
                for i in range(2):
                    load_a(L, 0, A_WO + i, wide(a["w_o"], L, i * 512, 512, MIX_ROWS))
                sp.wait_ge(s["actT_ready"], L * 16 + 12)
                load_norm(L, a["ln2_g"], a["ln2_b"])
                load_b(L, 0, B_PROJ, lambda half: a["ple_w_proj"][L, half * P:(half + 1) * P, :])
                for i in range(2):
                    load_a(L, 0, A_GATE + i, wide(a["ple_w_gate"], L, i * 512, 512))
                sp.wait_ge(s["gb_used"], L * 3 + 2)
                load_norm(L, a["ln3_g"], a["ln3_b"])
                ffn(L, a["ffn2_w_gate"], a["ffn2_w_up"], a["ffn2_w_down"], A_FFN2, B_FFN2)

            for t in range(NT):
                sp.wait_ge(s["x_ready"], DEPTH * NT + t + 1)
                load(a["out"][0][t * P:(t + 1) * P, :], x[:, t, :], s["stored"])
            sp.wait_ge(s["stored"], NT * 16)

        @block.gpsimd
        def _(pool):
            TT, MUL, ADD, SUB = pool.tensor_tensor, ALU.mult, ALU.add, ALU.subtract
            def load_setup(dst, src, done):
                pool.dma_start(dst, src).then_inc(done, 16)

            pool.memset(ident[:, :], 0.0)
            pool.drain()
            pool.affine_select(out=ident[:, :], in_=ident[:, :], compare_op=ALU.not_equal, fill=1.0, base=0,
                               pattern=[[-1, P]], channel_multiplier=1)
            pool.drain().then_inc(s["ident_set"], 1)
            load_setup(tw_re[0:REL_BUCKETS, 0, 0:N_ATT], a["rel_bias"], s["sel_loaded"])
            load_setup(tw_im[0:REL_BUCKETS, 0:2, :].rearrange("p a t -> p (a t)")[:, 0:3 * P], a["selector"], s["sel_loaded"])
            pool.memset(causal[:, :], 0.0)
            pool.memset(mhalf[:, :], -0.5)
            for layer in range(DEPTH):
                pool.memset(lam_consts[:, 0, layer:layer + 1], lam_init(layer))
                pool.memset(lam_consts[:, 1, layer:layer + 1], 1.0 - lam_init(layer))
            pool.memset(b_exp[:, :, :, :], 0.0)
            pool.drain()
            pool.affine_select(out=causal[:, :], in_=causal[:, :], compare_op=ALU.is_ge, fill=NEG, base=P,
                               pattern=[[-1, SEQ]], channel_multiplier=1)
            pool.drain().then_inc(s["causal_set"], 1)
            pool.wait_ge(s["table_out"], 1)
            pool.dma_start(a["table"], z[0:N_ATT, 0, 0:3 * P].unsqueeze(1).broadcast_to([N_ATT, P, 3 * P]))\
                .then_inc(s["table_stored"], 16)
            pool.wait_ge(s["table_stored"], 16)
            pool.dma_start(bias[:, :, :], a["table_rows"]).then_inc(s["bias_loaded"], 16)
            pool.wait_ge(s["bias_loaded"], 16)
            TT(bias[:, :, :], bias[:, :, :], rep(causal[:, :], N_ATT), ADD)
            pool.drain().then_inc(s["bias_ready"], 1)

            def power(L, k):
                for t in range(NT):
                    pool.wait_ge(s["var_ready"], L * 6 + 2 * k + t + 1)
                    TT(rstd[:, t:t + 1], var[:, t:t + 1], mhalf[:, 0:1], ALU.pow).then_inc(s["rs_ready"], 1)
                    if t == 0 and k < 2:
                        pool.drain()
                        TT(shift[:, 1:2], shift[:, 0:1], rstd[:, 0:1], MUL).then_inc(s["shift_ready"], 1)

            def update_x(L, k):
                pool.wait_ge(s["gb_loaded"], L * 96 + 32 * (k + 1))
                for t in range(NT):
                    pool.wait_ge(s[f"z{t}_ready"], L * 2 + k + 1)
                    TT(x[:, t, :], z[:, t, :], gb[:, 0, :], MUL)
                pool.drain()
                for t in range(NT):
                    TT(x[:, t, :], x[:, t, :], gb[:, 1, :], ADD)
                pool.drain().then_inc(s["x_updated"], 1)
                pool.sem_inc(s["gb_used"], 1)

            def rms_power(L, pair):
                pool.wait_ge(s["ss_scaled"], L * 2 + pair + 1)
                q = slice(2 * pair, 2 * pair + 2)
                TT(rms[:, :, q], ss[:, :, q], mhalf[:, 0:4].rearrange("p (t h) -> p t h", t=NT),
                   ALU.pow).then_inc(s["rms_ready"], 1)

            with pool.Fori(0, DEPTH) as L:
                pool.wait_ge(s["lp_ready"], L + 1)
                pool.wait_ge(s["ssm_loaded"], L * 64 + 64)
                fre, fim = bc(lp[:, Q_FRE, :], SSM_GROUP), bc(lp[:, Q_FIM, :], SSM_GROUP)
                pool.wait_ge(s["x_ready"], L * NT + NT)
                for part, (f0, f1, op) in enumerate(((fre, fim, SUB), (fim, fre, ADD))):
                    TT(b_tmp[:, 0, :, :], b_nat[:, 0, :, :], f0, MUL)
                    TT(b_tmp[:, 1, :, :], b_nat[:, 1, :, :], f1, MUL)
                    pool.drain()
                    for g in range(2):
                        q = slice(64 * g, 64 * g + 64)
                        TT(b_exp[q, part, :, 16 * g:16 * g + 16], b_tmp[q, 0, :, :], b_tmp[q, 1, :, :], op)
                    pool.drain()
                pool.drain().then_inc(s["b_ready"], 1)
                for part in range(2):
                    for q in range(2):
                        TT(c_exp[:, part, :, q, :], c_nat[:, part, :, :],
                           parity[:, q:q + 1].unsqueeze(2).broadcast_to([P, 2, SSM_STATE]), MUL)
                pool.drain().then_inc(s["c_ready"], 1)
                pool.memset(tw_re[:, :, 0:1], 1.0)
                pool.memset(tw_im[:, :, 0:1], 0.0)
                pool.tensor_copy(tw_re[:, :, 1:2], lp[:, Q_COS, :].unsqueeze(2))
                pool.tensor_copy(tw_im[:, :, 1:2], lp[:, Q_SIN, :].unsqueeze(2))
                pool.drain()

                k = 1
                while k < SEQ:
                    for c0 in range(0, min(k, SEQ - 1 - k), 64):
                        m = min(64, k - c0, SEQ - 1 - k - c0)
                        src, dst = slice(1 + c0, 1 + c0 + m), slice(k + 1 + c0, k + 1 + c0 + m)
                        tmp = [z[:, i // 2, (i % 2) * 512:(i % 2) * 512 + STATE_TILES * m]
                               .rearrange("p (j t) -> p j t", j=STATE_TILES) for i in range(4)]
                        wr = tw_re[:, :, k:k + 1].broadcast_to([P, STATE_TILES, m])
                        wi = tw_im[:, :, k:k + 1].broadcast_to([P, STATE_TILES, m])
                        TT(tmp[0], tw_re[:, :, src], wr, MUL)
                        TT(tmp[1], tw_im[:, :, src], wi, MUL)
                        TT(tmp[2], tw_re[:, :, src], wi, MUL)
                        TT(tmp[3], tw_im[:, :, src], wr, MUL)
                        pool.drain()
                        TT(tw_re[:, :, dst], tmp[0], tmp[1], SUB)
                        TT(tw_im[:, :, dst], tmp[2], tmp[3], ADD)
                        pool.drain()
                    k *= 2
                pool.drain().then_inc(s["twiddles"], 1)

                power(L, 0)
                update_x(L, 0)
                for n in range(STATE_TILES + 1):
                    if n < STATE_TILES:
                        j = TILE_ORDER[n]
                        pool.wait_ge(s["bu_out"], L * STATE_TILES + n + 1)
                        for i, tw in enumerate((tw_re, tw_im)):
                            TT(rot[:, i, :, :], bu_sb[:, n % 2, :, :], rep(tw[:, j, :], 2), MUL)
                        pool.drain().then_inc(s["bu_used"], 1)
                        if n >= 1:
                            pool.wait_ge(s["y_ready"], L * STATE_TILES + n)
                        TT(derot[:, 0, :], rot[:, 0, 0, :], rot[:, 1, 1, :], ADD)
                        TT(derot[:, 1, :], rot[:, 0, 1, :], rot[:, 1, 0, :], SUB)
                        pool.drain().then_inc(s["derot_ready"], 1)
                    if n >= 1:
                        m, j = n - 1, TILE_ORDER[n - 1]
                        if n == STATE_TILES:
                            pool.wait_ge(s["y_ready"], L * STATE_TILES + n)
                        if m >= 2:
                            pool.wait_ge(s["c_done"], L * STATE_TILES + m - 1)
                        for i, tw in enumerate((tw_re, tw_im)):
                            TT(prod[:, m % 2, i, :, :], ys[:, m % 2, :, :], rep(tw[:, j, :], 2), MUL)
                        pool.drain()
                        TT(prod[:, m % 2, 0, 0, :], prod[:, m % 2, 0, 0, :], prod[:, m % 2, 1, 1, :], SUB)
                        TT(prod[:, m % 2, 0, 1, :], prod[:, m % 2, 0, 1, :], prod[:, m % 2, 1, 0, :], ADD)
                        pool.drain().then_inc(s["prod_ready"], 1)
                rms_power(L, 0)
                rms_power(L, 1)
                power(L, 1)
                update_x(L, 1)
                power(L, 2)
                pool.wait_ge(s["x_ready"], L * NT + 2 * NT)
                pool.sem_inc(s["gb_used"], 1)

        @block.scalar
        def _(act):
            def hi_unit(L, n, k, p, cols=512):
                act.wait_ge(a_loaded[p // 2], L * (A_GROUPS * 32) + n * 32 + (k + 1) * 32)
                act.wait_ge(a_used, L * A_ALL + n * A_UNITS + (k * A_UNITS + p + 1))
                act.activation(hi_a[:, 2 * p:2 * p + 2, 0:cols], raw_a[:, 2 * p:2 * p + 2, 0:cols], ACT.Copy).then_inc(a_hi, 1)

            def hi_b_unit(L, m, k, u):
                act.wait_ge(b_loaded[u], L * (B_GROUPS * 16) + m * 16 + (k + 1) * 16)
                act.wait_ge(b_used, L * B_ALL + m * B_UNITS + (k * B_UNITS + u + 1))
                act.activation(hi_b[:, u, :], raw_b[:, u, :], ACT.Copy).then_inc(b_hi, 1)

            def copy_out(bank, dst, turned, count, done):
                act.wait_ge(s[turned], count)
                act.activation(dst, bank, ACT.Copy).then_inc(s[done], 1)

            def parameters(L):
                act.wait_ge(s["lam_in"], L + 1)
                act.activation(lams[:, :], lams[:, :], ACT.Exp).then_inc(s["lam_exp"], 1)
                act.wait_ge(s["prm_out"], L + 1)
                act.activation(small[:, 0, :], prmT[:, R_DT:R_DT + 8], ACT.Exp).then_inc(s["dt_exp"], 1)
                act.wait_ge(s["sin_in"], L + 1)
                act.activation(lp[:, Q_MAG, :], lp[:, Q_MAG, :], ACT.Exp)
                act.activation(lp[:, Q_SIN, :], small[:, 1, :], ACT.Sin)
                act.activation(lp[:, Q_COS, :], small[:, 1, :], ACT.Sin, scale=0.5).then_inc(s["sin_out"], 1)

            def ffn(L, a0, b0, f, following):
                base = f * CHUNKS

                def hidden(c, k):
                    act.wait_ge(a_used, L * A_ALL + c * A_UNITS + (A_UNITS + (a0 + k) * A_UNITS + A_UNITS))
                    act.wait_ge(s["h_turned"], L * 2 * CHUNKS + c + (base + k))
                    for t in range(NT):
                        act.activation(h[:, t, :], ps[:, GU + t, 0:CHUNK], ACT.Silu).then_inc(s["gate_act"], 1)

                def hidden_hi(c, k, dst=hT_hi[:, :, :]):
                    act.wait_ge(s["h_turned"], L * 2 * CHUNKS + c + (base + k + 1))
                    act.activation(dst.rearrange("p a t -> p (a t)"), ps[:, TR, :],
                                   ACT.Copy).then_inc(s["hT_hi_ready"], 1)

                for p in range(3):
                    hi_unit(L, 0, a0 + 1, p)
                hidden(0, 0)
                if not f:
                    copy_out(ps[:, ACC, :], pT_hi[:, :, :].rearrange("p a t -> p (a t)"), "p_turned", L + 1, "pT_hi_ready")
                hi_unit(L, 0, a0 + 1, 3)
                for u in range(2):
                    hi_b_unit(L, 0, b0, u)
                if not f:
                    parameters(L)
                with act.Fori(1, CHUNKS - 1) as c:
                    hi_unit(L, c, a0 + 1, 0)
                    hidden_hi(c, -1)
                    hi_unit(L, c, a0 + 1, 1)
                    hi_unit(L, c, a0 + 1, 2)
                    hidden(c, 0)
                    hi_unit(L, c, a0 + 1, 3)
                    for u in range(2):
                        hi_b_unit(L, c, b0, u)
                c = CHUNKS - 1
                if following:
                    hi_unit(L, 0, a0 + c + 1, 0)
                hidden_hi(0, c - 1)
                if following:
                    hi_unit(L, 0, a0 + c + 1, 1)
                    hi_unit(L, 0, a0 + c + 1, 2)
                hidden(0, c)
                if following:
                    hi_unit(L, 0, a0 + c + 1, 3)
                hidden_hi(0, c, actT_hi[:, 0:2, :])
                for u in range(2):
                    hi_b_unit(L, 0, b0 + c, u)

            def normalise(L, k):
                act.wait_ge(s["shift_ready"], L * 2 + k + 1)
                act.activation(z[:, 0, :], z[:, 0, :], ACT.Identity, bias=shift[:, 1:2],
                               scale=rstd[:, 0:1]).then_inc(s["z0_ready"], 1)

            def norm_turned(L, k, g, b):
                def scaled(i):
                    act.wait_ge(s["turned"], L * 12 + 4 * (k + 1) + i + 1)
                    for kk in range(2):
                        c = 2 * i + kk
                        ins = act.activation(lnT[:, c, :], ps[:, LN_BANKS[i], kk * SEQ:(kk + 1) * SEQ], ACT.Identity,
                                             bias=lp[:, b, c:c + 1], scale=lp[:, g, c:c + 1])
                    ins.then_inc(s["lnT_act"], 1)

                for i in range(4):
                    if i < 2:
                        act.wait_ge(s["lnT_scaled"], L * 4 + 2 * k + i + 1)
                    else:
                        act.wait_ge(s["lnT_act"], L * 4 + 2 * k + i - 1)
                    act.activation(actT_hi[:, 2 * i:2 * i + 2, :], lnT[:, 2 * i:2 * i + 2, :],
                                   ACT.Copy).then_inc(s["actT_hi_ready"], 1)
                    if i + 2 < 4:
                        scaled(i + 2)

            with act.Fori(0, DEPTH) as L:
                for p in range(2):
                    hi_unit(L, 0, A_FFN1, p)
                for i in range(4):
                    act.wait_ge(s["turned"], L * 12 + i + 1)
                    act.activation(actT_hi[:, 2 * i:2 * i + 2, :].rearrange("p k t -> p (k t)"),
                                   ps[:, LN_BANKS[i], :], ACT.Copy).then_inc(s["actT_hi_ready"], 1)
                for p in range(2, 4):
                    hi_unit(L, 0, A_FFN1, p)
                act.activation(junk[:, 0:1], x[:, 0, 0:1], ACT.Silu)
                ffn(L, A_FFN1, B_FFN1, 0, True)
                act.wait_ge(s["bc_turned"], L * 2 + 1)
                act.activation(inT[:, :, :, :].rearrange("p a r c -> p (a r c)"), ps[:, MISC, :],
                               ACT.Copy).then_inc(s["in_out"], 1)
                act.wait_ge(s["bc_turned"], L * 2 + 2)
                cT = ps[:, TR, :].rearrange("p (r j c) -> p r j c", r=2, c=32)
                for i, sign in enumerate((1.0, -1.0)):
                    ins = act.activation(outT[:, :, i, :], cT[:, i, :, :], ACT.Copy, scale=sign)
                ins.then_inc(s["c_out"], 1)
                normalise(L, 0)
                norm_turned(L, 0, Q_G1, Q_B1)
                def bu_out(n):
                    if n >= 2:
                        act.wait_ge(s["bu_used"], L * STATE_TILES + n - 1)
                    copy_out(ps[:, 6, :], bu_sb[:, n % 2, :, :].rearrange("p c t -> p (c t)"),
                             "bu_done", L * STATE_TILES + n + 1, "bu_out")

                def qk_out(n):
                    dst = (kT, qT)[n // 2][:, 2 * (n % 2):2 * (n % 2) + 2, :].rearrange("p a t -> p (a t)")
                    copy_out(ps[:, n % 2, :], dst, "qk_turned", L * 4 + n + 1, "qk_out")

                def w_in_middle(i):
                    ix = L * 5 + 1
                    if i == 1:
                        copy_out(ps[:, 6, :], iqT[:, :, :].rearrange("p a t -> p (a t)"), "ix_turned", ix, "ix_out")
                        copy_out(ps[:, 7, 0:SEQ], ksT[:, 0, :], "ix_turned", ix + 1, "ix_out")
                    if i == 2:
                        copy_out(ps[:, 6, :], saqT[:, :, :].rearrange("p a t -> p (a t)"), "ix_turned", ix + 2, "ix_out")
                        copy_out(ps[:, 7, 0:SEQ], ksT[:, 1, :], "ix_turned", ix + 3, "ix_out")
                        copy_out(ps[:, 7, SEQ:2 * SEQ], uT[:, 1, :], "ix_turned", ix + 3, "ix_out")
                    if i == 3:
                        copy_out(ps[:, 7, 0:SEQ], uT[:, 0, :], "ix_turned", ix + 4, "ix_out")
                        bu_out(1)
                    if i == 4:
                        bu_out(3)
                    if i == 5:
                        qk_out(0)
                        qk_out(1)
                        bu_out(5)

                for i in range(WIN_GROUPS):
                    cols = WIN_COLS if i + 1 < WIN_GROUPS else 512
                    hi_unit(L, 0, A_WIN + i + 1, 0, cols)
                    hi_unit(L, 0, A_WIN + i + 1, 1, cols)
                    w_in_middle(i)
                    hi_unit(L, 0, A_WIN + i + 1, 2, cols)
                    c0 = (WIN_GROUPS - 1 - i) * WIN_COLS
                    if i == 0:
                        act.wait_ge(s["actT_ready"], L * 16 + 8)
                    act.wait_ge(s["win_done"], L * WIN_GROUPS + i + 1)
                    for t in range(NT):
                        ins = act.activation(hp[:, t, c0:c0 + WIN_COLS], ps[:, 2 * (i % 2) + t, 0:WIN_COLS], ACT.Copy)
                    ins.then_inc(s["hp_ready"], 1)
                    hi_unit(L, 0, A_WIN + i + 1, 3, cols)
                    if 2 <= i <= 4:
                        bu_out(2 * i - 4)
                qk_out(2)
                qk_out(3)
                bu_out(6)

                def mix_hi(n, bank, scale=1.0):
                    act.wait_ge(s["mix_turned"], L * 3 + n + 1)
                    act.activation(actT_hi[:, 2 * n:2 * n + 2, :].rearrange("p k t -> p (k t)"), ps[:, bank, :],
                                   ACT.Copy, scale=scale).then_inc(s["mixT_hi"], 1)

                sub = lp[:, Q_MISC, M_SUB:M_SUB + 1]
                for i in range(UNITS + 3):
                    if i < UNITS:
                        N = P * (i % 2 + 1)
                        act.wait_ge(s["da_max"], L * UNITS + i + 1)
                        for c in range(2):
                            ins = act.activation(da_e[:, i % 2, c, 0:N], da_e[:, i % 2, c, 0:N], ACT.Exp,
                                                 bias=da_nm[:, i % 2, c:c + 1], accum_out=da_sum[:, i, c:c + 1])
                        ins.then_inc(s["da_exp"], 1)
                    if 0 <= i - 2 < UNITS:
                        u = i - 2
                        act.wait_ge(s["da_turned"], L * UNITS + u + 1)
                        act.activation(aT[:, u % 2, 0:P * (u % 2 + 1)], ps[:, 4, 0:P * (u % 2 + 1)],
                                       ACT.Copy).then_inc(s["da_aT"], 1)
                    if i >= 3:
                        u = i - 3
                        hd, qb = u // 2, u % 2
                        act.wait_ge(s["da_o"], L * UNITS + u + 1)
                        act.activation(hp[:, qb, hd * DA_V:(hd + 1) * DA_V], ps[:, 5, 0:P], ACT.Copy)
                        act.activation(junk, ps[:, 5, 0:P], ACT.Square,
                                       accum_out=ss[:, qb, hd:hd + 1]).then_inc(s["da_o_out"], 1)
                    if i in BU_LATE:
                        bu_out(BU_LATE[i])
                    if i - 1 in SA_SCORES:
                        qb = SA_SCORES[i - 1]
                        N = P * (qb + 1)
                        act.wait_ge(s["sa_max"], L * 2 + (1 - qb) + 1)
                        for hd in range(SA_HEADS):
                            ins = act.activation(sa_e[:, hd, 0:N], sa_e[:, hd, 0:N], ACT.Exp,
                                                 bias=sa_nm[:, qb, hd:hd + 1], accum_out=sa_sum[:, qb, hd:hd + 1])
                        ins.then_inc(s["sa_exp"], 1)
                    if i in SA_TURN:
                        w = 2 * P * (SA_TURN[i] + 1)
                        for half in range(2):
                            act.wait_ge(s["sa_turned"], L * 4 + 2 * (1 - SA_TURN[i]) + half + 1)
                            act.activation(sa_aT[:, half * 512:half * 512 + w], ps[:, 2 + half, 0:w],
                                           ACT.Copy).then_inc(s["sa_aT_ready"], 1)
                act.wait_ge(s["y_full"], L + 1)
                act.activation(ys2[:, 1, :, :], ys2[:, 0, :, :], ACT.Gelu_apprx_tanh).then_inc(s["gelu_done"], 1)
                mix_hi(0, 0, sub)
                mix_hi(1, 1)
                act.wait_ge(s["glu_done"], L + 1)
                act.activation(ysg.rearrange("p a t -> p (a t)"), ps[:, 6, :], ACT.Sigmoid).then_inc(s["glu_act"], 1)
                mix_hi(2, 0, sub)
                act.wait_ge(s["ssm_out"], L + 1)
                act.activation(actT_hi[:, 6:8, :], ysg, ACT.Copy).then_inc(s["mixT_hi"], 1)
                for p in range(4):
                    hi_unit(L, 0, A_WO + 1, p)
                for u in range(2):
                    hi_b_unit(L, 0, B_PROJ, u)
                for p in range(2):
                    hi_unit(L, 0, A_GATE, p)
                normalise(L, 1)
                for p in range(2, 4):
                    hi_unit(L, 0, A_GATE, p)
                norm_turned(L, 1, Q_G2, Q_B2)
                for i in range(2):
                    for p in range(4):
                        hi_unit(L, 0, A_GATE + i + 1, p)
                    act.wait_ge(s["gate_done"], L * 2 + i + 1)
                    act.wait_ge(s["x_updated"], L * 2 + 2)
                    for t in range(NT):
                        act.activation(z[:, t, i * 512:(i + 1) * 512], ps[:, (GU, TR)[i] + t, :],
                                       ACT.Sigmoid).then_inc(s["gate_sig"], 1)
                ffn(L, A_FFN2, B_FFN2, 1, False)

        @block.vector
        def _(dve):
            TT, TS, STT = dve.tensor_tensor, dve.tensor_scalar, dve.scalar_tensor_tensor
            MUL, ADD, SUB, MAX = ALU.mult, ALU.add, ALU.subtract, ALU.max

            def flat(t):
                return t.rearrange("p a t -> p (a t)")

            def lo_unit(L, n, k, p, cols=512):
                dve.wait_ge(a_hi, L * A_ALL + n * A_UNITS + (k * A_UNITS + p + 1))
                q = slice(2 * p, 2 * p + 2)
                TT(lo_a[:, q, 0:cols], raw_a[:, q, 0:cols], hi_a[:, q, 0:cols].bitcast(F32), SUB).then_inc(a_lo, 1)

            def lo_b_unit(L, m, k, u):
                dve.wait_ge(b_hi, L * B_ALL + m * B_UNITS + (k * B_UNITS + u + 1))
                TT(lo_b[:, u, :], raw_b[:, u, :], hi_b[:, u, :].bitcast(F32), SUB).then_inc(b_lo, 1)

            re, im = prmT[:, R_RE:R_RE + 8], prmT[:, R_IM:R_IM + 8]
            sm = [small[:, i, :] for i in range(8)]

            def parameters_in(L):
                dve.wait_ge(s["lamv_loaded"], L * 64 + 64)
                for i in range(2):
                    TT(lamv[:, 2 * i, :], lamv[:, 2 * i, :], lamv[:, 2 * i + 1, :], MUL)
                dve.memset(lp[:, Q_MISC, :], 0.0)
                dve.drain()
                dve.tensor_reduce(lams[:, 0:1], lamv[:, 0, :], AX.X, ADD)
                dve.tensor_reduce(lams[:, 1:2], lamv[:, 2, :], AX.X, ADD).then_inc(s["lam_in"], 1)
                dve.tensor_copy(lp[:, Q_G1:Q_B2 + 1, :], prmT[:, R_G1:R_B2 + 8].rearrange("p (q k) -> p q k", k=8))
                dve.tensor_copy(lp[:, Q_MISC, M_D:M_D + 2], prmT[:, R_D:R_D + 2])

            def parameters(L):
                dve.wait_ge(s["dt_exp"], L + 1)
                TT(lp[:, Q_MAG, :], re, sm[0], MUL)
                TT(sm[1], im, sm[0], MUL)
                dve.wait_ge(s["lam_exp"], L + 1)
                TT(lams[:, 0:1], lams[:, 1:2], lams[:, 0:1], SUB)
                dve.drain()
                TT(lp[:, Q_MISC, M_NLAM:M_NLAM + 1], lams[:, 0:1],
                   lam_consts[:, 0, bass.ds(L, 1)], SUB)
                TT(lp[:, Q_MISC, M_SUB:M_SUB + 1], prmT[:, R_SUB:R_SUB + 1],
                   lam_consts[:, 1, bass.ds(L, 1)], MUL)
                TS(sm[2], sm[1], 1 / TWO_PI, ROUND, MUL, ADD)
                dve.drain()
                TS(sm[2], sm[2], ROUND, None, SUB)
                for part in (PI_A, PI_B, PI_C):
                    dve.drain()
                    STT(sm[1], sm[2], -part, sm[1], MUL, ADD)
                dve.drain()
                TS(sm[1], sm[1], 3.1415925, -3.1415925, ALU.min, MAX)
                TT(sm[3], re, re, MUL)
                TT(sm[4], im, im, MUL)
                dve.drain().then_inc(s["sin_in"], 1)
                TT(sm[3], sm[3], sm[4], ADD)
                dve.drain()
                dve.reciprocal(sm[3], sm[3])
                dve.wait_ge(s["sin_out"], L + 1)
                mag, cos, sin = lp[:, Q_MAG, :], lp[:, Q_COS, :], lp[:, Q_SIN, :]
                TT(cos, cos, cos, MUL)
                TT(sm[4], mag, sin, MUL)
                dve.drain()
                TS(cos, cos, -2.0, 1.0, MUL, ADD)
                dve.drain()
                TT(sm[5], mag, cos, MUL)
                dve.drain()
                TS(sm[5], sm[5], -1.0, None, ADD)
                dve.drain()
                TT(sm[0], sm[5], re, MUL)
                TT(sm[1], sm[4], im, MUL)
                TT(sm[6], sm[4], re, MUL)
                TT(sm[7], sm[5], im, MUL)
                dve.drain()
                TT(sm[0], sm[0], sm[1], ADD)
                TT(sm[6], sm[6], sm[7], SUB)
                dve.drain()
                TT(lp[:, Q_FRE, :], sm[0], sm[3], MUL)
                TT(lp[:, Q_FIM, :], sm[6], sm[3], MUL)
                dve.drain().then_inc(s["lp_ready"], 1)

            def ffn(L, a0, b0, f, following):
                base = f * CHUNKS

                def hidden(c, k):
                    for t in range(NT):
                        dve.wait_ge(s["gate_act"], L * 4 * CHUNKS + c * 2 + (2 * (base + k) + t + 1))
                        TT(h[:, t, :], h[:, t, :], ps[:, GU + t, CHUNK:2 * CHUNK], MUL).then_inc(s["h_ready"], 1)

                def hidden_lo(c, k, hi=hT_hi[:, :, :], lo=hT_lo[:, :, :]):
                    dve.wait_ge(s["hT_hi_ready"], L * 2 * CHUNKS + c + (base + k + 1))
                    TT(flat(lo), ps[:, TR, :], flat(hi).bitcast(F32), SUB).then_inc(s["hT_ready"], 1)

                for p in range(3):
                    lo_unit(L, 0, a0 + 1, p)
                hidden(0, 0)
                if not f:
                    dve.wait_ge(s["rows_turned"], L + 1)
                    dve.tensor_copy(prmT[:, :], ps[:, ACC + 1, 0:ROWS]).then_inc(s["prm_out"], 1)
                    dve.wait_ge(s["pT_hi_ready"], L + 1)
                    TT(flat(pT_lo[:, :, :]), ps[:, ACC, :], flat(pT_hi[:, :, :]).bitcast(F32), SUB)\
                        .then_inc(s["pT_ready"], 1)
                    parameters_in(L)
                lo_unit(L, 0, a0 + 1, 3)
                for u in range(2):
                    lo_b_unit(L, 0, b0, u)
                if not f:
                    parameters(L)
                with dve.Fori(1, CHUNKS - 1) as c:
                    lo_unit(L, c, a0 + 1, 0)
                    hidden_lo(c, -1)
                    lo_unit(L, c, a0 + 1, 1)
                    lo_unit(L, c, a0 + 1, 2)
                    hidden(c, 0)
                    lo_unit(L, c, a0 + 1, 3)
                    for u in range(2):
                        lo_b_unit(L, c, b0, u)
                c = CHUNKS - 1
                if following:
                    lo_unit(L, 0, a0 + c + 1, 0)
                hidden_lo(0, c - 1)
                if following:
                    lo_unit(L, 0, a0 + c + 1, 1)
                    lo_unit(L, 0, a0 + c + 1, 2)
                hidden(0, c)
                if following:
                    lo_unit(L, 0, a0 + c + 1, 3)
                hidden_lo(0, c, actT_hi[:, 0:2, :], actT_lo[:, 0:2, :])
                for u in range(2):
                    lo_b_unit(L, 0, b0 + c, u)

            def residual(L, k, t, coef, eps):
                for half in range(2):
                    dve.wait_ge(s["ffn_done"], L * 12 + 4 * k + 2 * t + half + 1)
                    q = slice(512 * half, 512 * half + 512)
                    STT(z[:, t, q], x[:, t, q], coef, ps[:, ACC + 2 * t + half, :], MUL, ADD)
                dve.drain().then_inc(s["acc_read"], 1)
                for half in range(2):
                    dve.bn_stats(stats[:, t, half, :], z[:, t, 512 * half:512 * half + 512])
                dve.drain()
                dve.bn_aggr(mv[:, t, :], stats[:, t, :, :].rearrange("p a b -> p (a b)"))
                dve.drain()
                if t == 0:
                    TS(shift[:, 0:1], mv[:, 0, 0:1], -1.0, None, MUL)
                TS(var[:, t:t + 1], mv[:, t, 1:2], eps, None, ADD).then_inc(s["var_ready"], 1)

            def norm(L, k, coef, eps):
                for t in range(NT):
                    residual(L, k, t, coef, eps)
                dve.wait_ge(s["rs_ready"], L * 6 + 2 * k + 2)
                TS(z[:, 1, :], z[:, 1, :], mv[:, 1, 0:1], rstd[:, 1:2], SUB, MUL).then_inc(s["z1_ready"], 1)

            def last_norm(L):
                for t in range(NT):
                    residual(L, 2, t, 2.0, 4 * LN_EPS)
                    if t == 0:
                        dve.wait_ge(s["gb_loaded"], L * 96 + 96)
                    STT(z[:, t, :], z[:, t, :], mv[:, t, 0:1], gb[:, 0, :], SUB, MUL)
                dve.drain()
                for t in range(NT):
                    dve.wait_ge(s["rs_ready"], L * 6 + 5 + t)
                    STT(x[:, t, :], z[:, t, :], rstd[:, t:t + 1], gb[:, 1, :], MUL, ADD)\
                        .then_inc(s["x_ready"], 1)

            def norm_turned(L, k, g, b):
                for i in (0, 1):
                    dve.wait_ge(s["turned"], L * 12 + 4 * (k + 1) + i + 1)
                    for kk in range(2):
                        c = 2 * i + kk
                        ins = TS(lnT[:, c, :], ps[:, LN_BANKS[i], kk * SEQ:(kk + 1) * SEQ],
                                 lp[:, g, c:c + 1], lp[:, b, c:c + 1], MUL, ADD)
                    ins.then_inc(s["lnT_scaled"], 1)
                base = (4, 8)[k]
                for i in range(4):
                    dve.wait_ge(s["actT_hi_ready"], L * 12 + base + i + 1)
                    q = slice(2 * i, 2 * i + 2)
                    TT(actT_lo[:, q, :], lnT[:, q, :], actT_hi[:, q, :].bitcast(F32), SUB).then_inc(s["actT_ready"], 1)

            dve.sem_inc(a_lo, A_UNITS)
            dve.sem_inc(b_lo, B_UNITS)
            dve.sem_inc(s["x_ready"], NT)
            dve.wait_ge(s["ident_set"], 1)
            dve.tensor_reduce(parity[:, :], ident[:, :].rearrange("p (g q d) -> p q g d", q=2, d=SSM_GROUP),
                              AX.XY, ADD)
            dve.wait_ge(s["causal_set"], 1)
            dve.wait_ge(s["table_turned"], 1)
            dve.tensor_copy(z[0:N_ATT, 0, 0:3 * P], ps[0:N_ATT, 5, 0:3 * P]).then_inc(s["table_out"], 1)

            with dve.Fori(0, DEPTH) as L:
                for p in range(2):
                    lo_unit(L, 0, A_FFN1, p)
                for i in range(4):
                    dve.wait_ge(s["actT_hi_ready"], L * 12 + i + 1)
                    q = slice(2 * i, 2 * i + 2)
                    TT(flat(actT_lo[:, q, :]), ps[:, LN_BANKS[i], :], flat(actT_hi[:, q, :]).bitcast(F32),
                       SUB).then_inc(s["actT_ready"], 1)
                for p in range(2, 4):
                    lo_unit(L, 0, A_FFN1, p)
                dve.wait_ge(s["dtrow_loaded"], L * 16 + 16)
                dve.tensor_copy(rows[R_DT:R_DT + 8, :].rearrange("p (g q) -> p g q", g=2),
                                bc(dt_row[R_DT:R_DT + 8, :], SSM_STATE)).then_inc(s["dt_expanded"], 1)
                ffn(L, A_FFN1, B_FFN1, 0, True)
                dve.wait_ge(s["twiddles"], L + 1)
                norm(L, 0, 2 * ALPHA, 4 * LN_EPS)
                norm_turned(L, 0, Q_G1, Q_B1)

                def index_round(n):
                    qb, half = 1 - n // 2, n % 2
                    N = P * (qb + 1)
                    dve.wait_ge(s["ixs_done"], L * 4 + n + 1)
                    q = slice(4 * half, 4 * half + 4)
                    STT(relu_w[:, q, 0:N], ps[:, 4:6, :].rearrange("p b (h t) -> p (b h) t", h=2)[:, :, 0:N], 0.0,
                        bc(wis[:, qb, q], N), MAX, MUL)
                    dve.drain().then_inc(s["ixs_read"], 1)
                    if half:
                        dve.tensor_reduce(isc[:, qb, 0:N], relu_w[:, :, 0:N].rearrange("p h s -> p s h"), AX.X, ADD)
                        dve.drain()
                        TT(isc[:, qb, 0:N], isc[:, qb, 0:N], causal[:, SEQ - N:SEQ], ADD)

                def strike_out(times):
                    for _ in range(times):
                        dve.drain()
                        for qb in range(NT):
                            N = P * (qb + 1)
                            dve.max(top8[:, qb, :], isc[:, qb, 0:N])
                        dve.drain()
                        for qb in range(NT):
                            N = P * (qb + 1)
                            dve.match_replace(isc[:, qb, 0:N], top8[:, qb, :], isc[:, qb, 0:N], TAKEN)

                def scan(n):
                    dve.wait_ge(s["derot_ready"], L * STATE_TILES + n + 1)
                    if n >= 2:
                        dve.wait_ge(s["prod_ready"], L * STATE_TILES + n - 1)
                    j = TILE_ORDER[n]
                    for c in range(2):
                        dve.tensor_tensor_scan(ys[:, n % 2, c, :], lp[:, Q_MAG, j:j + 1].broadcast_to([P, SEQ]),
                                               derot[:, c, :], 0.0, MUL, ADD)
                    dve.drain().then_inc(s["y_ready"], 1)

                for i in range(WIN_GROUPS):
                    for p in range(4):
                        lo_unit(L, 0, A_WIN + i + 1, p, WIN_COLS if i + 1 < WIN_GROUPS else 512)
                        if i == 3 and p == 1:
                            index_round(2)
                            scan(0)
                        if i == 5 and p == 1:
                            scan(3)
                        if i >= 4 and p < 3:
                            strike_out(1)
                    if i == 0:
                        dve.wait_ge(s["hp_ready"], L * WIN_GROUPS + 1)
                        dve.tensor_copy(kdup[:, :, 0:P].rearrange("p t (r d) -> p t r d", r=4),
                                        hp[:, :, C_IK:C_IK + 32].unsqueeze(2).broadcast_to([P, NT, 4, 32]))
                        for t in range(NT):
                            TS(wis[:, t, :].rearrange("p (b h) -> p b h", h=2),
                               hp[:, t, C_IW:C_IW + 8].rearrange("p (h b) -> p b h", h=2),
                               IDX_HEADS ** -0.5 * IDX_DIM ** -0.5, None, MUL)
                        dve.drain().then_inc(s["kdup_ready"], 1)
                    if i == 1:
                        dve.wait_ge(s["hp_ready"], L * WIN_GROUPS + 2)
                        dve.tensor_copy(kdup[:, :, P:2 * P].rearrange("p t (r d) -> p t r d", r=2),
                                        hp[:, :, C_SK:C_SK + 64].unsqueeze(2).broadcast_to([P, NT, 2, 64]))
                        dve.drain().then_inc(s["kdup_ready"], 1)
                        index_round(0)
                    if i == 2:
                        index_round(1)
                    if i == 3:
                        index_round(3)
                        scan(1)
                        strike_out(TOPK // 8 - 7)
                    if i == 4:
                        scan(2)
                    if i == 5:
                        scan(4)

                dve.wait_ge(s["bias_ready"], 1)

                def rms_scaled(pair):
                    dve.wait_ge(s["da_o_out"], L * UNITS + 4 * pair + 4)
                    q = slice(2 * pair, 2 * pair + 2)
                    TS(ss[:, :, q], ss[:, :, q], 1.0 / DA_V, LN_EPS, MUL, ADD).then_inc(s["ss_scaled"], 1)

                def normalise_heads(pair):
                    dve.wait_ge(s["rms_ready"], L * 2 + pair + 1)
                    for t in range(NT):
                        m = hp[:, t, 2 * pair * DA_V:(2 * pair + 2) * DA_V].rearrange("p (h e) -> p h e", h=2)
                        TT(m, m, bc(rms[:, t, 2 * pair:2 * pair + 2], DA_V), MUL)
                    dve.drain().then_inc(s["mix_da"], 1)

                for i in range(UNITS + 3):
                    if i in SA_SCALE:
                        qb = SA_SCALE[i]
                        dve.reciprocal(sa_sum[:, qb, :], sa_sum[:, qb, :])
                        dve.drain()
                        dve.wait_ge(s["sa_o"], L * 2 + (1 - qb) + 1)
                        TT(hp[:, qb, 768:1024].rearrange("p (h e) -> p h e", h=SA_HEADS),
                           ps[:, 2, 0:256].rearrange("p (h e) -> p h e", h=SA_HEADS), bc(sa_sum[:, qb, :], SA_DIM),
                           MUL).then_inc(s["mix_sa"], 1)
                    if i < UNITS:
                        hd, qb = i // 2, i % 2
                        N = P * (qb + 1)
                        dve.wait_ge(s["das_done"], L * UNITS + i + 1)
                        if i >= 2:
                            dve.wait_ge(s["da_turned"], L * UNITS + i - 1)
                        STT(da_e[:, i % 2, :, 0:N], ps[:, 0:2, 0:N],
                            DA_QK ** -0.5, rep(bias[:, hd, SEQ - N:SEQ], 2), MUL, ADD)
                        dve.drain().then_inc(s["das_read"], 1)
                        dve.tensor_reduce(da_nm[:, i % 2, :], da_e[:, i % 2, :, 0:N], AX.X, MAX,
                                          negate=True).then_inc(s["da_max"], 1)
                        if i == 0:
                            strike_out(1)
                            dve.drain()
                            for t in range(NT):
                                w = P * (t + 1)
                                TS(sel[:, t, 0:w], isc[:, t, 0:w], TAKEN, NEG, ALU.not_equal, MUL)
                            dve.drain()
                    if 1 <= i <= UNITS:
                        u = i - 1
                        N = P * (u % 2 + 1)
                        dve.wait_ge(s["da_exp"], L * UNITS + u + 1)
                        dve.reciprocal(da_r[:, u, :], da_sum[:, u, :])
                        dve.drain()
                        TT(da_r[:, u, 1:2], da_r[:, u, 1:2], lp[:, Q_MISC, M_NLAM:M_NLAM + 1], MUL)
                        TS(da_e[:, u % 2, 0, 0:N], da_e[:, u % 2, 0, 0:N], da_r[:, u, 0:1], None, MUL)
                        dve.drain()
                        STT(da_e[:, u % 2, 0, 0:N], da_e[:, u % 2, 1, 0:N], da_r[:, u, 1:2],
                            da_e[:, u % 2, 0, 0:N], MUL, ADD)
                        dve.drain().then_inc(s["da_a"], 1)
                    if i in SCAN_LATE:
                        scan(SCAN_LATE[i])
                    if i in SA_SCORES:
                        qb = SA_SCORES[i]
                        N = P * (qb + 1)
                        dve.wait_ge(s["sas_done"], L * 2 + (1 - qb) + 1)
                        for b in range(2):
                            STT(sa_e[:, b::2, 0:N], ps[:, 2 + b, :].rearrange("p (h t) -> p h t", h=2)[:, :, 0:N],
                                SA_DIM ** -0.5, bias[:, DA_HEADS + b::2, SEQ - N:SEQ], MUL, ADD)
                        dve.drain().then_inc(s["sas_read"], 1)
                        TT(sa_e[:, :, 0:N], sa_e[:, :, 0:N], rep(sel[:, qb, 0:N], SA_HEADS), ADD)
                        dve.drain()
                        dve.tensor_reduce(sa_nm[:, qb, :], sa_e[:, :, 0:N], AX.X, MAX,
                                          negate=True).then_inc(s["sa_max"], 1)
                    if i == 8:
                        rms_scaled(0)
                    if i == 9:
                        normalise_heads(0)
                        dve.wait_ge(s["c_done"], L * STATE_TILES + STATE_TILES)
                        for t in range(2):
                            ins = STT(ys2[:, 0, t, :], uT[:, t, :], lp[:, Q_MISC, M_D + t:M_D + t + 1],
                                      ps[:, 7, t * SEQ:(t + 1) * SEQ], MUL, ADD)
                        ins.then_inc(s["y_full"], 1)

                def mix_lo(n, bank, scaled):
                    dve.wait_ge(s["mixT_hi"], L * 4 + n + 1)
                    q = slice(2 * n, 2 * n + 2)
                    hi = flat(actT_hi[:, q, :]).bitcast(F32)
                    if scaled:
                        ins = STT(flat(actT_lo[:, q, :]), ps[:, bank, :], lp[:, Q_MISC, M_SUB:M_SUB + 1], hi, MUL, SUB)
                    else:
                        ins = TT(flat(actT_lo[:, q, :]), ps[:, bank, :], hi, SUB)
                    ins.then_inc(s["actT_ready"], 1)

                rms_scaled(1)
                mix_lo(0, 0, True)
                normalise_heads(1)
                mix_lo(1, 1, False)
                dve.wait_ge(s["glu_act"], L + 1)
                TT(ysg, ysg, ys2[:, 1, :, :], MUL).then_inc(s["ssm_out"], 1)
                mix_lo(2, 0, True)
                dve.wait_ge(s["mixT_hi"], L * 4 + 4)
                TT(actT_lo[:, 6:8, :], ysg, actT_hi[:, 6:8, :].bitcast(F32), SUB).then_inc(s["actT_ready"], 1)
                for p in range(4):
                    lo_unit(L, 0, A_WO + 1, p)
                for u in range(2):
                    lo_b_unit(L, 0, B_PROJ, u)
                norm(L, 1, ALPHA, LN_EPS)
                for p in range(2):
                    lo_unit(L, 0, A_GATE, p)
                norm_turned(L, 1, Q_G2, Q_B2)
                for p in range(2, 4):
                    lo_unit(L, 0, A_GATE, p)
                for i in range(2):
                    for p in range(4):
                        lo_unit(L, 0, A_GATE + i + 1, p)
                    for t in range(NT):
                        q = slice(512 * i, 512 * i + 512)
                        dve.wait_ge(s["gate_sig"], L * 4 + 2 * i + t + 1)
                        if i == 0 and t == 0:
                            dve.wait_ge(s["proj_done"], L * 4 + 4)
                        TT(z[:, t, q], z[:, t, q], ps[:, ACC + 2 * t + i, :], MUL)
                        dve.drain()
                        STT(x[:, t, q], x[:, t, q], ALPHA, z[:, t, q], MUL, ADD).then_inc(s["ple_done"], 1)
                ffn(L, A_FFN2, B_FFN2, 1, False)
                last_norm(L)

        @block.tensor
        def _(pe):
            def turn(out, src):
                return pe.transpose(out, src, ident[:, :])

            def wait_a(L, n, k, p):
                pe.wait_ge(a_lo, L * A_ALL + n * A_UNITS + (A_UNITS + k * A_UNITS + p + 1))

            def group(L, n, k, bank, cols, middle=None, acts=None):
                for p in range(A_UNITS):
                    wait_a(L, n, k, p)
                    if acts is not None:
                        wait_act(L, acts + max(p + 1, 2))
                    for kt in (2 * p, 2 * p + 1):
                        for t in range(NT):
                            q = slice(t * P, (t + 1) * P)
                            ins = mm3(pe, ps[:, bank + t, 0:cols], actT_hi[:, kt, q], actT_lo[:, kt, q],
                                      hi_a[:, kt, 0:cols], lo_a[:, kt, 0:cols], kt == 0, kt == KT - 1)
                    ins.then_inc(a_used, 1)
                    if p == 1 and middle:
                        middle()

            def rows2(L, m, k, hi, lo, first, last, done=None, middle=None):
                for u in range(B_UNITS):
                    pe.wait_ge(b_lo, L * B_ALL + m * B_UNITS + (B_UNITS + k * B_UNITS + u + 1))
                    final = last and u == B_UNITS - 1
                    for t in range(NT):
                        for half in range(2):
                            q, w = slice(t * P, (t + 1) * P), slice(half * 512, half * 512 + 512)
                            ins = mm3(pe, ps[:, ACC + 2 * t + half, :], hi[:, u, q], lo[:, u, q],
                                      hi_b[:, u, w], lo_b[:, u, w], first and u == 0, final)
                            if final:
                                ins.then_inc(s[done], 1)
                    if not last:
                        ins.then_inc(b_used, 1)
                    if u == 0 and middle:
                        middle()
                if last:
                    pe.drain().then_inc(b_used, B_UNITS)

            def ffn(L, a0, b0, f, before_down, after_first=None, acts=None):
                base = f * CHUNKS

                def turn_h(c, k):
                    pe.wait_ge(s["h_ready"], L * 4 * CHUNKS + c * 2 + 2 * (base + k + 1))
                    for u in range(2):
                        for t in range(NT):
                            ins = turn(ps[:, TR, u * SEQ + t * P:u * SEQ + (t + 1) * P], h[:, t, u * P:(u + 1) * P])
                    ins.then_inc(s["h_turned"], 1)

                def gate_up(c, k, middle=None, acts=None):
                    pe.wait_ge(s["h_ready"], L * 4 * CHUNKS + c * 2 + 2 * (base + k))
                    group(L, c, a0 + k, GU, 2 * CHUNK, middle, acts)

                def down(c, k, hi=hT_hi, lo=hT_lo, first=False, last=False, middle=None):
                    pe.wait_ge(s["hT_ready"], L * 2 * CHUNKS + c + (base + k + 1))
                    rows2(L, c, b0 + k, hi, lo, first, last, "ffn_done", middle)

                gate_up(0, 0, acts=acts)
                if after_first:
                    after_first()
                gate_up(0, 1, lambda: turn_h(0, 0))
                before_down()
                down(0, 0, first=True)
                with pe.Fori(2, CHUNKS - 1) as c:
                    gate_up(c, 0, lambda: turn_h(c, -1))
                    down(c, -1)
                c = CHUNKS - 1
                gate_up(0, c, lambda: turn_h(0, c - 1))
                down(0, c - 1, middle=lambda: turn_h(0, c))
                down(0, c, actT_hi, actT_lo, last=True)

            def turn_norm(L, k, src, ready):
                for t in range(NT):
                    ready(t)
                    for i in range(4):
                        for kk in range(2):
                            c = 2 * i + kk
                            ins = turn(ps[:, LN_BANKS[i], kk * SEQ + t * P:kk * SEQ + (t + 1) * P],
                                       src[:, t, c * P:(c + 1) * P])
                        if t == NT - 1:
                            ins.then_inc(s["turned"], 1)

            def wait_act(L, k):
                pe.wait_ge(s["actT_ready"], L * 16 + k)

            pe.sem_inc(a_used, A_UNITS)
            pe.sem_inc(b_used, B_UNITS)
            pe.wait_ge(s["ident_set"], 1)
            pe.wait_ge(s["sel_loaded"], 32)
            pe.matmul(ps[0:N_ATT, 5, 0:3 * P], tw_re[0:REL_BUCKETS, 0, 0:N_ATT],
                      tw_im[0:REL_BUCKETS, 0:2, :].rearrange("p a t -> p (a t)")[:, 0:3 * P],
                      start=True, stop=True).then_inc(s["table_turned"], 1)
            pe.wait_ge(s["x_loaded"], 16)
            pe.wait_ge(s["table_out"], 1)

            with pe.Fori(0, DEPTH) as L:
                def input_ready(t):
                    pe.wait_ge(s["x_ready"], L * NT + t + 1)
                turn_norm(L, 0, x, input_ready)

                def turn_small():
                    pe.wait_ge(s["rows_loaded"], L * 128 + 128)
                    pe.wait_ge(s["dt_expanded"], L + 1)
                    pe.wait_ge(s["p_loaded"], L * 16 + 16)
                    for u in range(2):
                        for t in range(NT):
                            ins = turn(ps[:, ACC, u * SEQ + t * P:u * SEQ + (t + 1) * P], p_nat[:, t, u * P:(u + 1) * P])
                    ins.then_inc(s["p_turned"], 1)
                    pe.transpose(ps[:, ACC + 1, 0:ROWS], rows[0:ROWS, :], ident[0:ROWS, 0:ROWS])\
                        .then_inc(s["rows_turned"], 1)

                def small_out():
                    pe.wait_ge(s["prm_out"], L + 1)
                    pe.wait_ge(s["pT_ready"], L + 1)

                ffn(L, A_FFN1, B_FFN1, 0, small_out, turn_small, acts=0)
                pe.wait_ge(s["b_ready"], L + 1)
                for half in range(2):
                    for part in range(2):
                        ins = turn(ps[:, MISC, (2 * half + part) * P:(2 * half + part + 1) * P],
                                   b_exp[:, part, 4 * half:4 * half + 4, :].rearrange("p j c -> p (j c)"))
                ins.then_inc(s["bc_turned"], 1)
                pe.wait_ge(s["c_ready"], L + 1)
                pe.wait_ge(s["hT_ready"], L * 2 * CHUNKS + CHUNKS)
                for part in range(2):
                    for half in range(2):
                        ins = turn(ps[:, TR, (2 * part + half) * P:(2 * part + half + 1) * P],
                                   c_exp[:, part, half, :, :].rearrange("p q d -> p (q d)"))
                ins.then_inc(s["bc_turned"], 1)
                pe.wait_ge(s["in_out"], L + 1)
                pe.wait_ge(s["c_out"], L + 1)
                turn_norm(L, 1, z, lambda t: pe.wait_ge(s[f"z{t}_ready"], L * 2 + 1))
                def turn_block(bank, c, t, src, c0):
                    return turn(ps[:, bank, c * SEQ + t * P:c * SEQ + (t + 1) * P], src[:, t, c0:c0 + P])

                def turn_pair(bank, src, c0, done):
                    for u in range(2):
                        for t in range(NT):
                            ins = turn_block(bank, u, t, src, c0 + u * P)
                    ins.then_inc(s[done], 1)

                def turn_tile(bank, c, src, c0):
                    for t in range(NT):
                        ins = turn_block(bank, c, t, src, c0)
                    return ins

                def index_round(n):
                    qb, half = 1 - n // 2, n % 2
                    N = P * (qb + 1)
                    if n == 0:
                        pe.wait_ge(s["ix_out"], L * 6 + 2)
                    else:
                        pe.wait_ge(s["ixs_read"], L * 4 + n)
                    for b in range(2):
                        r = 32 * (2 * half + b)
                        for hh in range(2):
                            pe.matmul(ps[:, 4 + b, hh * SEQ:hh * SEQ + N], iqT[r:r + 32, hh, qb * P:(qb + 1) * P],
                                      ksT[r:r + 32, 0, 0:N], start=True, stop=True)
                    pe.drain().then_inc(s["ixs_done"], 1)

                def bu(n):
                    j = TILE_ORDER[n]
                    if n == 0:
                        pe.wait_ge(s["ix_out"], L * 6 + 5)
                    elif n == 4:
                        pe.wait_ge(s["ix_out"], L * 6 + 6)
                    if n >= 1:
                        pe.wait_ge(s["bu_out"], L * STATE_TILES + n)
                    r = slice(32 * (j % 4), 32 * (j % 4) + 32)
                    for part in range(2):
                        ins = pe.matmul(ps[:, 6, part * SEQ:(part + 1) * SEQ], inT[r, j // 4, part, :],
                                        uT[r, j // 4, :], start=True, stop=True)
                    ins.then_inc(s["bu_done"], 1)

                def states_out(n):
                    j = TILE_ORDER[n]
                    if n == 0:
                        pe.wait_ge(s["ix_out"], L * 6 + 6)
                    pe.wait_ge(s["prod_ready"], L * STATE_TILES + n + 1)
                    r = slice(32 * (j % 4), 32 * (j % 4) + 32)
                    for part in range(2):
                        ins = pe.matmul(ps[r, 7, (j // 4) * SEQ:(j // 4 + 1) * SEQ], outT[:, j, part, :],
                                        prod[:, n % 2, 0, part, :], start=part == 0, stop=part == 1)
                    ins.then_inc(s["c_done"], 1)

                def w_in_middle(i):
                    if i == 1:
                        pe.wait_ge(s["hp_ready"], L * WIN_GROUPS + 1)
                        turn_pair(6, hp, C_IQ, "ix_turned")
                        pe.wait_ge(s["kdup_ready"], L * 2 + 1)
                        turn_tile(7, 0, kdup, 0).then_inc(s["ix_turned"], 1)
                    if i == 2:
                        pe.wait_ge(s["hp_ready"], L * WIN_GROUPS + 2)
                        turn_pair(6, hp, C_SQ, "ix_turned")
                        pe.wait_ge(s["kdup_ready"], L * 2 + 2)
                        turn_tile(7, 0, kdup, P)
                        turn_tile(7, 1, hp, C_U + P).then_inc(s["ix_turned"], 1)
                    if i == 3:
                        pe.wait_ge(s["ix_out"], L * 6 + 5)
                        pe.wait_ge(s["hp_ready"], L * WIN_GROUPS + 3)
                        turn_tile(7, 0, hp, C_U).then_inc(s["ix_turned"], 1)
                        bu(1)
                        index_round(2)
                    if i == 4:
                        bu(3)
                    if i == 5:
                        pe.wait_ge(s["hp_ready"], L * WIN_GROUPS + 5)
                        for n in range(2):
                            turn_pair(n, hp, C_K + 2 * n * P, "qk_turned")
                        bu(5)
                        states_out(1)

                for i in range(WIN_GROUPS):
                    if i >= 2:
                        pe.wait_ge(s["hp_ready"], L * WIN_GROUPS + i - 1)
                    group(L, 0, A_WIN + i, 2 * (i % 2), WIN_COLS, lambda: w_in_middle(i), 4 if i == 0 else None)
                    pe.drain().then_inc(s["win_done"], 1)
                    if i == 1:
                        index_round(0)
                    if i == 2:
                        index_round(1)
                        bu(0)
                    if i == 3:
                        index_round(3)
                        bu(2)
                    if i == 4:
                        states_out(0)
                        bu(4)
                    if i == 5:
                        bu(6)
                pe.wait_ge(s["hp_ready"], L * WIN_GROUPS + WIN_GROUPS)
                pe.wait_ge(s["qk_out"], L * 4 + 2)
                for n in range(2):
                    turn_pair(n, hp, C_Q + 2 * n * P, "qk_turned")
                def scores(u):
                    hd, qb = u // 2, u % 2
                    N = P * (qb + 1)
                    if u == 0:
                        pe.wait_ge(s["qk_out"], L * 4 + 4)
                    else:
                        pe.wait_ge(s["das_read"], L * UNITS + u)
                    for c in range(2):
                        r = slice(64 * c, 64 * c + 64)
                        pe.matmul(ps[:, c, 0:N], qT[r, hd, qb * P:(qb + 1) * P], kT[r, hd, 0:N],
                                  start=True, stop=True)
                    pe.drain().then_inc(s["das_done"], 1)

                scores(0)
                states_out(2)
                for i in range(UNITS + 3):
                    if 0 <= i - 2 < UNITS:
                        u = i - 2
                        pe.wait_ge(s["da_a"], L * UNITS + u + 1)
                        if u >= 1:
                            pe.wait_ge(s["da_aT"], L * UNITS + u)
                        else:
                            pe.wait_ge(s["ixs_read"], L * 4 + 4)
                        for kb in range(u % 2 + 1):
                            ins = turn(ps[:, 4, kb * P:(kb + 1) * P], da_e[:, u % 2, 0, kb * P:(kb + 1) * P])
                        ins.then_inc(s["da_turned"], 1)
                    if i >= 3:
                        u = i - 3
                        hd, qb = u // 2, u % 2
                        pe.wait_ge(s["da_aT"], L * UNITS + u + 1)
                        if u >= 1:
                            pe.wait_ge(s["da_o_out"], L * UNITS + u)
                        for kb in range(qb + 1):
                            ins = pe.matmul(ps[:, 5, 0:P], aT[:, u % 2, kb * P:(kb + 1) * P],
                                            hp[:, kb, C_V + hd * DA_V:C_V + (hd + 1) * DA_V],
                                            start=kb == 0, stop=kb == qb)
                        ins.then_inc(s["da_o"], 1)
                    if i + 1 < UNITS:
                        scores(i + 1)
                    if i in SA_SCORES:
                        qb = SA_SCORES[i]
                        N = P * (qb + 1)
                        if qb == 0:
                            pe.wait_ge(s["mix_sa"], L * 2 + 1)
                        for hd in range(SA_HEADS):
                            r = slice(64 * (hd % 2), 64 * (hd % 2) + 64)
                            pe.matmul(ps[:, 2 + hd % 2, (hd // 2) * SEQ:(hd // 2) * SEQ + N],
                                      saqT[r, hd // 2, qb * P:(qb + 1) * P], ksT[r, 1, 0:N],
                                      start=True, stop=True)
                        pe.drain().then_inc(s["sas_done"], 1)
                    if i in C_LATE:
                        states_out(C_LATE[i])
                    if i in BU_LATE:
                        bu(BU_LATE[i])
                    if i in SA_TURN:
                        qb = SA_TURN[i]
                        pe.wait_ge(s["sa_exp"], L * 2 + (1 - qb) + 1)
                        pe.wait_ge(s["sas_read"], L * 2 + (1 - qb) + 1)
                        for half in range(2):
                            for b in range(2 * (qb + 1)):
                                hd, kb = 2 * half + b // (qb + 1), b % (qb + 1)
                                ins = turn(ps[:, 2 + half, b * P:(b + 1) * P], sa_e[:, hd, kb * P:(kb + 1) * P])
                            ins.then_inc(s["sa_turned"], 1)
                    if i in SA_OUT:
                        qb = SA_OUT[i]
                        pe.wait_ge(s["sa_aT_ready"], L * 4 + 2 * (1 - qb) + 2)
                        for hd in range(SA_HEADS):
                            for kb in range(qb + 1):
                                c0 = (hd // 2) * 512 + ((hd % 2) * (qb + 1) + kb) * P
                                ins = pe.matmul(ps[:, 2, hd * SA_DIM:(hd + 1) * SA_DIM], sa_aT[:, c0:c0 + P],
                                                hp[:, kb, C_SV:C_SV + SA_DIM], start=kb == 0, stop=kb == qb)
                        ins.then_inc(s["sa_o"], 1)
                pe.wait_ge(s["das_read"], L * UNITS + UNITS)
                pe.wait_ge(s["mix_da"], L * 2 + 1)
                turn_pair(0, hp, 0, "mix_turned")
                pe.wait_ge(s["mix_sa"], L * 2 + 2)
                turn_pair(1, hp, 768, "mix_turned")

                pe.wait_ge(s["gelu_done"], L + 1)
                pe.wait_ge(s["glu_loaded"], L * 16 + 16)
                for o in range(2):
                    for t in range(2):
                        ins = pe.matmul(ps[:, 6, o * SEQ:(o + 1) * SEQ], glu[:, t, o * P:(o + 1) * P],
                                        ys2[:, 1, t, :], start=t == 0, stop=t == 1)
                ins.then_inc(s["glu_done"], 1)

                def project(i, kt, t):
                    q = slice(t * P, (t + 1) * P)
                    return mm3(pe, ps[:, ACC + 2 * t + i, :], actT_hi[:, kt, q], actT_lo[:, kt, q],
                               hi_a[:, kt, :], lo_a[:, kt, :], kt == 0, kt == KT - 1)

                pe.wait_ge(s["da_aT"], L * UNITS + UNITS)
                for p in range(A_UNITS):
                    wait_act(L, 8 + p + 1)
                    if p == 1:
                        pe.wait_ge(s["mix_da"], L * 2 + 2)
                        turn_pair(0, hp, 256, "mix_turned")
                    wait_a(L, 0, A_WO, p)
                    for kt in (2 * p, 2 * p + 1):
                        for t in range(NT):
                            ins = project(0, kt, t)
                    ins.then_inc(a_used, 1)
                pe.wait_ge(s["da_o_out"], L * UNITS + UNITS)
                for t in range(NT):
                    for kt in range(KT):
                        if t == 0 and kt % 2 == 0:
                            wait_a(L, 0, A_WO + 1, kt // 2)
                        ins = project(1, kt, t)
                        if t == NT - 1 and kt % 2 and kt < KT - 1:
                            ins.then_inc(a_used, 1)
                    ins.then_inc(s["ffn_done"], 2)
                pe.drain().then_inc(a_used, 1)
                turn_norm(L, 2, z, lambda t: pe.wait_ge(s[f"z{t}_ready"], L * 2 + 2))
                pe.wait_ge(s["acc_read"], L * 6 + 4)
                rows2(L, 0, B_PROJ, pT_hi, pT_lo, True, True, "proj_done")
                for i in range(2):
                    group(L, 0, A_GATE + i, (GU, TR)[i], 512, acts=12 if i == 0 else None)
                    pe.drain().then_inc(s["gate_done"], 1)
                pe.wait_ge(s["gate_sig"], L * 4 + 2)
                ffn(L, A_FFN2, B_FFN2, 1, lambda: pe.wait_ge(s["ple_done"], L * 4 + 4))


INS = ["x", "p", "rel_bias", "ffn1_w_gate", "ffn1_w_up", "ffn1_w_down", "ln1_g", "ln1_b", "w_in", "w_o",
       "da_lam_q1", "da_lam_k1", "da_lam_q2", "da_lam_k2", "da_subln_g", "ssm_lam_re", "ssm_lam_im", "ssm_log_dt",
       "ssm_b_re", "ssm_b_im", "ssm_c_re", "ssm_c_im", "ssm_d", "ssm_w_glu", "ln2_g", "ln2_b", "ffn2_w_gate",
       "ffn2_w_up", "ffn2_w_down", "ple_w_proj", "ple_w_gate", "ln3_g", "ln3_b"]


def kernel(**inputs):
    import concourse.bacc as bacc
    from concourse.bass_utils import run_bass_kernel_spmd

    nc = bacc.Bacc("TRN2", target_bir_lowering=False, num_devices=1)
    arrays, args = {}, {}
    for name in INS + ["selector"]:
        v = np.ascontiguousarray(inputs[name]) if name != "selector" else bucket_selector()
        arrays[f"in_{name}"] = v
        args[name] = nc.dram_tensor(f"in_{name}", v.shape, mybir.dt.from_np(v.dtype), kind="ExternalInput").ap()
    args["out"] = nc.dram_tensor("out_x", (1, SEQ, D_MODEL), F32, kind="ExternalOutput").ap()
    table = nc.dram_tensor("bias_table", (N_ATT, P, 3 * P), F32).ap()
    args["table"] = table
    args["table_rows"] = bass.AP(table.tensor, P - 1, [[3 * P - 1, P], [P * 3 * P, N_ATT], [1, SEQ]])
    build(nc, args)
    r = run_bass_kernel_spmd(nc, [arrays], core_ids=[0])
    return r.results[0]["out_x"]
```
